# Optimizing a Trainium2 kernel written in Bass

```python
import math
import jax, jax.numpy as jnp
from jax import lax
import numpy as np

D_MODEL = 1024
BATCH = 1
SEQ = 256
DEPTH = 1
DEC_BATCH = 1
DEC_SEQ = 64
PAST_LEN = 128

CHUNK = 64
QBLOCK = 128
GLA_HEADS = 4
GLA_DK = D_MODEL // 8
GLA_DV = D_MODEL // 4
GLA_LOW_RANK = 16
GLA_TAU = 16.0
SB_HEADS = 16
SB_DH = D_MODEL // SB_HEADS
N_GROUPS = 4
EXPERTS_PER_GROUP = 8
N_EXPERTS = N_GROUPS * EXPERTS_PER_GROUP
TOP_K_IN_GROUP = 2
EXPERT_FF = D_MODEL // 2
DEEPNORM_ALPHA = (2.0 * DEPTH) ** 0.25
DEEPNORM_BETA = (8.0 * DEPTH) ** -0.25
LN_EPS = 1e-5

GLA_QK = GLA_HEADS * GLA_DK
GLA_V = GLA_HEADS * GLA_DV
SB_W = SB_HEADS * SB_DH
IN_SPLITS = (GLA_QK, GLA_QK, GLA_V, GLA_V, GLA_LOW_RANK, SB_W, SB_W, SB_W, D_MODEL, D_MODEL)
IN_WIDTH = sum(IN_SPLITS)
IN_OFFSETS = tuple(int(o) for o in np.cumsum(IN_SPLITS)[:-1])

kernel_name = "streaming_gla_stickbreak_hmoe"

def layer_norm(x, g=None, b=None):
    xf = x.astype(jnp.float32)
    mu = xf.mean(-1, keepdims=True)
    var = jnp.square(xf - mu).mean(-1, keepdims=True)
    y = (xf - mu) * lax.rsqrt(var + LN_EPS)
    if g is not None:
        y = y * g.astype(jnp.float32) + b.astype(jnp.float32)
    return y.astype(x.dtype)

def rms_norm_heads(o, g):
    of = o.astype(jnp.float32)
    y = of * lax.rsqrt(jnp.mean(jnp.square(of), -1, keepdims=True) + LN_EPS) * g.astype(jnp.float32)
    return y.astype(o.dtype)

def gla_chunked(q, k, v, log_a, s0):
    bsz, t, h, dk = q.shape
    dv = v.shape[-1]
    c = CHUNK if t % CHUNK == 0 else t
    n = t // c

    def to_chunks(a):
        return a.reshape(bsz, n, c, h, a.shape[-1]).transpose(1, 0, 2, 3, 4)

    causal = jnp.tril(jnp.ones((c, c), dtype=bool))

    def step(s, inp):
        qc, kc, vc, lc = inp
        qf, kf, vf = qc.astype(jnp.float32), kc.astype(jnp.float32), vc.astype(jnp.float32)
        b = jnp.cumsum(lc, axis=1)
        o_inter = jnp.einsum('bthk,bhkv->bthv', qf * jnp.exp(b), s)
        diff = b[:, :, None] - b[:, None, :]
        decay = jnp.exp(jnp.where(causal[None, :, :, None, None], diff, -jnp.inf))
        scores = jnp.einsum('bthk,bshk,btshk->bhts', qf, kf, decay)
        o_intra = jnp.einsum('bhts,bshv->bthv', scores, vf)
        b_last = b[:, -1]
        s_new = jnp.exp(b_last)[..., None] * s + jnp.einsum(
            'bshk,bshv->bhkv', kf * jnp.exp(b_last[:, None] - b), vf)
        return s_new, o_inter + o_intra

    s_fin, o = lax.scan(step, s0.astype(jnp.float32),
                        (to_chunks(q), to_chunks(k), to_chunks(v), to_chunks(log_a)))
    o = o.transpose(1, 0, 2, 3, 4).reshape(bsz, t, h, dv)
    return o.astype(v.dtype), s_fin.astype(s0.dtype)

def stick_breaking(q, k, v, q_off):
    bsz, tq, h, d = q.shape
    tk = k.shape[1]
    blk = QBLOCK if tq % QBLOCK == 0 else tq
    nb = tq // blk
    qb = q.reshape(bsz, nb, blk, h, d).transpose(1, 0, 2, 3, 4)
    kpos = jnp.arange(tk)
    scale = d ** -0.5

    def one_block(args):
        qi, i = args
        qpos = q_off + i * blk + jnp.arange(blk)
        z = jnp.einsum('bqhd,bkhd->bhqk', qi, k).astype(jnp.float32) * scale
        mask = (kpos[None, :] < qpos[:, None])[None, None]
        log_1mb = jnp.where(mask, jax.nn.log_sigmoid(-z), 0.0)
        rest = lax.cumsum(log_1mb, axis=3, reverse=True) - log_1mb
        weights = jnp.exp(jnp.where(mask, jax.nn.log_sigmoid(z) + rest, -jnp.inf))
        return jnp.einsum('bhqk,bkhd->bqhd', weights.astype(v.dtype), v)

    out = lax.map(one_block, (qb, jnp.arange(nb)))
    return out.transpose(1, 0, 2, 3, 4).reshape(bsz, tq, h, d)

def token_mixer(h, sb_k_past, sb_v_past, gla_s0, p):
    bsz, t, _ = h.shape
    proj = h @ p['w_in']
    (qa, ka, va, ga, lra, qb, kb, vb, gate_a, gate_b) = jnp.split(proj, IN_OFFSETS, axis=-1)
    qa = qa.reshape(bsz, t, GLA_HEADS, GLA_DK) * (GLA_DK ** -0.5)
    ka = ka.reshape(bsz, t, GLA_HEADS, GLA_DK)
    va = va.reshape(bsz, t, GLA_HEADS, GLA_DV)
    log_a = jax.nn.log_sigmoid((lra @ p['w_gla_a2'] + p['b_gla_a']).astype(jnp.float32)) / GLA_TAU
    log_a = log_a.reshape(bsz, t, GLA_HEADS, GLA_DK)
    oa, s_new = gla_chunked(qa, ka, va, log_a, gla_s0)
    oa = rms_norm_heads(oa, p['gla_norm_g']).reshape(bsz, t, GLA_V) * jax.nn.silu(ga)
    qb = qb.reshape(bsz, t, SB_HEADS, SB_DH)
    kb = kb.reshape(bsz, t, SB_HEADS, SB_DH)
    vb = vb.reshape(bsz, t, SB_HEADS, SB_DH)
    k_all = jnp.concatenate([sb_k_past.astype(kb.dtype), kb], axis=1)
    v_all = jnp.concatenate([sb_v_past.astype(vb.dtype), vb], axis=1)
    ob = stick_breaking(qb, k_all, v_all, sb_k_past.shape[1]).reshape(bsz, t, SB_W)
    merged = (jax.nn.sigmoid(gate_a) * (oa @ p['w_branch_a'])
              + jax.nn.sigmoid(gate_b) * (ob @ p['w_branch_b']))
    return merged @ p['w_out'], kb, vb, s_new

def hier_moe(h, p):
    bsz, t, d = h.shape
    tok = h.reshape(-1, d)
    gl = (tok @ p['w_group'] + p['b_group']).astype(jnp.float32)
    pg = jax.nn.softmax(gl, axis=-1)
    gi = jnp.argmax(gl, axis=-1)
    p_top = jnp.take_along_axis(pg, gi[:, None], axis=1)[:, 0]
    el = (tok @ p['w_router'] + p['b_router']).astype(jnp.float32).reshape(-1, N_GROUPS, EXPERTS_PER_GROUP)
    sel = jnp.take_along_axis(el, gi[:, None, None], axis=1)[:, 0]
    vals, idx = lax.top_k(sel, TOP_K_IN_GROUP)
    w2 = jax.nn.softmax(vals, axis=-1) * p_top[:, None]
    eid = gi[:, None] * EXPERTS_PER_GROUP + idx
    combine = jnp.einsum('nk,nke->ne', w2, jax.nn.one_hot(eid, N_EXPERTS, dtype=jnp.float32))
    y = jnp.zeros(tok.shape, jnp.float32)
    for e in range(N_EXPERTS):
        he = jax.nn.silu(tok @ p['w_exp_gate'][e]) * (tok @ p['w_exp_up'][e])
        y = y + combine[:, e:e + 1] * (he @ p['w_exp_down'][e]).astype(jnp.float32)
    return y.astype(h.dtype).reshape(bsz, t, d)

def trunk_layer(x, c, sb_k_past, sb_v_past, gla_s0, p):
    mod = jax.nn.silu(c) @ p['w_cond'] + p['b_cond']
    shift_m, scale_m, gate_m, shift_f, scale_f, gate_f = jnp.split(mod, 6, axis=-1)
    h = layer_norm(x) * (1 + scale_m[:, None]) + shift_m[:, None]
    mix, k_new, v_new, s_new = token_mixer(h, sb_k_past, sb_v_past, gla_s0, p)
    x = layer_norm(DEEPNORM_ALPHA * x + gate_m[:, None] * mix, p['ln1_g'], p['ln1_b'])
    h = layer_norm(x) * (1 + scale_f[:, None]) + shift_f[:, None]
    x = layer_norm(DEEPNORM_ALPHA * x + gate_f[:, None] * hier_moe(h, p), p['ln2_g'], p['ln2_b'])
    return x, k_new, v_new, s_new

def setup_inputs(seed: int = 0) -> dict:
    key = jax.random.key(seed)
    ks = jax.random.split(key, 32)
    f32 = jnp.float32
    nrm = lambda k, shape, s: jax.random.normal(k, shape, f32) * s
    D = D_MODEL
    return {
        "x_prompt": nrm(ks[0], (BATCH, SEQ, D), 1.0),
        "x_sample": nrm(ks[1], (DEC_BATCH, DEC_SEQ, D), 1.0),
        "cache_sb_k": nrm(ks[2], (DEPTH, DEC_BATCH, PAST_LEN, SB_HEADS, SB_DH), 1.0),
        "cache_sb_v": nrm(ks[3], (DEPTH, DEC_BATCH, PAST_LEN, SB_HEADS, SB_DH), 1.0),
        "state_gla": nrm(ks[4], (DEPTH, DEC_BATCH, GLA_HEADS, GLA_DK, GLA_DV), 1.0),
        "c_prompt": nrm(ks[5], (BATCH, D), 1.0),
        "c_sample": nrm(ks[6], (DEC_BATCH, D), 1.0),
        "w_cond": nrm(ks[7], (DEPTH, D, 6 * D), 0.5 * D ** -0.5),
        "b_cond": nrm(ks[8], (DEPTH, 6 * D), 0.02),
        "w_in": nrm(ks[9], (DEPTH, D, IN_WIDTH), D ** -0.5),
        "w_gla_a2": nrm(ks[10], (DEPTH, GLA_LOW_RANK, GLA_QK), GLA_LOW_RANK ** -0.5),
        "b_gla_a": nrm(ks[11], (DEPTH, GLA_QK), 0.1),
        "gla_norm_g": 1.0 + nrm(ks[12], (DEPTH, GLA_HEADS, GLA_DV), 0.02),
        "w_branch_a": nrm(ks[13], (DEPTH, GLA_V, D), DEEPNORM_BETA * GLA_V ** -0.5),
        "w_branch_b": nrm(ks[14], (DEPTH, SB_W, D), DEEPNORM_BETA * SB_W ** -0.5),
        "w_out": nrm(ks[15], (DEPTH, D, D), DEEPNORM_BETA * D ** -0.5),
        "ln1_g": 1.0 + nrm(ks[16], (DEPTH, D), 0.02),
        "ln1_b": nrm(ks[17], (DEPTH, D), 0.02),
        "w_group": nrm(ks[18], (DEPTH, D, N_GROUPS), D ** -0.5),
        "b_group": nrm(ks[19], (DEPTH, N_GROUPS), 0.01),
        "w_router": nrm(ks[20], (DEPTH, D, N_EXPERTS), D ** -0.5),
        "b_router": nrm(ks[21], (DEPTH, N_EXPERTS), 0.01),
        "w_exp_gate": nrm(ks[22], (DEPTH, N_EXPERTS, D, EXPERT_FF), D ** -0.5),
        "w_exp_up": nrm(ks[23], (DEPTH, N_EXPERTS, D, EXPERT_FF), D ** -0.5),
        "w_exp_down": nrm(ks[24], (DEPTH, N_EXPERTS, EXPERT_FF, D), DEEPNORM_BETA * EXPERT_FF ** -0.5),
        "ln2_g": 1.0 + nrm(ks[25], (DEPTH, D), 0.02),
        "ln2_b": nrm(ks[26], (DEPTH, D), 0.02),
    }

def reference(x_prompt, x_sample, cache_sb_k, cache_sb_v, state_gla, c_prompt, c_sample,
              w_cond, b_cond, w_in, w_gla_a2, b_gla_a, gla_norm_g, w_branch_a, w_branch_b,
              w_out, ln1_g, ln1_b, w_group, b_group, w_router, b_router,
              w_exp_gate, w_exp_up, w_exp_down, ln2_g, ln2_b):
    yp, ys = x_prompt, x_sample
    kp_l, vp_l, sp_l, ks_l, vs_l, ss_l = [], [], [], [], [], []
    bp = x_prompt.shape[0]
    for l in range(DEPTH):
        p = dict(w_cond=w_cond[l], b_cond=b_cond[l], w_in=w_in[l], w_gla_a2=w_gla_a2[l],
                 b_gla_a=b_gla_a[l], gla_norm_g=gla_norm_g[l], w_branch_a=w_branch_a[l],
                 w_branch_b=w_branch_b[l], w_out=w_out[l], ln1_g=ln1_g[l], ln1_b=ln1_b[l],
                 w_group=w_group[l], b_group=b_group[l], w_router=w_router[l],
                 b_router=b_router[l], w_exp_gate=w_exp_gate[l], w_exp_up=w_exp_up[l],
                 w_exp_down=w_exp_down[l], ln2_g=ln2_g[l], ln2_b=ln2_b[l])
        empty = jnp.zeros((bp, 0, SB_HEADS, SB_DH), yp.dtype)
        s0 = jnp.zeros((bp, GLA_HEADS, GLA_DK, GLA_DV), yp.dtype)
        yp, kp, vp, sp = trunk_layer(yp, c_prompt, empty, empty, s0, p)
        ys, kss, vss, sss = trunk_layer(ys, c_sample, cache_sb_k[l], cache_sb_v[l], state_gla[l], p)
        kp_l.append(kp); vp_l.append(vp); sp_l.append(sp)
        ks_l.append(kss); vs_l.append(vss); ss_l.append(sss)
    return (yp, ys, jnp.stack(kp_l), jnp.stack(vp_l), jnp.stack(sp_l),
            jnp.stack(ks_l), jnp.stack(vs_l), jnp.stack(ss_l))


_drawn_inputs = setup_inputs


def setup_inputs(seed=0):
    import zlib

    import numpy as np

    out = dict(_drawn_inputs(seed))
    spreads = {}
    factors = {'cache_sb_k': 22.139,
     'cache_sb_v': 8.0,
     'state_gla': 4.096,
     'gla_norm_g': 64.0,
     'ln1_g': 7.808,
     'ln1_b': 7.807,
     'b_group': 64.0,
     'b_router': 64.0,
     'ln2_g': 7.724,
     'ln2_b': 21.631,
     'w_group': 3.601,
     'w_router': 3.616,
     'w_exp_gate': 3.495,
     'w_exp_up': 3.265,
     'w_exp_down': 3.261}
    for name, (base, spread) in spreads.items():
        noise = np.random.default_rng([zlib.crc32(name.encode()), seed]).standard_normal(out[name].shape)
        drawn = base * np.exp(spread * noise) if base else spread * noise
        out[name] = __import__('jax').numpy.asarray(drawn.astype(out[name].dtype))
    for name, factor in factors.items():
        out[name] = (out[name] * factor).astype(out[name].dtype)
    return out
```

```python
from contextlib import ExitStack

import concourse.bass as bass
from concourse import mybir

F32 = mybir.dt.float32
BF16 = mybir.dt.bfloat16
I32 = mybir.dt.int32
ALU = mybir.AluOpType
ACT = mybir.ActivationFunctionType
AXX = mybir.AxisListType.X

P = 128
D = 1024
KT = D // P
SEQ, DSEQ, PAST = 256, 64, 128
T = SEQ + DSEQ
TR = (128, 128, 64)
TC = (slice(0, 128), slice(128, 256), slice(256, 320))
GH, DK, DV = 4, 128, 256
SH, SD = 16, 64
RANK = 16
NG, EPG = 4, 8
E = NG * EPG
FF = 512
FT = FF // P
EPS = 1e-5
ALPHA = 2.0 ** 0.25
TAU = 16.0
NEG = -1e30
FAR = 1e4
SKIP = 100000
SLOTS = 64
EXTRA = (2 * T) // SLOTS
ROUNDS = -(-T // SLOTS) - 1
CB = 512
CW = KT * CB
DENSE_RING = 3
RING = 9
LEVELS = 8


def dense_chunks():
    order = [("cond", c * CB) for c in range(4)]
    for name, first, n in (("qa", 0, 1), ("ka", 512, 1), ("va", 1024, 2), ("qb", 3088, 2), ("kb", 4112, 2),
                           ("vb", 5136, 2), ("ga", 2048, 2), ("gta", 6160, 2), ("gtb", 7184, 2)):
        order += [("in", first + c * CB) for c in range(n)]
    order += [("cond", c * CB) for c in range(4, 12)]
    order += [("ba", 0), ("ba", CB), ("bb", 0), ("bb", CB), ("out", 0), ("out", CB)]
    return order


DENSE = dense_chunks()
ND = len(DENSE)

GROUPS = [("lra", 0, "act")]
for _name, _n in (("qa", 4), ("ka", 4), ("va", 6), ("qb", 8), ("kb", 8), ("vb", 6), ("ga", 8), ("gta", 8), ("gtb", 8)):
    GROUPS += [(_name, _i, "act") for _i in range(_n)]
for _name in ("ba", "bb", "out"):
    GROUPS += [(_name, _i, "dve") for _i in range(8)]
PROJ_BANKS = 3


def taken_count(upto, engine):
    return sum(g[2] == engine for g in GROUPS[:upto + 1])


def build(nc, a, out):
    ctx = ExitStack()
    with ctx:
        def sb(name, shape, dt=F32, stack=ctx):
            return stack.enter_context(nc.sbuf_tensor(name, shape, dt))

        def sem(name):
            return ctx.enter_context(nc.semaphore(name))

        ident = sb("ident", [P, P])
        ones = sb("ones", [P, P])
        neg_tri = sb("neg_tri", [P, P])
        neg_ones = sb("neg_ones", [P, P])
        tri_strict = sb("tri_strict", [P, P])
        tri_tau = sb("tri_tau", [P, 2 * P])
        ident_b = sb("ident_b", [P, P], BF16)
        mask_sb = sb("mask_sb", [P, 512], BF16)
        slot_iota = sb("slot_iota", [P, SLOTS])
        iota_i = sb("iota_i", [P, SLOTS], I32)
        e_iota = sb("e_iota", [P, 3, E])
        g_iota = sb("g_iota", [P, 3, NG])
        tokval = sb("tokval", [P, 3])
        half_base = sb("half_base", [P, 1])
        valid = sb("valid", [P, 3])
        q_iota = sb("q_iota", [P, 2])
        x_iota = sb("x_iota", [P, EXTRA])
        cols = sb("cols", [P, 72])
        silu_c = sb("silu_c", [P, 2, KT])
        mod = sb("mod", [P, 6 * KT, 2])
        small = sb("small", [P, 64])
        eps_col = sb("eps_col", [P, 1])
        stats = sb("stats", [P, 12, 12])
        mv = sb("mv", [P, 12, 2])
        rstd = sb("rstd", [P, 12])
        wts = sb("wts", [P, 2, 3])
        ring = [sb(f"ring{i}", [P, CW]) for i in range(DENSE_RING)]

        s1 = ExitStack()
        levels = sb("levels", [P, LEVELS, P], F32, s1)
        qa = sb("qa", [P, GH, T], F32, s1)
        ka = sb("ka", [P, GH, T], F32, s1)
        la = sb("la", [P, 3, 512], F32, s1)
        pd = [sb(f"pd{i}", [P, GH, T], F32, s1) for i in range(2)]
        bt = sb("bt", [P, GH, T], F32, s1)
        va = sb("va", [P, 3, D], F32, s1)
        acc = sb("acc", [P, 3, GH, P], F32, s1)
        cross = sb("cross", [P, GH, P], F32, s1)
        s0 = sb("s0", [P, GH, DV], F32, s1)
        mtmp = sb("mtmp", [P, 2, 512], F32, s1)
        mtmp_s = sb("mtmp_s", [DSEQ, GH, DSEQ], F32, s1)
        hT = sb("hT", [P, KT, T], F32, s1)
        on = sb("on", [P, 3, D], F32, s1)
        obT = sb("obT", [P, KT, T], F32, s1)
        ckT = sb("ckT", [P, KT, P], F32, s1)
        cv = sb("cv", [P, D], F32, s1)
        qb = sb("qb", [P, KT, T], F32, s1)
        kb = sb("kb", [P, KT, T + 64], F32, s1)
        vb = sb("vb", [P, 3, D], F32, s1)
        ab = [sb(f"ab{i}", [P, 512], F32, s1) for i in range(2)]
        sp_ = [sb(f"sp{i}", [P, 512], F32, s1) for i in range(2)]
        wgt = [sb(f"wgt{i}", [P, 512], F32, s1) for i in range(2)]
        w_lra = sb("w_lra", [P, KT, RANK], F32, s1)
        lraT = ab[1][0:32, 0:T]
        wa2 = sp_[1][0:32, :]
        rows = ab[0][:, 0:P]
        xt = vb
        xn = on
        ck = wgt
        ke = pd[0]
        ket = la
        s1.close()

        s2 = ExitStack()
        ga = sb("ga", [P, KT, T], F32, s2)
        gta = sb("gta", [P, KT, T], F32, s2)
        gtb = sb("gtb", [P, KT, T], F32, s2)
        oaT = sb("oaT", [P, KT, T], F32, s2)
        merged = sb("merged", [P, KT, T], F32, s2)
        kbtok = sb("kbtok", [P, 3, D], F32, s2)
        s2.close()
        s3 = ExitStack()
        h2T = sb("h2T", [P, KT, T], F32, s3)
        ln1 = sb("ln1", [P, 2, D], F32, s3)
        gmT = sb("gmT", [P, KT, T], F32, s3)
        x2n = sb("x2n", [P, 3, D], F32, s3)
        s3.close()

        ring += [sb(f"ring{i}", [P, CW]) for i in range(DENSE_RING, RING)]
        x1 = sb("x1", [P, 3, D])
        hf = sb("hf", [P, 3, D])
        gf_rows = sb("gf_rows", [P, 2, D])
        diag = sb("diag", [P, P])
        w_route = sb("w_route", [P, KT, NG + E])
        b_route = sb("b_route", [1, NG + E])
        lg = sb("lg", [P, 3, NG + E])
        r4 = [sb(f"r4_{i}", [P, 3, NG]) for i in range(4)]
        r32 = [sb(f"r32_{i}", [P, 3, E]) for i in range(3)]
        r1 = sb("r1", [P, 16, 3])
        oh2 = sb("oh2", [P, 3, E])
        chosen = sb("chosen", [P, 3, E])
        pos = sb("pos", [P, 3, E])
        val = sb("val", [P, 3, E])
        rep = sb("rep", [P, 3, ROUNDS, E])
        q_rep = sb("q_rep", [P, P])
        flags = sb("flags", [P, 4])
        pick = sb("pick", [P, EXTRA])
        plan_f = sb("plan_f", [1, 2 * EXTRA + 1])
        plan_i = sb("plan_i", [1, 2 * EXTRA + 1], I32)
        first_slot = sb("first_slot", [P, EXTRA])
        onehot = sb("onehot", [P, 3, SLOTS])
        pcol = sb("pcol", [P, 3])
        vcol = sb("vcol", [P, 3])
        sidx = [sb(f"sidx{i}", [P, 1], I32) for i in range(3)]
        xrow = sb("xrow", [P, CB])
        xg = sb("xg", [P, 4, 2, SLOTS])
        gs = sb("gs", [P, FF])
        he = sb("he", [P, FT, SLOTS])
        ystage = [sb(f"ystage{i}", [P, CB]) for i in range(2)]
        comb = [ring[6 + t // 2][:, (t % 2) * 2 * D:(t % 2 + 1) * 2 * D] for t in range(3)]
        ln2 = ring[8][:, 0:2 * D].rearrange("p (a d) -> p a d", a=2)

        ybuf = nc.dram_tensor("expert_rows", [4 * T, CB], F32, kind="Internal").ap()

        bank = [ctx.enter_context(nc.psum_tensor(f"bank{i}", [P, 512], F32)) for i in range(8)]

        names = """const_ready rows_in x_in lra_in misc_in vecs_in x1_in cols_t silu_ready cond_done mod_ready xn_ready xn_t h_dve h_act proj_ready taken_act taken_dve xla_ps la_ready b_ps b_ready
            dec_ready exp_ready pd_ready lev_ps lev_taken lev_added kd_ready ke_ready ke_t ket_ready
            st_ps st_ready qe_ready go_ps go_ready ck_t ck_ready z_ready l_ready sp_ready rest_ready w_ready
            o_ready o_taken kb_t kb_tok on_ready on_t oa_ready sig_ready merged_ready gm_t gm_added
            norm_ready norm_t h2_ready lg_ps lg_ready ex_in ex_out rank_in rank_ps pos_ready hb_t hb_ready
            flag_ready xr_ps pick_ready plan_ps plan_ready gfr_in gfr_ps gf_ready onehot_ready gather_ps xrow_ready
            xg_t xg_ready gu_ps gs_ready hrow_ready he_t he_ready down_ps ys_ready scattered0 scattered1 comb_in0 comb_in1 comb_in2
            vcol_ready pcol_ready fin_ready stored act_chain dve_chain pool_chain gla_stored rstd_ready nrm_sum
            pe_passed pool_passed""".split()
        S = {n: sem(n) for n in names}
        chunk_in = [sem(f"chunk_in{i}") for i in range(RING)]

        class Chain:

            def __init__(self, eng, s):
                self.eng, self.s, self.n = eng, s, 0

            def add(self, ins):
                self.n += 1
                return ins.then_inc(self.s, 1)

            def done(self):
                self.eng.wait_ge(self.s, self.n)

        def consumed(i):
            name = DENSE[i][0]
            if name == "cond":
                return S["cond_done"], sum(c[0] == "cond" for c in DENSE[:i + 1])
            groups = 1
            for c in DENSE[:i + 1]:
                if c[0] != "cond":
                    token_major = c[0] == "in" and (1024 <= c[1] < 2048 or 5136 <= c[1] < 6160)
                    groups += 3 if token_major else 4
            return S["proj_ready"], groups

        USED = ("gu_ps", "gu_ps", "down_ps")

        def dense_use(i):
            return 16 * (i // DENSE_RING + 1)

        def expert_use(s, turn):
            before = len(range(s, ND, DENSE_RING)) if s < DENSE_RING else 0
            return 16 * (before + turn + 1)

        SRC = {"cond": a["w_cond"][0], "in": a["w_in"][0], "ba": a["w_branch_a"][0], "bb": a["w_branch_b"][0],
               "out": a["w_out"][0]}

        block = ctx.enter_context(nc.Block())

        @block.sync
        def _(sp):
            def expert_chunk(e, q, slot):
                s = chunk_in[slot]
                dst = ring[slot]
                if q < 2:
                    w = (a["w_exp_gate"], a["w_exp_up"])[q][0]
                    src = w[bass.ds(e, 1)].rearrange("e (k p) n -> p (e k) n", p=P)
                    sp.dma_start(dst[:, :].rearrange("p (k n) -> p k n", k=KT), src).then_inc(s, 16)
                else:
                    src = a["w_exp_down"][0][bass.ds(e, 1)].rearrange("e (k p) n -> p (e k) n", p=P)
                    sp.dma_start(dst[:, :].rearrange("p (k n) -> p k n", k=FT), src).then_inc(s, 16)

            for i, (name, c0) in enumerate(DENSE):
                if i >= DENSE_RING:
                    sp.wait_ge(*consumed(i - DENSE_RING))
                src = SRC[name].rearrange("(k p) n -> p k n", p=P)[:, :, c0:c0 + CB]
                sp.dma_start(ring[i % DENSE_RING][:, :].rearrange("p (k n) -> p k n", k=KT), src)\
                  .then_inc(chunk_in[i % DENSE_RING], 16)
            for m in range(RING):
                if m < DENSE_RING:
                    last = max(range(m, ND, DENSE_RING))
                    sp.wait_ge(*consumed(last))
                elif m == DENSE_RING:
                    sp.wait_ge(S["hb_ready"], 6)
                    sp.wait_ge(S["lg_ready"], 3)
                    sp.wait_ge(S["stored"], 32)
                expert_chunk(m // 3, m % 3, m)
            with sp.Fori(0, E // 3 - 1) as it:
                for r in range(3):
                    for q in range(3):
                        sp.wait_ge(S[USED[q]], it * 3 + (r + 1))
                        expert_chunk(it * 3 + (3 + r), q, 3 * r + q)
            for e in (30, 31):
                for q in range(3):
                    sp.wait_ge(S[USED[q]], e - 2)
                    expert_chunk(e, q, (3 * e + q) % RING)
            sp.wait_ge(S["plan_ready"], 1)
            n_over = sp.value_load(plan_i[0:1, 2 * EXTRA:2 * EXTRA + 1], min_val=0, max_val=EXTRA)
            with sp.If(n_over > 0):
                with sp.Fori(0, n_over) as i:
                    e = sp.value_load(plan_i[0:1, bass.ds(i, 1)], min_val=0, max_val=E - 1)
                    for q in range(3):
                        sp.wait_ge(S[USED[q]], i + E)
                        expert_chunk(e, q, q)
                sp.nop()
            with sp.Else():
                sp.nop()

        @block.gpsimd
        def _(pool):
            ch = Chain(pool, S["pool_chain"])

            def select(t, pattern, base, cm, fill, op=ALU.is_ge):
                ch.done()
                ch.add(pool.affine_select(out=t, in_=t, compare_op=op, fill=fill, base=base, pattern=pattern,
                                          channel_multiplier=cm))

            ch.add(pool.memset(ident[:, :], 0.0))
            ch.add(pool.memset(eps_col[:, :], EPS))
            ch.add(pool.memset(lraT, 1.0))
            ch.add(pool.memset(mv[:, :, :], 1.0))
            select(ident[:, :], [[-1, P]], 0, 1, 1.0, ALU.not_equal)
            ch.done()
            pool.nop().then_inc(S["const_ready"], 1)
            for t, v in ((ones[:, :], 1.0), (neg_ones[:, :], -1.0),
                         (neg_tri[:, :], -1.0), (tri_strict[:, :], 1.0), (tri_tau[:, :], 1.0 / TAU),
                         (ident_b[:, :], 0.0), (mask_sb[:, :], 0.0), (valid[:, :], 1.0),
                         (levels[:, :, :], 1.0), (kb[:, :, T:T + 64], 0.0)):
                ch.add(pool.memset(t, v))
            select(ident_b[:, :], [[-1, P]], 0, 1, 1.0, ALU.not_equal)
            select(neg_tri[:, :], [[-1, P]], 0, 1, 0.0)
            select(tri_strict[:, :], [[1, P]], -1, -1, 0.0)
            select(tri_tau[:, 0:P], [[1, P]], 0, -1, 0.0)
            for c in (0, 256):
                select(mask_sb[:, c:c + P], [[1, P]], -1, -1, NEG)
            select(mask_sb[:, 448:512], [[1, 64]], -1, -1, NEG)
            select(valid[:, 2:3], [[0, 1]], 63, -1, 0.0)
            select(levels[:, 0, :], [[-1, P]], 0, 1, 0.0, ALU.is_equal)
            for n in range(1, LEVELS):
                size = 2 ** n
                view = levels[:, n, :].rearrange("p (b c) -> p b c", c=size)
                right = view[:, :, size // 2:size]
                blocks = P // size
                select(right, [[-size, blocks], [0, size // 2]], 0, 1, 0.0)
                select(right, [[size, blocks], [0, size // 2]], size // 2 - 1, -1, 0.0)
                ch.add(pool.memset(view[:, :, 0:size // 2], 0.0))

            def iota(dst, width, pattern, base, cm):
                ch.done()
                ch.add(pool.iota(iota_i[:, 0:width], pattern=pattern, base=base, channel_multiplier=cm))
                ch.done()
                ch.add(pool.tensor_copy(dst, iota_i[:, 0:width]))

            iota(slot_iota[:, :], SLOTS, [[1, SLOTS]], 0, 0)
            for t in range(3):
                iota(e_iota[:, t, :], E, [[1, E]], 0, 0)
                iota(g_iota[:, t, :], NG, [[1, NG]], 0, 0)
            iota(tokval[:, :], 3, [[2 * P, 3]], -SKIP, 2)
            ch.done()
            ch.add(pool.memset(half_base[0:SLOTS, :], 2.0 * SKIP))
            ch.done()
            ch.add(pool.memset(half_base[SLOTS:P, :], 2.0 * SKIP + 1.0))
            iota(x_iota[:, :], EXTRA, [[1, EXTRA]], 0, 0)
            for j in range(ROUNDS):
                ch.done()
                lo, hi = E * j, E * j + E
                ch.add(pool.memset(q_iota[lo:hi, 1:2], float(SLOTS * (j + 1))))
                ch.done()
                ch.add(pool.iota(iota_i[lo:hi, 0:1], pattern=[[0, 1]], base=0, channel_multiplier=1))
                ch.done()
                ch.add(pool.tensor_copy(q_iota[lo:hi, 0:1], iota_i[lo:hi, 0:1]))
            ch.done()
            pool.nop().then_inc(S["const_ready"], 1)

            for n in range(1, LEVELS):
                pool.wait_ge(S["lev_taken"], n + 1)
                if n < LEVELS - 1:
                    pool.tensor_tensor(acc[0:64, 2, :, 0:64], acc[0:64, 2, :, 0:64],
                                       mtmp_s[:, :, :], ALU.add)
                for t in range(2):
                    last = pool.tensor_tensor(acc[:, t, :, :], acc[:, t, :, :],
                                              mtmp[:, t, :].rearrange("p (h t) -> p h t", h=GH), ALU.add)
                last.then_inc(S["lev_added"], 1)

            pool.wait_ge(S["o_ready"], KT)
            pool.wait_ge(S["kb_t"], 6)
            pool.wait_ge(S["gla_stored"], 16 * 6)
            pool.dma_start(x1[:, 0:2, :], a["x_prompt"][0].rearrange("(t p) d -> p t d", p=P)).then_inc(S["x1_in"], 16)
            pool.dma_start(x1[0:64, 2, :], a["x_sample"][0]).then_inc(S["x1_in"], 16)
            pool.dma_start(w_route[:, :, 0:NG], a["w_group"][0].rearrange("(k p) n -> p k n", p=P)).then_inc(S["x1_in"], 16)
            pool.dma_start(w_route[:, :, NG:NG + E], a["w_router"][0].rearrange("(k p) n -> p k n", p=P)).then_inc(S["x1_in"], 16)
            pool.dma_start(b_route[:, 0:NG], a["b_group"]).then_inc(S["x1_in"], 16)
            pool.dma_start(b_route[:, NG:NG + E], a["b_router"]).then_inc(S["x1_in"], 16)
            for j in range(KT):
                pool.wait_ge(S["taken_dve"], KT + j + 1)
                pool.tensor_tensor(merged[:, j, :], merged[:, j, :], gtb[:, j, :], ALU.add).then_inc(S["merged_ready"], 1)
            pool.dma_start(ln1[:, 0, :], a["ln1_g"][0].partition_broadcast(P)).then_inc(S["vecs_in"], 16)
            pool.dma_start(ln1[:, 1, :], a["ln1_b"][0].partition_broadcast(P)).then_inc(S["vecs_in"], 16)

            def scatter(n, r, b):
                pool.wait_ge(S["ys_ready"], n + 1)
                if not isinstance(n, int):
                    pool.sem_inc(S["pool_passed"], 1)
                pool.indirect_dma_start(out=ybuf[:, :], out_offset=bass.IndirectOffsetOnAxis(ap=sidx[r][:, 0:1], axis=0),
                                        in_=ystage[b][:, :], in_offset=None, bounds_check=4 * T - 1,
                                        oob_is_err=False).then_inc(S[f"scattered{b}"], 16)

            scatter(0, 0, 0)
            with pool.Fori(0, (E - 2) // 6) as it:
                for r in range(1, 7):
                    scatter(it * 6 + r, r % 3, r % 2)
            scatter(E - 1, (E - 1) % 3, (E - 1) % 2)
            pool.wait_ge(S["plan_ready"], 1)
            n_over = pool.value_load(plan_i[0:1, 2 * EXTRA:2 * EXTRA + 1], min_val=0, max_val=EXTRA)
            with pool.If(n_over > 0):
                with pool.Fori(0, n_over) as i:
                    scatter(i + E, 0, 0)
                pool.wait_ge(S["scattered1"], 8 * E)
                pool.wait_ge(S["scattered0"], n_over * 16 + 8 * E)
                pool.nop()
            with pool.Else():
                pool.wait_ge(S["scattered1"], 8 * E)
                pool.wait_ge(S["scattered0"], 8 * E)
                pool.nop()
            pool.wait_ge(S["down_ps"], E)
            for t in range(3):
                n = TR[t]
                pool.dma_start(comb[t][0:n, :], ybuf[4 * P * t:4 * P * t + 4 * n, :].rearrange("(p k) d -> p (k d)", k=4))\
                    .then_inc(S[f"comb_in{t}"], 16)
            pool.dma_start(ln2[:, 0, :], a["ln2_g"][0].partition_broadcast(P)).then_inc(S["vecs_in"], 16)
            pool.dma_start(ln2[:, 1, :], a["ln2_b"][0].partition_broadcast(P)).then_inc(S["vecs_in"], 16)

        @block.scalar
        def _(act):
            ch = Chain(act, S["act_chain"])
            X = nc.scalar

            act.dma_start(xt[:, 0:2, :], a["x_prompt"][0].rearrange("(t p) d -> p t d", p=P)).then_inc(S["x_in"], 16)
            act.dma_start(xt[0:64, 2, :], a["x_sample"][0]).then_inc(S["x_in"], 16)
            act.wait_ge(S["const_ready"], 1)
            act.dma_start(rows[0:8, :], a["c_prompt"].rearrange("a (k p) -> (a k) p", p=P)).then_inc(S["rows_in"], 16)
            act.dma_start(rows[8:16, :], a["c_sample"].rearrange("a (k p) -> (a k) p", p=P)).then_inc(S["rows_in"], 16)
            act.dma_start(rows[16:64, :], a["b_cond"].rearrange("a (k p) -> (a k) p", p=P)).then_inc(S["rows_in"], 16)
            act.dma_start(rows[64:72, :], a["gla_norm_g"].rearrange("a h (j p) -> (a h j) p", p=P)).then_inc(S["rows_in"], 16)
            act.dma_start(w_lra[:, :, :], a["w_in"][0].rearrange("(k p) n -> p k n", p=P)[:, :, 3072:3088]).then_inc(S["lra_in"], 16)
            act.dma_start(wa2[0:RANK, :], a["w_gla_a2"][0]).then_inc(S["lra_in"], 16)
            act.dma_start(wa2[RANK:RANK + 1, :], a["b_gla_a"]).then_inc(S["lra_in"], 16)
            act.dma_start(s0[:, :, :], a["state_gla"][0, 0].rearrange("h k v -> k h v")).then_inc(S["misc_in"], 16)
            act.dma_start(cv[:, :], a["cache_sb_v"][0, 0].rearrange("s h d -> s (h d)")).then_inc(S["misc_in"], 16)
            act.dma_start(ck[0][:, :], a["cache_sb_k"][0, 0].rearrange("s h d -> s (h d)")[:, 0:512]).then_inc(S["misc_in"], 16)
            act.dma_start(ck[1][:, :], a["cache_sb_k"][0, 0].rearrange("s h d -> s (h d)")[:, 512:D]).then_inc(S["misc_in"], 16)

            act.wait_ge(S["cols_t"], 1)
            X.activation(silu_c[:, :, :], bank[7][:, 0:16].rearrange("p (g k) -> p g k", g=2), ACT.Silu).then_inc(S["silu_ready"], 1)

            def rsqrt(i0, n):
                ch.add(X.activation(rstd[:, i0:i0 + n], mv[:, i0:i0 + n, 1], ACT.Ln, bias=eps_col[:, 0:1]))
                ch.done()
                X.activation(rstd[:, i0:i0 + n], rstd[:, i0:i0 + n], ACT.Exp, scale=-0.5).then_inc(S["rstd_ready"], 1)

            act.wait_ge(S["nrm_sum"], 1)
            rsqrt(0, 3)
            act.wait_ge(S["mod_ready"], 1)
            for k in range(1, KT, 2):
                act.wait_ge(S["xn_t"], k + 1)
                for g_, c in ((0, slice(0, SEQ)), (1, slice(SEQ, T))):
                    last = X.activation(hT[:, k, c], bank[3 + k % 2][:, c], ACT.Identity, bias=mod[:, k, g_:g_ + 1],
                                        scale=mod[:, KT + k, g_:g_ + 1])
                last.then_inc(S["h_act"], 1)

            g = [0]

            def take(name, i):
                n = g[0]
                assert GROUPS[n][:2] == (name, i)
                src = bank[n % PROJ_BANKS]
                act.wait_ge(S["proj_ready"], n + 1)
                if name == "lra":
                    ins = X.activation(lraT[0:RANK, :], src[0:RANK, 0:T], ACT.Copy)
                elif name == "qa":
                    ins = X.activation(qa[:, i, :], src[:, 0:T], ACT.Copy, scale=DK ** -0.5)
                elif name == "qb":
                    ins = X.activation(qb[:, i, :], src[:, 0:T], ACT.Copy, scale=SD ** -0.5)
                elif name == "ka":
                    ins = X.activation(ka[:, i, :], src[:, 0:T], ACT.Copy)
                elif name == "kb":
                    ins = X.activation(kb[:, i, 0:T], src[:, 0:T], ACT.Copy)
                elif name in ("va", "vb"):
                    dst = va if name == "va" else vb
                    c, t = divmod(i, 3)
                    ins = X.activation(dst[0:TR[t], t, c * CB:c * CB + CB], src[0:TR[t], :], ACT.Copy)
                else:
                    dst = {"ga": ga, "gta": gta, "gtb": gtb}[name]
                    ins = X.activation(dst[:, i, :], src[:, 0:T], ACT.Copy)
                ins.then_inc(S["taken_act"], 1)
                g[0] += 1

            def log_gate(t):
                n = TR[t]
                act.wait_ge(S["xla_ps"], t + 1)
                ch.add(X.activation(la[0:n, t, :], bank[3 + t][0:n, :], ACT.Abs))
                ch.done()
                ch.add(X.activation(la[0:n, t, :], la[0:n, t, :], ACT.Exp, scale=-1.0))
                ch.done()
                X.activation(la[0:n, t, :], la[0:n, t, :], ACT.Ln, bias=1.0).then_inc(S["exp_ready"], 1)

            take("lra", 0)
            for i in range(4):
                take("qa", i)
            for t in range(3):
                log_gate(t)
            for i in range(4):
                take("ka", i)
            for i in range(6):
                take("va", i)

            def level_exp(n):
                act.wait_ge(S["dec_ready"], n)
                c = T if n < 7 else SEQ
                X.activation(pd[n % 2][:, :, 0:c], pd[n % 2][:, :, 0:c], ACT.Exp).then_inc(S["exp_ready"], 1)

            second = [("qb", i) for i in range(8)] + [("kb", i) for i in range(8)] + [("vb", i) for i in range(6)]
            for i, (name, j) in enumerate(second):
                take(name, j)
                if i % 2 == 1 and i // 2 < LEVELS:
                    level_exp(i // 2 + 1)
                if i == 19:
                    act.wait_ge(S["lev_ps"], LEVELS + 1)
                    for h in range(GH):
                        X.activation(pd[0][:, h, 0:SEQ], bt[:, h, 0:SEQ], ACT.Exp, scale=-1.0, bias=bt[:, h, SEQ - 1:SEQ])
                        X.activation(pd[0][:, h, SEQ:T], bt[:, h, SEQ:T], ACT.Exp, scale=-1.0, bias=bt[:, h, T - 1:T])
                        last = X.activation(pd[1][:, h, 0:DSEQ], bt[:, h, SEQ:T], ACT.Exp)
                    last.then_inc(S["kd_ready"], 1)
            act.wait_ge(S["taken_act"], taken_count(GROUPS.index(("vb", 5, "act")), "act"))
            act.dma_start(out["sb_v_prompt"][0, 0].rearrange("(t p) h d -> p t (h d)", p=P), vb[:, 0:2, :]).then_inc(S["gla_stored"], 16)
            act.dma_start(out["sb_v_sample"][0, 0].rearrange("s h d -> s (h d)"), vb[0:64, 2, :]).then_inc(S["gla_stored"], 16)
            for p in range(2):
                act.wait_ge(S["st_ready"], p + 1)
                act.dma_start(out["gla_state_prompt"][0, 0].rearrange("h k v -> k h v")[:, 2 * p:2 * p + 2, :],
                              sp_[p][:, :].rearrange("p (h v) -> p h v", h=2)).then_inc(S["gla_stored"], 16)
            for p in range(2):
                act.wait_ge(S["st_ready"], p + 3)
                act.dma_start(out["gla_state_sample"][0, 0].rearrange("h k v -> k h v")[:, 2 * p:2 * p + 2, :],
                              ab[p][:, :].rearrange("p (h v) -> p h v", h=2)).then_inc(S["gla_stored"], 16)
            act.wait_ge(S["nrm_sum"], 2)
            rsqrt(0, 12)

            def soft(h):
                b = ab[h % 2]
                act.wait_ge(S["z_ready"], h + 1)
                if h >= 2:
                    act.wait_ge(S["sp_ready"], h - 1)
                ch.add(X.activation(b[:, :], bank[5 + h % 3][:, :], ACT.Abs))
                ch.done()
                ch.add(X.activation(b[:, :], b[:, :], ACT.Exp, scale=-1.0))
                ch.done()
                X.activation(b[:, :], b[:, :], ACT.Ln, bias=1.0).then_inc(S["l_ready"], 1)

            def weights(h):
                act.wait_ge(S["rest_ready"], h + 1)
                X.activation(wgt[h % 2][:, :], bank[5 + h % 3][:, :], ACT.Exp).then_inc(S["w_ready"], 1)

            gates = [(n, i) for n in ("ga", "gta", "gtb") for i in range(8)]
            done = 0
            act.wait_ge(S["go_ps"], 6)
            act.wait_ge(S["gla_stored"], 16 * 6)
            for i in range(SH + 1):
                if i < SH:
                    soft(i)
                if i >= 1:
                    weights(i - 1)
                while done < min(len(gates), (i + 1) * 3 // 2):
                    take(*gates[done])
                    done += 1
            act.wait_ge(S["taken_act"], g[0])
            for src in (gta, gtb):
                ch.add(X.activation(src[:, :, :], src[:, :, :], ACT.Sigmoid))
            X.activation(ga[:, :, :], ga[:, :, :], ACT.Silu).then_inc(S["sig_ready"], 1)
            act.wait_ge(S["kb_tok"], 6)
            act.dma_start(out["sb_k_prompt"][0, 0].rearrange("(t p) h d -> p t (h d)", p=P), kbtok[:, 0:2, :]).then_inc(S["stored"], 16)
            act.dma_start(out["sb_k_sample"][0, 0].rearrange("s h d -> s (h d)"), kbtok[0:64, 2, :]).then_inc(S["stored"], 16)
            for n in range(2):
                act.wait_ge(S["nrm_sum"], 3 + n)
                rsqrt(0, 3)
            act.wait_ge(S["ex_in"], 1)
            X.activation(r4[1][:, :, :], r4[0][:, :, :], ACT.Exp).then_inc(S["ex_out"], 1)
            act.wait_ge(S["ex_in"], 2)
            X.activation(r1[:, 5, :], r1[:, 4, :], ACT.Exp).then_inc(S["ex_out"], 1)

            def rows_of(n):
                act.wait_ge(S["gather_ps"], n + 1)
                X.activation(xrow[:, :], bank[0][:, :], ACT.Copy).then_inc(S["xrow_ready"], 1)

            def silu(n):
                act.wait_ge(S["gu_ps"], n + 1)
                X.activation(gs[SLOTS:P, :], bank[1][0:SLOTS, :], ACT.Silu).then_inc(S["gs_ready"], 1)

            def rows_out(n, b, before):
                act.wait_ge(S["down_ps"], n + 1)
                if before is not None:
                    act.wait_ge(S[f"scattered{b}"], before * 16)
                X.activation(ystage[b][:, :], bank[3][:, :], ACT.Copy).then_inc(S["ys_ready"], 1)

            def step(n, b, before):
                silu(n)
                rows_of(n + 1)
                rows_out(n, b, before)

            rows_of(0)
            step(0, 0, None)
            step(1, 1, None)
            with act.Fori(0, (E - 4) // 2) as it:
                for r in range(2, 4):
                    step(it * 2 + r, r % 2, it + 1)
            step(E - 2, 0, E // 2 - 1)
            silu(E - 1)
            rows_out(E - 1, (E - 1) % 2, (E - 1) // 2)
            act.wait_ge(S["plan_ready"], 1)
            n_over = act.value_load(plan_i[0:1, 2 * EXTRA:2 * EXTRA + 1], min_val=0, max_val=EXTRA)
            with act.If(n_over > 0):
                with act.Fori(0, n_over) as i:
                    rows_of(i + E)
                    silu(i + E)
                    rows_out(i + E, 0, i + E // 2)
                act.nop()
            with act.Else():
                act.nop()
            act.wait_ge(S["nrm_sum"], 5)
            rsqrt(0, 3)
            for t in range(3):
                act.wait_ge(S["fin_ready"], t + 1)
                dst = out["y_prompt"][0][t * P:t * P + P, :] if t < 2 else out["y_sample"][0]
                act.dma_start(dst, x1[0:TR[t], t, :]).then_inc(S["stored"], 16)
            act.wait_ge(S["stored"], 16 * 5)

        @block.tensor
        def _(pe):
            mm = nc.tensor.matmul
            cur = [0]

            def chunk():
                i = cur[0]
                pe.wait_ge(chunk_in[i % DENSE_RING], dense_use(i))
                cur[0] += 1
                return ring[i % DENSE_RING][:, :].rearrange("p (k n) -> p k n", k=KT)

            pe.wait_ge(S["const_ready"], 1)
            pe.wait_ge(S["rows_in"], 64)
            nc.tensor.transpose(bank[7][:, 0:72], rows[0:72, :], ident[0:72, 0:72]).then_inc(S["cols_t"], 1)

            def cond(n_chunks, first):
                for c in range(n_chunks):
                    w = chunk()
                    for m in range(4):
                        j = first + 4 * c + m
                        for k in range(KT):
                            last = mm(bank[6][:, 2 * j:2 * j + 2], w[:, k, m * P:m * P + P], silu_c[:, :, k],
                                      start=(k == 0), stop=(k == KT - 1))
                    last.then_inc(S["cond_done"], 1)

            pe.wait_ge(S["silu_ready"], 1)
            cond(4, 0)
            pe.wait_ge(S["xn_ready"], 3)
            for k in range(KT):
                b = bank[3 + k % 2]
                if k >= 2:
                    pe.wait_ge(S["h_act" if k % 2 else "h_dve"], k // 2)
                for t in range(3):
                    n = TR[t]
                    last = nc.tensor.transpose(b[:, TC[t]], xn[0:n, t, k * P:k * P + P], ident[0:n, 0:n])
                last.then_inc(S["xn_t"], 1)

            g = [0]

            def free_bank():
                n = g[0]
                if n >= PROJ_BANKS:
                    who = GROUPS[n - PROJ_BANKS][2]
                    pe.wait_ge(S["taken_act" if who == "act" else "taken_dve"], taken_count(n - PROJ_BANKS, who))
                return bank[n % PROJ_BANKS]

            def close(ins):
                g[0] += 1
                ins.then_inc(S["proj_ready"], 1)

            state = {}

            def feat(i, rhs):
                if i % 4 == 0:
                    state["w"] = chunk()
                b = free_bank()
                for k in range(KT):
                    last = mm(b[:, 0:T], state["w"][:, k, (i % 4) * P:(i % 4 + 1) * P], rhs[:, k, :],
                              start=(k == 0), stop=(k == KT - 1))
                close(last)

            def tok(i, lhs):
                if i % 3 == 0:
                    state["w"] = chunk()
                b = free_bank()
                t = i % 3
                for k in range(KT):
                    last = mm(b[0:TR[t], :], lhs[:, k, TC[t]], state["w"][:, k, :], start=(k == 0), stop=(k == KT - 1))
                close(last)

            pe.wait_ge(S["h_dve"], KT // 2)
            pe.wait_ge(S["h_act"], KT // 2)
            pe.wait_ge(S["lra_in"], 48)
            b = free_bank()
            for k in range(KT):
                last = mm(b[0:RANK, 0:T], w_lra[:, k, :], hT[:, k, :], start=(k == 0), stop=(k == KT - 1))
            close(last)
            for i in range(4):
                feat(i, hT)
            pe.wait_ge(S["taken_act"], 1)
            pe.wait_ge(S["const_ready"], 2)
            for t in range(3):
                mm(bank[3 + t][0:TR[t], :], lraT[0:RANK + 1, TC[t]], wa2[0:RANK + 1, :], start=True, stop=True)\
                    .then_inc(S["xla_ps"], 1)
            for i in range(4):
                feat(i, hT)
            for i in range(3):
                tok(i, hT)
            pe.wait_ge(S["la_ready"], 3)
            for h in range(GH):
                b = bank[3 + h]
                hs = slice(h * DK, h * DK + DK)
                mm(b[:, 0:SEQ], la[:, 0, hs], tri_tau[:, :], start=True, stop=False, skip_group_check=True)
                mm(b[:, 128:SEQ], la[:, 1, hs], tri_tau[:, 0:P], start=False, stop=True, skip_group_check=True)
                mm(b[:, SEQ:T], la[0:64, 2, hs], tri_tau[0:64, 0:64], start=False, stop=True, skip_group_check=True)\
                    .then_inc(S["b_ps"], 1)
            for i in range(3, 6):
                tok(i, hT)

            def level(n):
                lhs, rhs = (ka, qa) if n == 0 else (pd[n % 2], pd[n % 2])
                if n:
                    pe.wait_ge(S["pd_ready"], n)
                else:
                    pe.wait_ge(S["b_ready"], 1)
                if n == LEVELS:
                    for h in range(GH):
                        last = mm(bank[6][:, h * P:h * P + P], lhs[:, h, TC[0]], rhs[:, h, TC[1]], start=True, stop=True)
                    last.then_inc(S["lev_ps"], 1)
                    return
                if n:
                    pe.wait_ge(S["lev_taken"], n)
                for h in range(GH):
                    for t in range(2):
                        last = mm(bank[3 + t][:, h * P:h * P + P], lhs[:, h, TC[t]], rhs[:, h, TC[t]], start=True, stop=True)
                    if n < 7:
                        last = mm(bank[5][0:64, h * 64:h * 64 + 64], lhs[:, h, SEQ:T], rhs[:, h, SEQ:T], start=True, stop=True)
                last.then_inc(S["lev_ps"], 1)

            def second(i):
                if i < 16:
                    feat(i % 8, hT)
                else:
                    tok(i - 16, hT)

            for i in range(22):
                second(i)
                if i % 2 == 1 and i // 2 <= LEVELS:
                    level(i // 2)
            pe.wait_ge(S["ke_ready"], 1)
            pe.wait_ge(S["lev_taken"], LEVELS + 1)
            for t in range(3):
                n = TR[t]
                for h in range(GH):
                    last = nc.tensor.transpose(bank[3 + t][0:n, h * P:h * P + P], ke[:, h, TC[t]], ident[:, :])
                last.then_inc(S["ke_t"], 1)
            pe.wait_ge(S["misc_in"], 64)
            for j in range(KT):
                last = nc.tensor.transpose(bank[6 + j // 4][:, (j % 4) * P:(j % 4 + 1) * P],
                                           ck[j // 4][:, (j % 4) * P:(j % 4 + 1) * P], ident[:, :])
            last.then_inc(S["ck_t"], 1)
            pe.wait_ge(S["ket_ready"], 3)
            pe.wait_ge(S["ck_ready"], 2)
            for p in range(2):
                b = bank[6 + p]
                for h in (2 * p, 2 * p + 1):
                    c = slice((h % 2) * DV, (h % 2 + 1) * DV)
                    hv = slice(h * DV, h * DV + DV)
                    for t in range(2):
                        last = mm(b[:, c], ket[:, t, h * DK:h * DK + DK], va[:, t, hv], start=(t == 0), stop=(t == 1))
                last.then_inc(S["st_ps"], 1)
            for p in range(2):
                b = bank[3 + p]
                for h in (2 * p, 2 * p + 1):
                    c = slice((h % 2) * DV, (h % 2 + 1) * DV)
                    last = mm(b[:, c], ket[0:64, 2, h * DK:h * DK + DK], va[0:64, 2, h * DV:h * DV + DV], start=True, stop=True)
                last.then_inc(S["st_ps"], 1)
            pe.wait_ge(S["lev_added"], LEVELS - 1)
            pe.wait_ge(S["qe_ready"], 1)
            for n in range(6):
                t, p = divmod(n, 2)
                b = bank[5 + n % 3]
                if n == 1:
                    pe.wait_ge(S["st_ready"], 1)
                elif n == 2:
                    pe.wait_ge(S["st_ready"], 2)
                elif n >= 3:
                    pe.wait_ge(S["go_ready"], n - 2)
                for h in (2 * p, 2 * p + 1):
                    c = slice((h % 2) * DV, (h % 2 + 1) * DV)
                    hv = slice(h * DV, h * DV + DV)
                    if t == 0:
                        last = mm(b[:, c], acc[:, 0, h, :], va[:, 0, hv], start=True, stop=True)
                    elif t == 1:
                        mm(b[:, c], cross[:, h, :], va[:, 0, hv], start=True, stop=False)
                        last = mm(b[:, c], acc[:, 1, h, :], va[:, 1, hv], start=False, stop=True)
                    else:
                        mm(b[0:64, c], acc[0:64, 2, h, 0:64], va[0:64, 2, hv], start=True, stop=False)
                        last = mm(b[0:64, c], pd[1][:, h, 0:DSEQ], s0[:, h, :], start=False, stop=True)
                last.then_inc(S["go_ps"], 1)

            def scores(h):
                z, j, r = bank[5 + h % 3], h // 2, slice(64 * (h % 2), 64 * (h % 2) + 64)
                if h < 3:
                    pe.wait_ge(S["go_ready"], 6)
                else:
                    pe.wait_ge(S["w_ready"], h - 2)
                mm(z[:, :], ident_b[:, :], mask_sb[:, :], start=True, stop=False, skip_group_check=True)
                mm(z[:, 0:256], kb[r, j, 0:128], qb[r, j, 0:256], start=False, stop=False, skip_group_check=True)
                mm(z[:, 256:384], kb[r, j, 128:256], qb[r, j, 128:256], start=False, stop=False, skip_group_check=True)
                mm(z[:, 384:448], ckT[r, j, :], qb[r, j, SEQ:T], start=False, stop=False, skip_group_check=True)
                mm(z[:, 448:512], kb[r, j, SEQ:T + 64], qb[r, j, SEQ:T], start=False, stop=True, skip_group_check=True)\
                    .then_inc(S["z_ready"], 1)

            def rest(h):
                z, s = bank[5 + h % 3], sp_[h % 2]
                pe.wait_ge(S["sp_ready"], h + 1)
                mm(z[:, :], neg_tri[:, :], s[:, :], start=False, stop=False, skip_group_check=True)
                mm(z[:, 128:256], neg_ones[:, :], s[:, 256:384], start=False, stop=False, skip_group_check=True)
                mm(z[:, 384:448], neg_ones[:, :], s[:, 448:512], start=False, stop=True, skip_group_check=True)\
                    .then_inc(S["rest_ready"], 1)

            def attend(h):
                j, r, w = h // 2, slice(64 * (h % 2), 64 * (h % 2) + 64), wgt[h % 2]
                b, hd = bank[3 + j % 2], slice(h * SD, h * SD + SD)
                pe.wait_ge(S["w_ready"], h + 1)
                if h < 4:
                    pe.wait_ge(S["st_ready"], 4)
                elif h % 2 == 0:
                    pe.wait_ge(S["o_taken"], j - 1)
                mm(b[r, 0:256], vb[:, 0, hd], w[:, 0:256], start=True, stop=False, skip_group_check=True)
                mm(b[r, 128:256], vb[:, 1, hd], w[:, 256:384], start=False, stop=True, skip_group_check=True)
                mm(b[r, 256:T], cv[:, hd], w[:, 384:448], start=False, stop=False, skip_group_check=True)
                last = mm(b[r, 256:T], vb[0:64, 2, hd], w[0:64, 448:512], start=False, stop=True, skip_group_check=True)
                if h % 2:
                    last.then_inc(S["o_ready"], 1)

            done = 0
            for i in range(SH + 2):
                if i < SH:
                    scores(i)
                if 1 <= i <= SH:
                    rest(i - 1)
                if i >= 2:
                    attend(i - 2)
                while done < min(24, (i + 1) * 3 // 2):
                    feat(done % 8, hT)
                    done += 1
            for n in range(6):
                t, c = divmod(n, 2)
                b = bank[5 + n % 3]
                if n >= 3:
                    pe.wait_ge(S["kb_tok"], n - 2)
                elif n == 0:
                    pe.wait_ge(S["w_ready"], SH)
                for j in range(4):
                    last = nc.tensor.transpose(b[0:TR[t], j * P:j * P + P], kb[:, 4 * c + j, TC[t]], ident[:, :])
                last.then_inc(S["kb_t"], 1)
            pe.wait_ge(S["kb_tok"], 6)
            cond(8, 16)
            pe.wait_ge(S["on_ready"], 1)
            for j in range(KT):
                b = bank[3 + j % 2]
                if j >= 2:
                    pe.wait_ge(S["oa_ready"], j - 1)
                else:
                    pe.wait_ge(S["o_taken"], KT)
                for t in range(3):
                    n = TR[t]
                    last = nc.tensor.transpose(b[:, TC[t]], on[0:n, t, j * P:j * P + P], ident[0:n, 0:n])
                last.then_inc(S["on_t"], 1)
            pe.wait_ge(S["oa_ready"], KT)
            for i in range(8):
                feat(i, oaT)
            for i in range(8):
                feat(i, obT)
            pe.wait_ge(S["merged_ready"], KT)
            for i in range(8):
                feat(i, merged)
            for n in range(6):
                t, c = divmod(n, 2)
                b = bank[5 + n % 3]
                pe.wait_ge(S["taken_dve"], 2 * KT + 4 * c + 4)
                if n >= 3:
                    pe.wait_ge(S["gm_added"], n - 2)
                for j in range(4):
                    last = nc.tensor.transpose(b[0:TR[t], j * P:j * P + P], gmT[:, 4 * c + j, TC[t]], ident[:, :])
                last.then_inc(S["gm_t"], 1)
            for n in range(2 * KT):
                g_, j = divmod(n, KT)
                pe.wait_ge(S["gfr_in"], n + 1)
                if n >= 8:
                    pe.wait_ge(S["gf_ready"], 2)
                mm(bank[1 + j // 4][:, (j % 4) * P:(j % 4 + 1) * P], ones[:, :], diag[:, :], start=True, stop=True)\
                    .then_inc(S["gfr_ps"], 1)
            pe.wait_ge(S["norm_ready"], 1)
            for k in range(KT):
                b = bank[3 + k % 2]
                if k >= 2:
                    pe.wait_ge(S["h2_ready"], k - 1)
                for t in range(3):
                    n = TR[t]
                    last = nc.tensor.transpose(b[:, TC[t]], x2n[0:n, t, k * P:k * P + P], ident[0:n, 0:n])
                last.then_inc(S["norm_t"], 1)
            pe.wait_ge(S["h2_ready"], KT)
            pe.wait_ge(S["x1_in"], 96)
            for t in range(3):
                lo = bank[0][0:TR[t], 40 * t:40 * t + NG + E]
                for k in range(KT):
                    mm(lo, h2T[:, k, TC[t]], w_route[:, k, :], start=(k == 0), stop=False)
                mm(lo, ones[0:1, 0:TR[t]], b_route[:, :], start=False, stop=True).then_inc(S["lg_ps"], 1)
            for n in range(6):
                t, c = divmod(n, 2)
                b = bank[5 + n % 3]
                if n >= 3:
                    pe.wait_ge(S["hb_ready"], n - 2)
                for j in range(4):
                    last = nc.tensor.transpose(b[0:TR[t], j * P:j * P + P], h2T[:, 4 * c + j, TC[t]], ident[:, :])
                last.then_inc(S["hb_t"], 1)
            pe.wait_ge(S["rank_in"], 1)
            for t in range(3):
                r = bank[1][:, E * t:E * t + E]
                for u in range(t):
                    mm(r, ones[:, :], chosen[:, u, :], start=(u == 0), stop=False)
                mm(r, tri_strict[:, :], chosen[:, t, :], start=(t == 0), stop=True)
            for t in range(3):
                last = mm(bank[1][:, 128:129], rep[:, t, :, :].rearrange("p j e -> p (j e)"),
                          ones[:, 0:1], start=(t == 0), stop=(t == 2))
            last.then_inc(S["rank_ps"], 1)
            pe.wait_ge(S["flag_ready"], 1)
            mm(bank[2][:, 0:1], tri_strict[:, :], flags[:, 0:1], start=True, stop=True).then_inc(S["xr_ps"], 1)
            pe.wait_ge(S["pick_ready"], 1)
            mm(bank[2][:, 64:64 + EXTRA], q_rep[:, :], pick[:, :], start=True, stop=True)
            mm(bank[2][0:1, 96:96 + EXTRA], q_iota[:, 0:1], pick[:, :], start=True, stop=True)
            mm(bank[2][0:1, 128:129], flags[:, 0:1], ones[:, 0:1], start=True, stop=True).then_inc(S["plan_ps"], 1)

            def gather(n):
                pe.wait_ge(S["onehot_ready"], n + 1)
                for t in range(3):
                    m = TR[t]
                    for c in range(2):
                        mm(bank[0][64 * c:64 * c + 64, :], onehot[0:m, t, :], hf[0:m, t, c * CB:c * CB + CB],
                           start=(t == 0), stop=(t == 2), skip_group_check=True)
                for t in range(3):
                    m = TR[t]
                    for c in range(2):
                        last = mm(bank[5][64 * c:64 * c + 64, 0:1], onehot[0:m, t, :], vcol[0:m, t:t + 1],
                                  start=(t == 0), stop=(t == 2), skip_group_check=True)
                last.then_inc(S["gather_ps"], 1)

            def turn_rows(n):
                pe.wait_ge(S["xrow_ready"], n + 1)
                if not isinstance(n, int):
                    pe.sem_inc(S["pe_passed"], 1)
                for q in range(4):
                    last = nc.tensor.transpose(bank[2][:, q * P:q * P + P], xrow[:, q * P:q * P + P], ident[:, :])
                last.then_inc(S["xg_t"], 1)

            def gate_up(n, s, turn):
                pe.wait_ge(S["xg_ready"], n + 1)
                pe.wait_ge(chunk_in[s], turn(s))
                pe.wait_ge(chunk_in[s + 1], turn(s + 1))
                for k in range(KT):
                    for q in range(2):
                        last = mm(bank[1][64 * q:64 * q + 64, :], xg[:, k % 4, k // 4, :],
                                  ring[s + q][:, k * FF:k * FF + FF], start=(k == 0), stop=(k == KT - 1),
                                  skip_group_check=True)
                last.then_inc(S["gu_ps"], 1)

            def turn_hidden(n):
                pe.wait_ge(S["hrow_ready"], n + 1)
                if not isinstance(n, int):
                    pe.sem_inc(S["pe_passed"], 1)
                for f in range(FT):
                    last = nc.tensor.transpose(bank[6][:, f * SLOTS:(f + 1) * SLOTS], gs[0:SLOTS, f * P:f * P + P],
                                               ident[0:SLOTS, 0:SLOTS])
                last.then_inc(S["he_t"], 1)

            def down(n, s, turn):
                pe.wait_ge(S["he_ready"], n + 1)
                pe.wait_ge(chunk_in[s + 2], turn(s + 2))
                if not isinstance(n, int) or n:
                    pe.wait_ge(S["ys_ready"], n)
                for f in range(FT):
                    for c in range(2):
                        last = mm(bank[3][64 * c:64 * c + 64, :], he[:, f, :],
                                  ring[s + 2][:, f * D + c * CB:f * D + c * CB + CB], start=(f == 0),
                                  stop=(f == FT - 1), skip_group_check=True)
                last.then_inc(S["down_ps"], 1)

            def step(e, s, use):
                gate_up(e, s, use)
                gather(e + 1)
                turn_hidden(e)
                turn_rows(e + 1)
                down(e, s, use)

            pe.wait_ge(S["plan_ready"], 1)
            pe.wait_ge(S["hb_ready"], 6)
            pe.wait_ge(S["gf_ready"], 4)
            gather(0)
            turn_rows(0)
            step(0, 0, lambda s: expert_use(s, 0))
            with pe.Fori(0, (E - 2) // 3) as it:
                for r in range(1, 4):
                    step(it * 3 + r, 3 * (r % 3), lambda s, r=r: it * 16 + expert_use(s, r // 3))
            last_use = lambda s: expert_use(s, (E - 1) // 3)
            gate_up(E - 1, 3 * ((E - 1) % 3), last_use)
            turn_hidden(E - 1)
            down(E - 1, 3 * ((E - 1) % 3), last_use)
            n_over = pe.value_load(plan_i[0:1, 2 * EXTRA:2 * EXTRA + 1], min_val=0, max_val=EXTRA)
            with pe.If(n_over > 0):
                with pe.Fori(0, n_over) as i:
                    use = lambda s: i * 16 + expert_use(s, len(range(0, E, 3)))
                    gather(i + E)
                    turn_rows(i + E)
                    gate_up(i + E, 0, use)
                    turn_hidden(i + E)
                    down(i + E, 0, use)
                pe.nop()
            with pe.Else():
                pe.nop()

        @block.vector
        def _(dve):
            V = nc.vector
            ch = Chain(dve, S["dve_chain"])

            def tile_stats(i0, src, n):
                for c in range(2):
                    ch.add(V.bn_stats(stats[0:n, i0, 6 * c:6 * c + 6], src[:, c * 512:c * 512 + 512]))
                ch.done()
                return V.bn_aggr(mv[0:n, i0, :], stats[0:n, i0, :])

            dve.wait_ge(S["const_ready"], 1)
            dve.wait_ge(S["x_in"], 32)
            for t in range(3):
                last = tile_stats(t, xt[0:TR[t], t, :], TR[t])
            last.then_inc(S["nrm_sum"], 1)
            dve.wait_ge(S["silu_ready"], 1)
            ch.add(V.tensor_copy(cols[:, :], bank[7][:, 0:72]))
            dve.wait_ge(S["rstd_ready"], 1)
            for t in range(3):
                n = TR[t]
                V.tensor_scalar(xn[0:n, t, :], xt[0:n, t, :], mv[0:n, t, 0:1], rstd[0:n, t:t + 1], ALU.subtract,
                                ALU.mult).then_inc(S["xn_ready"], 1)

            def take_mod(first, n):
                ch.done()
                for g_ in range(2):
                    ch.add(V.tensor_tensor(mod[:, first:first + n, g_],
                                           bank[6][:, 2 * first:2 * (first + n)].rearrange("p (j g) -> p j g", g=2)[:, :, g_],
                                           cols[:, 16 + first:16 + first + n], ALU.add))
                ch.done()
                s = 8 if first == 0 else 32
                V.tensor_scalar(mod[:, s:s + 8, :], mod[:, s:s + 8, :], 1.0, None, ALU.add).then_inc(S["mod_ready"], 1)

            dve.wait_ge(S["cond_done"], 4)
            take_mod(0, 16)
            dve.wait_ge(S["mod_ready"], 1)
            for k in range(0, KT, 2):
                dve.wait_ge(S["xn_t"], k + 1)
                for g_, c in ((0, slice(0, SEQ)), (1, slice(SEQ, T))):
                    last = V.tensor_scalar(hT[:, k, c], bank[3 + k % 2][:, c], mod[:, KT + k, g_:g_ + 1],
                                           mod[:, k, g_:g_ + 1], ALU.mult, ALU.add)
                last.then_inc(S["h_dve"], 1)
            for t in range(3):
                n = TR[t]
                dve.wait_ge(S["exp_ready"], t + 1)
                V.scalar_tensor_tensor(out=la[0:n, t, :], in0=bank[3 + t][0:n, :], scalar=0.0, in1=la[0:n, t, :],
                                       op0=ALU.min, op1=ALU.subtract).then_inc(S["la_ready"], 1)
            dve.wait_ge(S["b_ps"], GH)
            for h in range(GH):
                last = V.tensor_copy(bt[:, h, :], bank[3 + h][:, 0:T])
            last.then_inc(S["b_ready"], 1)

            def halves(t, n):
                size = 2 ** n
                if n < 7:
                    v = t[:, :, :].rearrange("p h t -> p (h t)").rearrange("p (b c) -> p b c", c=size)
                    return v[:, :, 0:size // 2], v[:, :, size // 2:size], v[:, :, size // 2 - 1:size // 2]
                v = t[:, :, 0:SEQ].rearrange("p h (b c) -> p h b c", c=size)
                return v[:, :, :, 0:size // 2], v[:, :, :, size // 2:size], v[:, :, :, size // 2 - 1:size // 2]

            def log_decay(n):
                bl, br, mid = halves(bt, n)
                dl, dr, _ = halves(pd[n % 2], n)
                if n >= 3:
                    dve.wait_ge(S["lev_ps"], n - 1)
                V.tensor_tensor(dl, mid.to_broadcast(list(bl.shape)), bl, ALU.subtract)
                V.tensor_tensor(dr, br, mid.to_broadcast(list(br.shape)), ALU.subtract).then_inc(S["dec_ready"], 1)

            def decayed(n):
                dl, dr, _ = halves(pd[n % 2], n)
                dve.wait_ge(S["exp_ready"], 3 + n)
                V.tensor_tensor(dl, dl, halves(ka, n)[0], ALU.mult)
                V.tensor_tensor(dr, dr, halves(qa, n)[1], ALU.mult).then_inc(S["pd_ready"], 1)

            def masked(n):
                dve.wait_ge(S["lev_ps"], n + 1)
                if n == LEVELS:
                    V.tensor_copy(cross[:, :, :].rearrange("p h t -> p (h t)"), bank[6][:, :]).then_inc(S["lev_taken"], 1)
                    return
                if n >= 2:
                    dve.wait_ge(S["lev_added"], n - 1)
                mask = levels[:, n, :].unsqueeze(1)
                for t in range(2):
                    dst = acc[:, t, :, :] if n == 0 else mtmp[:, t, :].rearrange("p (h t) -> p h t", h=GH)
                    last = V.tensor_tensor(dst, bank[3 + t][:, :].rearrange("p (h t) -> p h t", h=GH),
                                           mask.to_broadcast([P, GH, P]), ALU.mult)
                if n < 7:
                    dst = acc[0:64, 2, :, 0:64] if n == 0 else mtmp_s[:, :, :]
                    last = V.tensor_tensor(dst, bank[5][0:64, 0:256].rearrange("p (h t) -> p h t", h=GH),
                                           levels[0:64, n, 0:64].unsqueeze(1).to_broadcast([64, GH, 64]), ALU.mult)
                last.then_inc(S["lev_taken"], 1)

            dve.wait_ge(S["const_ready"], 2)
            dve.wait_ge(S["b_ready"], 1)
            dve.wait_ge(S["taken_act"], 9)
            log_decay(1)
            log_decay(2)
            decayed(1)
            masked(0)
            for n in range(2, LEVELS + 1):
                decayed(n)
                masked(n - 1)
                if n < LEVELS:
                    log_decay(n + 1)
            masked(LEVELS)
            dve.wait_ge(S["kd_ready"], 1)
            V.tensor_tensor(ke[:, :, :], ke[:, :, :], ka[:, :, :], ALU.mult).then_inc(S["ke_ready"], 1)
            ch.add(V.tensor_copy(small[:, 8:12], pd[1][:, :, DSEQ - 1]))
            ch.done()
            V.tensor_tensor(pd[1][:, :, 0:DSEQ], pd[1][:, :, 0:DSEQ], qa[:, :, SEQ:T], ALU.mult).then_inc(S["qe_ready"], 1)
            for t in range(3):
                dve.wait_ge(S["ke_t"], t + 1)
                V.tensor_copy(ket[0:TR[t], t, :], bank[3 + t][0:TR[t], :]).then_inc(S["ket_ready"], 1)
            dve.wait_ge(S["ck_t"], 1)
            for c in range(2):
                V.tensor_copy(ckT[:, 4 * c:4 * c + 4, :].rearrange("p k s -> p (k s)"), bank[6 + c][:, :]).then_inc(S["ck_ready"], 1)
            for p in range(2):
                dve.wait_ge(S["st_ps"], p + 1)
                V.tensor_copy(sp_[p][:, :], bank[6 + p][:, :]).then_inc(S["st_ready"], 1)
            for p in range(2):
                dve.wait_ge(S["st_ps"], 3 + p)
                for h in (2 * p, 2 * p + 1):
                    last = V.scalar_tensor_tensor(out=ab[p][:, (h % 2) * DV:(h % 2 + 1) * DV], in0=s0[:, h, :], scalar=small[:, 8 + h:9 + h],
                                                  in1=bank[3 + p][:, (h % 2) * DV:(h % 2 + 1) * DV], op0=ALU.mult, op1=ALU.add)
                last.then_inc(S["st_ready"], 1)
            for n in range(6):
                t, p = divmod(n, 2)
                m = TR[t]
                dve.wait_ge(S["go_ps"], n + 1)
                V.tensor_copy(on[0:m, t, p * 512:p * 512 + 512], bank[5 + n % 3][0:m, :])
                for h in range(2):
                    ins = V.bn_stats(stats[0:m, 4 * t + 2 * p + h, 0:6], bank[5 + n % 3][0:m, h * DV:h * DV + DV])
                ins.then_inc(S["go_ready"], 1)
            dve.wait_ge(S["go_ready"], 6)
            ch.done()
            for i in range(12):
                m = TR[i // 4]
                ch.add(V.bn_aggr(mv[0:m, i, :], stats[0:m, i, 0:6]))
            ch.done()
            ch.add(V.tensor_tensor(mv[:, :, 0], mv[:, :, 0], mv[:, :, 0], ALU.mult))
            ch.done()
            V.tensor_tensor(mv[:, :, 1], mv[:, :, 1], mv[:, :, 0], ALU.add).then_inc(S["nrm_sum"], 1)

            def soft_sum(h):
                dve.wait_ge(S["l_ready"], h + 1)
                if h >= 2:
                    dve.wait_ge(S["rest_ready"], h - 1)
                V.scalar_tensor_tensor(out=sp_[h % 2][:, :], in0=bank[5 + h % 3][:, :], scalar=0.0, in1=ab[h % 2][:, :],
                                       op0=ALU.max, op1=ALU.add).then_inc(S["sp_ready"], 1)

            def take_o(j):
                dve.wait_ge(S["o_ready"], j + 1)
                V.tensor_copy(obT[:, j, :], bank[3 + j % 2][:, 0:T]).then_inc(S["o_taken"], 1)

            dve.wait_ge(S["gla_stored"], 16 * 6)
            dve.wait_ge(S["ck_ready"], 2)
            for i in range(SH + 2):
                if i < SH:
                    soft_sum(i)
                if i == 2:
                    dve.wait_ge(S["rstd_ready"], 2)
                    for n in range(12):
                        t, h = divmod(n, GH)
                        m = TR[t]
                        v = on[0:m, t, h * DV:h * DV + DV]
                        last = V.tensor_scalar(v, v, rstd[0:m, n:n + 1], None, ALU.mult)
                    last.then_inc(S["on_ready"], 1)
                if i >= 3 and i % 2 == 1:
                    take_o((i - 3) // 2)
            for n in range(6):
                t, c = divmod(n, 2)
                dve.wait_ge(S["kb_t"], n + 1)
                V.tensor_copy(kbtok[0:TR[t], t, c * 512:c * 512 + 512], bank[5 + n % 3][0:TR[t], :]).then_inc(S["kb_tok"], 1)
            dve.wait_ge(S["cond_done"], 12)
            take_mod(16, 32)
            dve.wait_ge(S["sig_ready"], 1)
            for j in range(KT):
                dve.wait_ge(S["on_t"], j + 1)
                V.scalar_tensor_tensor(out=oaT[:, j, :], in0=bank[3 + j % 2][:, 0:T], scalar=cols[:, 64 + j:65 + j],
                                       in1=ga[:, j, :], op0=ALU.mult, op1=ALU.mult).then_inc(S["oa_ready"], 1)
            g0 = GROUPS.index(("ba", 0, "dve"))
            for j in range(KT):
                n = g0 + j
                dve.wait_ge(S["proj_ready"], n + 1)
                V.tensor_tensor(merged[:, j, :], bank[n % PROJ_BANKS][:, 0:T], gta[:, j, :], ALU.mult).then_inc(S["taken_dve"], 1)
            for j in range(KT):
                n = g0 + 8 + j
                dve.wait_ge(S["proj_ready"], n + 1)
                V.tensor_tensor(gtb[:, j, :], bank[n % PROJ_BANKS][:, 0:T], gtb[:, j, :], ALU.mult).then_inc(S["taken_dve"], 1)
            dve.wait_ge(S["mod_ready"], 2)
            for j in range(KT):
                n = g0 + 16 + j
                src = bank[n % PROJ_BANKS]
                dve.wait_ge(S["proj_ready"], n + 1)
                if j == 0:
                    dve.wait_ge(S["merged_ready"], KT)
                V.tensor_scalar(gmT[:, j, 0:SEQ], src[:, 0:SEQ], mod[:, 16 + j, 0:1], None, ALU.mult)
                V.tensor_scalar(gmT[:, j, SEQ:T], src[:, SEQ:T], mod[:, 16 + j, 1:2], None, ALU.mult)\
                    .then_inc(S["taken_dve"], 1)
            dve.wait_ge(S["x1_in"], 96)
            for n in range(6):
                t, c = divmod(n, 2)
                m = TR[t]
                v = x1[0:m, t, c * 512:c * 512 + 512]
                dve.wait_ge(S["gm_t"], n + 1)
                V.scalar_tensor_tensor(out=v, in0=v, scalar=ALPHA, in1=bank[5 + n % 3][0:m, :], op0=ALU.mult,
                                       op1=ALU.add).then_inc(S["gm_added"], 1)
            for n in range(2 * KT):
                g_, j = divmod(n, KT)
                if n:
                    dve.wait_ge(S["gfr_ps"], n)
                if n == 8:
                    for c in range(2):
                        V.tensor_copy(gf_rows[:, 0, c * 512:c * 512 + 512], bank[1 + c][:, :]).then_inc(S["gf_ready"], 1)
                V.tensor_scalar(diag[:, :], ident[:, :], mod[:, 40 + j, g_:g_ + 1], None, ALU.mult).then_inc(S["gfr_in"], 1)
            dve.wait_ge(S["gfr_ps"], 16)
            for c in range(2):
                V.tensor_copy(gf_rows[:, 1, c * 512:c * 512 + 512], bank[1 + c][:, :]).then_inc(S["gf_ready"], 1)
            dve.wait_ge(S["gm_added"], 6)

            def norm_stats():
                for t in range(3):
                    last = tile_stats(t, x1[0:TR[t], t, :], TR[t])
                last.then_inc(S["nrm_sum"], 1)

            def affine_norm(vec):
                for t in range(3):
                    m = TR[t]
                    ch.add(V.scalar_tensor_tensor(out=x1[0:m, t, :], in0=x1[0:m, t, :], scalar=mv[0:m, t, 0:1],
                                                  in1=vec[0:m, 0, :], op0=ALU.subtract, op1=ALU.mult))
                ch.done()
                for t in range(3):
                    m = TR[t]
                    yield V.scalar_tensor_tensor(out=x1[0:m, t, :], in0=x1[0:m, t, :], scalar=rstd[0:m, t:t + 1],
                                                 in1=vec[0:m, 1, :], op0=ALU.mult, op1=ALU.add)

            norm_stats()
            dve.wait_ge(S["vecs_in"], 32)
            dve.wait_ge(S["rstd_ready"], 3)
            for ins in affine_norm(ln1):
                ch.add(ins)
            ch.done()
            norm_stats()
            dve.wait_ge(S["rstd_ready"], 4)
            for t in range(3):
                m = TR[t]
                last = V.tensor_scalar(x2n[0:m, t, :], x1[0:m, t, :], mv[0:m, t, 0:1], rstd[0:m, t:t + 1],
                                       ALU.subtract, ALU.mult)
            last.then_inc(S["norm_ready"], 1)
            for k in range(KT):
                dve.wait_ge(S["norm_t"], k + 1)
                b = bank[3 + k % 2]
                V.tensor_scalar(h2T[:, k, 0:SEQ], b[:, 0:SEQ], mod[:, 32 + k, 0:1], mod[:, 24 + k, 0:1], ALU.mult, ALU.add)
                V.tensor_scalar(h2T[:, k, SEQ:T], b[:, SEQ:T], mod[:, 32 + k, 1:2], mod[:, 24 + k, 1:2], ALU.mult,
                                ALU.add).then_inc(S["h2_ready"], 1)
            ch.add(V.memset(lg[:, :, :], 0.0))
            ch.done()
            dve.wait_ge(S["lg_ps"], 3)
            for t in range(3):
                V.tensor_copy(lg[0:TR[t], t, :], bank[0][0:TR[t], 40 * t:40 * t + NG + E]).then_inc(S["lg_ready"], 1)
            for n in range(6):
                t, c = divmod(n, 2)
                dve.wait_ge(S["hb_t"], n + 1)
                V.tensor_copy(hf[0:TR[t], t, c * 512:c * 512 + 512], bank[5 + n % 3][0:TR[t], :]).then_inc(S["hb_ready"], 1)
            dve.wait_ge(S["lg_ready"], 3)

            def op(ins):
                ch.add(ins)
                ch.done()

            gl, el = lg[:, :, 0:NG], lg[:, :, NG:NG + E]

            def wide(col, n):
                return col.unsqueeze(2).to_broadcast([P, 3, n])

            def first_max(vals, iota, n, top, tmp, oh):
                op(V.tensor_reduce(top, vals, AXX, ALU.max))
                op(V.tensor_tensor(tmp, vals, wide(top, n), ALU.is_ge))
                op(V.scalar_tensor_tensor(out=tmp, in0=tmp, scalar=-100.0, in1=iota, op0=ALU.mult, op1=ALU.add))
                op(V.tensor_reduce(r1[:, 15, :], tmp, AXX, ALU.min))
                op(V.tensor_tensor(oh, tmp, wide(r1[:, 15, :], n), ALU.is_equal))

            first_max(gl, g_iota[:, :, :], NG, r1[:, 0, :], r4[2][:, :, :], r4[3][:, :, :])
            V.tensor_tensor(r4[0][:, :, :], gl, wide(r1[:, 0, :], NG), ALU.subtract).then_inc(S["ex_in"], 1)
            op(V.tensor_scalar(r4[2][:, :, :], r4[3][:, :, :], 1.0, -NEG, ALU.subtract, ALU.mult))
            selm, tmp32, oh1 = (r[:, :, :] for r in r32)
            for t in range(3):
                ch.add(V.tensor_tensor(r32[0][:, t, :].rearrange("p (g e) -> p g e", g=NG),
                                       lg[:, t, NG:NG + E].rearrange("p (g e) -> p g e", g=NG),
                                       r4[2][:, t, :].unsqueeze(2).to_broadcast([P, NG, EPG]), ALU.add))
            ch.done()
            first_max(selm, e_iota[:, :, :], E, r1[:, 1, :], tmp32, oh1)
            op(V.scalar_tensor_tensor(out=selm, in0=oh1, scalar=2 * NEG, in1=selm, op0=ALU.mult, op1=ALU.add))
            first_max(selm, e_iota[:, :, :], E, r1[:, 2, :], tmp32, oh2[:, :, :])
            V.tensor_tensor(r1[:, 4, :], r1[:, 2, :], r1[:, 1, :], ALU.subtract).then_inc(S["ex_in"], 1)
            op(V.tensor_tensor(chosen[:, :, :], oh1, oh2[:, :, :], ALU.add))
            op(V.tensor_tensor(chosen[:, :, :], chosen[:, :, :], wide(valid[:, :], E), ALU.mult))
            op(V.tensor_copy(q_rep[:, :], q_iota[:, 1:2].to_broadcast([P, P])))
            for t in range(3):
                last = V.tensor_copy(rep[:, t, :, :], chosen[:, t, :].unsqueeze(1).to_broadcast([P, ROUNDS, E]))
            last.then_inc(S["rank_in"], 1)
            dve.wait_ge(S["ex_out"], 2)
            op(V.tensor_reduce(r1[:, 6, :], r4[1][:, :, :], AXX, ALU.add))
            op(V.tensor_scalar(r1[:, 7, :], r1[:, 5, :], 1.0, None, ALU.add))
            op(V.tensor_tensor(r1[:, 8, :], r1[:, 6, :], r1[:, 7, :], ALU.mult))
            op(V.reciprocal(wts[:, 0, :], r1[:, 8, :]))
            op(V.tensor_tensor(wts[:, 1, :], wts[:, 0, :], r1[:, 5, :], ALU.mult))
            op(V.tensor_tensor(val[:, :, :], oh2[:, :, :], wide(tokval[:, :], E), ALU.add))
            dve.wait_ge(S["rank_ps"], 1)
            op(V.scalar_tensor_tensor(out=pos[:, :, :], in0=chosen[:, :, :], scalar=-FAR,
                                      in1=bank[1][:, 0:3 * E].rearrange("p (t e) -> p t e", t=3), op0=ALU.mult, op1=ALU.add))
            op(V.tensor_scalar(pos[:, :, :], pos[:, :, :], FAR, None, ALU.add))
            V.tensor_tensor(flags[:, 0:1], bank[1][:, 128:129], q_iota[:, 1:2], ALU.is_gt).then_inc(S["flag_ready"], 1)
            dve.wait_ge(S["xr_ps"], 1)
            op(V.tensor_copy(flags[:, 1:2], bank[2][:, 0:1]))
            V.tensor_scalar(pick[:, :], x_iota[:, :], flags[:, 1:2], flags[:, 0:1], ALU.is_equal, ALU.mult)\
                .then_inc(S["pick_ready"], 1)
            dve.wait_ge(S["plan_ps"], 1)
            op(V.tensor_copy(first_slot[:, :], bank[2][:, 64:64 + EXTRA]))
            op(V.tensor_copy(plan_i[0:1, 0:EXTRA], bank[2][0:1, 96:96 + EXTRA]))
            op(V.memset(plan_i[0:1, EXTRA:2 * EXTRA], 0))
            V.tensor_copy(plan_i[0:1, 2 * EXTRA:2 * EXTRA + 1], bank[2][0:1, 128:129]).then_inc(S["plan_ready"], 1)

            def one_hots(n, e, shift):
                if not isinstance(n, int) or n:
                    dve.wait_ge(S["gather_ps"], n)
                V.tensor_copy(vcol[:, :], val[:, :, bass.ds(e, 1)].rearrange("p t e -> p (t e)"))\
                    .then_inc(S["vcol_ready"], 1)
                src = pos[:, :, bass.ds(e, 1)].rearrange("p t e -> p (t e)")
                if shift is None:
                    V.tensor_copy(pcol[:, :], src).then_inc(S["pcol_ready"], 1)
                else:
                    V.tensor_scalar(pcol[:, :], src, shift, None, ALU.subtract).then_inc(S["pcol_ready"], 1)
                dve.wait_ge(S["pcol_ready"], n + 1)
                dve.wait_ge(S["vcol_ready"], n + 1)
                for t in range(3):
                    last = V.tensor_scalar(onehot[:, t, :], slot_iota[:, :], pcol[:, t:t + 1], None, ALU.is_equal)
                last.then_inc(S["onehot_ready"], 1)

            def gathered(n, r):
                dve.wait_ge(S["gather_ps"], n + 1)
                V.tensor_scalar(sidx[r][:, :], bank[5][:, 0:1], 2.0, half_base[:, 0:1], ALU.mult, ALU.add)
                dve.wait_ge(S["xg_t"], n + 1)
                V.tensor_copy(xg[:, :, :, :].rearrange("p q c s -> p (q c s)"), bank[2][:, :]).then_inc(S["xg_ready"], 1)

            def gated(n):
                dve.wait_ge(S["gs_ready"], n + 1)
                V.tensor_tensor(gs[0:SLOTS, :], gs[SLOTS:P, :], bank[1][SLOTS:P, :], ALU.mult).then_inc(S["hrow_ready"], 1)

            def turned(n):
                dve.wait_ge(S["he_t"], n + 1)
                V.tensor_copy(he[:, :, :].rearrange("p f s -> p (f s)"), bank[6][:, 0:FT * SLOTS]).then_inc(S["he_ready"], 1)

            def step(n, r):
                one_hots(n + 1, n + 1, None)
                gated(n)
                turned(n)
                gathered(n + 1, r)

            dve.wait_ge(S["plan_ready"], 1)
            one_hots(0, 0, None)
            gathered(0, 0)
            step(0, 1)
            step(1, 2)
            with dve.Fori(0, (E - 3) // 6) as it:
                for r in range(2, 8):
                    dve.wait_ge(S[f"scattered{r % 2}"], it * 48 + 16 * (r // 2))
                    step(it * 6 + r, (r + 1) % 3)
            for e in range(2 + (E - 3) // 6 * 6, E - 1):
                dve.wait_ge(S[f"scattered{e % 2}"], 16 * (e // 2))
                step(e, (e + 1) % 3)
            gated(E - 1)
            turned(E - 1)
            n_over = dve.value_load(plan_i[0:1, 2 * EXTRA:2 * EXTRA + 1], min_val=0, max_val=EXTRA)
            with dve.If(n_over > 0):
                with dve.Fori(0, n_over) as i:
                    e = dve.value_load(plan_i[0:1, bass.ds(i, 1)], min_val=0, max_val=E - 1)
                    dve.wait_ge(S["scattered0"], i * 16 + 8 * E)
                    one_hots(i + E, e, first_slot[:, bass.ds(i, 1)])
                    gathered(i + E, 0)
                    gated(i + E)
                    turned(i + E)
                dve.nop()
            with dve.Else():
                dve.nop()
            for t in range(3):
                m = TR[t]
                y1, y2 = comb[t][0:m, 0:D], comb[t][0:m, D:2 * D]
                dve.wait_ge(S[f"comb_in{t}"], 16)
                op(V.tensor_scalar(y1, y1, wts[0:m, 0, t:t + 1], None, ALU.mult))
                op(V.scalar_tensor_tensor(out=y1, in0=y2, scalar=wts[0:m, 1, t:t + 1], in1=y1, op0=ALU.mult, op1=ALU.add))
                op(V.tensor_tensor(y1, y1, gf_rows[0:m, t // 2, :], ALU.mult))
                op(V.scalar_tensor_tensor(out=x1[0:m, t, :], in0=x1[0:m, t, :], scalar=ALPHA, in1=y1, op0=ALU.mult, op1=ALU.add))
            norm_stats()
            dve.wait_ge(S["vecs_in"], 64)
            dve.wait_ge(S["rstd_ready"], 5)
            for ins in affine_norm(ln2):
                ins.then_inc(S["fin_ready"], 1)


_INS = ['x_prompt', 'x_sample', 'cache_sb_k', 'cache_sb_v', 'state_gla', 'c_prompt', 'c_sample', 'w_cond', 'b_cond',
        'w_in', 'w_gla_a2', 'b_gla_a', 'gla_norm_g', 'w_branch_a', 'w_branch_b', 'w_out', 'ln1_g', 'ln1_b', 'w_group',
        'b_group', 'w_router', 'b_router', 'w_exp_gate', 'w_exp_up', 'w_exp_down', 'ln2_g', 'ln2_b']
_OUTS = [("y_prompt", (1, SEQ, D)), ("y_sample", (1, DSEQ, D)), ("sb_k_prompt", (1, 1, SEQ, SH, SD)),
         ("sb_v_prompt", (1, 1, SEQ, SH, SD)), ("gla_state_prompt", (1, 1, GH, DK, DV)),
         ("sb_k_sample", (1, 1, DSEQ, SH, SD)), ("sb_v_sample", (1, 1, DSEQ, SH, SD)),
         ("gla_state_sample", (1, 1, GH, DK, DV))]


def kernel(**inputs):
    import numpy as _np
    import concourse.bacc as _bacc
    from concourse.bass_utils import run_bass_kernel_spmd as _run

    nc = _bacc.Bacc("TRN2", target_bir_lowering=False, num_devices=1)
    arrays, args, outs = {}, {}, {}
    for name in _INS:
        v = _np.ascontiguousarray(inputs[name])
        arrays[f"in_{name}"] = v
        args[name] = nc.dram_tensor(f"in_{name}", v.shape, mybir.dt.from_np(v.dtype), kind="ExternalInput").ap()
    for name, shape in _OUTS:
        outs[name] = nc.dram_tensor(f"out_{name}", shape, F32, kind="ExternalOutput").ap()
    build(nc, args, outs)
    r = _run(nc, [arrays], core_ids=[0])
    return tuple(r.results[0][f"out_{name}"] for name, _ in _OUTS)
```

```python
from contextlib import ExitStack

import concourse.bass as bass
from concourse import mybir

F32 = mybir.dt.float32
BF16 = mybir.dt.bfloat16
I32 = mybir.dt.int32
ALU = mybir.AluOpType
ACT = mybir.ActivationFunctionType
AXX = mybir.AxisListType.X

P = 128
D = 1024
KT = D // P
SEQ, DSEQ, PAST = 256, 64, 128
T = SEQ + DSEQ
TR = (128, 128, 64)
TC = (slice(0, 128), slice(128, 256), slice(256, 320))
GH, DK, DV = 4, 128, 256
SH, SD = 16, 64
RANK = 16
NG, EPG = 4, 8
E = NG * EPG
FF = 512
FT = FF // P
EPS = 1e-5
ALPHA = 2.0 ** 0.25
TAU = 16.0
NEG = -1e30
FAR = 1e4
SKIP = 100000
SLOTS = 64
EXTRA = (2 * T) // SLOTS
ROUNDS = -(-T // SLOTS) - 1
CB = 512
CW = KT * CB
DENSE_RING = 3
RING = 9
LEVELS = 8
NORM_ORDER = (0, 1, 3, 2, 4, 5)


def projection_groups():
    groups, chunks = [], []

    def chunk(matrix, col):
        chunks.append((matrix, col))
        return len(chunks) - 1

    def cond(c, part):
        groups.append(("c" + part, c, "act", chunk("cond", c * CB) if part == "r" else len(chunks) - 1))

    def stretch(items, first_cond, last_cond):
        c, per = first_cond, 4
        for i, (name, j, col) in enumerate(items):
            per = 3 if name == "vb" else 4
            if j % per == 0:
                w = chunk("in", col + j // per * CB)
            groups.append((name, j, "act", w))
            if c > first_cond and j % per == 0 and groups[-2][0] == "cr":
                cond(c - 1, "t")
            if j % per == per - 1 and c < last_cond:
                cond(c, "r")
                c += 1

    for c in range(4):
        cond(c, "r")
        cond(c, "t")
    groups.append(("lra", 0, "act", len(chunks) - 1))
    for name, first, n, per in (("qa", 0, 4, 4), ("ka", 512, 4, 4), ("va", 1024, 6, 3)):
        for i in range(n):
            if i % per == 0:
                w = chunk("in", first + i // per * CB)
            groups.append((name, i, "act", w))
    stretch([("qb", i, 3088) for i in range(8)] + [("kb", i, 4112) for i in range(8)]
            + [("vb", i, 5136) for i in range(6)], 4, 9)
    stretch([("ga", i, 2048) for i in range(8)] + [("gta", i, 6160) for i in range(8)]
            + [("gtb", i, 7184) for i in range(8)], 9, 12)
    for name in ("ba", "bb", "out"):
        for i in range(8):
            if i % 4 == 0:
                w = chunk(name, i // 4 * CB)
            groups.append((name, i, "dve", w))
    return groups, chunks


GROUPS, DENSE = projection_groups()
ND = len(DENSE)
PROJ_BANKS = 3


def group_index(name, i):
    return [g[:2] for g in GROUPS].index((name, i))


def taken_count(upto, engine):
    return sum(g[2] == engine for g in GROUPS[:upto + 1])


def build(nc, a, out):
    ctx = ExitStack()
    with ctx:
        def sb(name, shape, dt=F32, stack=ctx):
            return stack.enter_context(nc.sbuf_tensor(name, shape, dt))

        def sem(name):
            return ctx.enter_context(nc.semaphore(name))

        ident = sb("ident", [P, P])
        ones = sb("ones", [P, P])
        neg_tri = sb("neg_tri", [P, P])
        neg_ones = sb("neg_ones", [P, P])
        tri_strict = sb("tri_strict", [P, P])
        tri_tau = sb("tri_tau", [P, 2 * P])
        ident_b = sb("ident_b", [P, P], BF16)
        mask_sb = sb("mask_sb", [P, 512], BF16)
        slot_iota = sb("slot_iota", [P, SLOTS])
        iota_i = sb("iota_i", [P, SLOTS], I32)
        e_iota = sb("e_iota", [P, 3, E])
        g_iota = sb("g_iota", [P, 3, NG])
        tokval = sb("tokval", [P, 3])
        half_base = sb("half_base", [P, 1])
        valid = sb("valid", [P, 3])
        q_iota = sb("q_iota", [P, 2])
        x_iota = sb("x_iota", [P, EXTRA])
        cols = sb("cols", [P, 72])
        silu_c = sb("silu_c", [P, KT, 32])
        mod = sb("mod", [P, 6 * KT, 2])
        total = sb("total", [P, GH])
        eps_col = sb("eps_col", [P, 1])
        stats = sb("stats", [P, 12, 12])
        mv = sb("mv", [P, 12, 2])
        rstd = sb("rstd", [P, 12])
        newton = sb("newton", [P, 12])
        wts = sb("wts", [P, 2, 3])
        ring = [sb(f"ring{i}", [P, CW]) for i in range(DENSE_RING)]

        s1 = ExitStack()
        levels = sb("levels", [P, LEVELS, P], F32, s1)
        qa = sb("qa", [P, GH, T], F32, s1)
        ka = sb("ka", [P, GH, T], F32, s1)
        la = sb("la", [P, 3, 512], F32, s1)
        pd = [sb(f"pd{i}", [P, GH, T], F32, s1) for i in range(2)]
        bt = sb("bt", [P, GH, T], F32, s1)
        va = sb("va", [P, 3, D], F32, s1)
        acc = sb("acc", [P, 3, GH, P], F32, s1)
        cross = sb("cross", [P, GH, P], F32, s1)
        s0 = sb("s0", [P, GH, DV], F32, s1)
        mtmp = sb("mtmp", [P, 2, 512], F32, s1)
        mtmp_s = sb("mtmp_s", [DSEQ, GH, DSEQ], F32, s1)
        hT = sb("hT", [P, KT, T], F32, s1)
        on = sb("on", [P, 3, D], F32, s1)
        obT = sb("obT", [P, KT, T], F32, s1)
        ckT = sb("ckT", [P, KT, P], F32, s1)
        cv = sb("cv", [P, D], F32, s1)
        qb = sb("qb", [P, KT, T], F32, s1)
        kb = sb("kb", [P, KT, T + 64], F32, s1)
        vb = sb("vb", [P, 3, D], F32, s1)
        ab = [sb(f"ab{i}", [P, 512], F32, s1) for i in range(2)]
        sp_ = [sb(f"sp{i}", [P, 512], F32, s1) for i in range(2)]
        wgt = [sb(f"wgt{i}", [P, 512], F32, s1) for i in range(2)]
        w_lra = sb("w_lra", [P, KT, RANK], F32, s1)
        crow = sb("crow", [P, P], F32, s1)
        lraT = ab[1][0:32, 0:T]
        wa2 = sp_[1][0:32, :]
        rows = ab[0][:, 0:P]
        xt = vb
        xn = on
        ck = wgt
        ke = pd[0]
        ket = la
        s1.close()

        s2 = ExitStack()
        ga = sb("ga", [P, KT, T], F32, s2)
        gta = sb("gta", [P, KT, T], F32, s2)
        gtb = sb("gtb", [P, KT, T], F32, s2)
        oaT = sb("oaT", [P, KT, T], F32, s2)
        merged = sb("merged", [P, KT, T], F32, s2)
        kbtok = sb("kbtok", [P, 3, D], F32, s2)
        s2.close()
        s3 = ExitStack()
        h2T = sb("h2T", [P, KT, T], F32, s3)
        gmT = sb("gmT", [P, KT, T], F32, s3)
        s3.close()

        ring += [sb(f"ring{i}", [P, CW]) for i in range(DENSE_RING, RING)]
        x1 = sb("x1", [P, 3, D])
        hf = sb("hf", [P, 3, D])
        x2n = hf
        gf_rows = sb("gf_rows", [P, 2, D])
        ones_b = sb("ones_b", [P, P], BF16)
        tri_b = sb("tri_b", [P, P], BF16)
        w_route = sb("w_route", [P, KT, NG + E])
        b_route = sb("b_route", [NG + E, 1])
        lg = sb("lg", [P, 3, NG + E])
        r4 = [sb(f"r4_{i}", [P, 3, NG]) for i in range(4)]
        r32 = [sb(f"r32_{i}", [P, 3, E]) for i in range(3)]
        r1 = sb("r1", [P, 16, 3])
        oh2 = sb("oh2", [P, 3, E])
        chosen = sb("chosen", [P, 3, E], BF16)
        pos = sb("pos", [P, 3, E])
        val = sb("val", [P, 3, E])
        rep = sb("rep", [P, 3, ROUNDS, E], BF16)
        q_rep = sb("q_rep", [P, P])
        flags = sb("flags", [P, 4])
        pick = sb("pick", [P, EXTRA])
        plan_f = sb("plan_f", [1, 2 * EXTRA + 1])
        plan_i = sb("plan_i", [1, 2 * EXTRA + 1], I32)
        first_slot = sb("first_slot", [P, EXTRA])
        onehot = sb("onehot", [P, 3, SLOTS])
        pcol = sb("pcol", [P, 3])
        vcol = sb("vcol", [P, 3])
        sidx = [sb(f"sidx{i}", [P, 1], I32) for i in range(3)]
        s4 = ExitStack()
        ln1 = sb("ln1", [P, 2, D], F32, s4)
        s4.close()
        xrow = sb("xrow", [P, CB])
        xg = sb("xg", [P, 4, 2, SLOTS])
        gs = sb("gs", [P, FF])
        ystage = [sb(f"ystage{i}", [P, CB]) for i in range(2)]
        he = sb("he", [P, FT, SLOTS])
        diag = ystage[1]
        lgT = xrow[0:NG + E, 0:T]
        comb = [ring[3 + t // 2][:, (t % 2) * 2 * D:(t % 2 + 1) * 2 * D] for t in range(3)]
        ln2 = ring[5][:, 0:2 * D].rearrange("p (a d) -> p a d", a=2)

        ybuf = nc.dram_tensor("expert_rows", [4 * T, CB], F32, kind="Internal").ap()

        bank = [ctx.enter_context(nc.psum_tensor(f"bank{i}", [P, 512], F32)) for i in range(8)]

        names = """const_ready rows_in x_in lra_in misc_in vecs_in x1_in cols_t silu_ready mod_ready xn_ready xn_t h_dve h_act proj_ready taken_act taken_dve xla_ps la_ready b_ps b_ready
            dec_ready exp_ready pd_ready lev_ps lev_taken lev_added kd_ready ke_ready ke_t ket_ready
            st_ps st_ready qe_ready go_ps go_ready ck_t ck_ready z_ready l_ready sp_ready rest_ready w_ready
            o_ready o_taken kb_t kb_tok on_ready on_t oa_ready sig_ready merged_ready gm_t gm_added
            norm_ready norm_t h2_dve h2_act lgt_ps lgt_ready lg_ps lg_ready ex_in ex_out rank_in rank_ps pos_ready hb_t hb_ready
            flag_ready xr_ps pick_ready plan_ps plan_ready gfr_in gfr_ps gf_ready onehot_ready gather_ps xrow_ready
            xg_t xg_ready gu_ps gs_ready hrow_ready he_t he_ready down_ps ys_ready scattered0 scattered1 comb_in0 comb_in1 comb_in2
            vcol_ready pcol_ready fin_ready stored act_chain dve_chain pool_chain gla_stored rstd_ready nrm_sum
            pe_passed pool_passed""".split()
        S = {n: sem(n) for n in names}
        chunk_in = [sem(f"chunk_in{i}") for i in range(RING)]

        class Chain:

            def __init__(self, eng, s):
                self.eng, self.s, self.n = eng, s, 0

            def add(self, ins):
                self.n += 1
                return ins.then_inc(self.s, 1)

            def done(self):
                self.eng.wait_ge(self.s, self.n)

        def consumed(i):
            return S["proj_ready"], max(n for n, g in enumerate(GROUPS) if g[3] == i) + 1

        USED = ("gu_ps", "gu_ps", "down_ps")

        def dense_use(i):
            return 16 * (i // DENSE_RING + 1)

        def base(e):
            return 3 * (-e % 3)

        def expert_use(s, turn):
            before = len(range(s, ND, DENSE_RING)) if s < DENSE_RING else 0
            return 16 * (before + turn + 1)

        SRC = {"cond": a["w_cond"][0], "in": a["w_in"][0], "ba": a["w_branch_a"][0], "bb": a["w_branch_b"][0],
               "out": a["w_out"][0]}

        block = ctx.enter_context(nc.Block())

        @block.sync
        def _(sp):
            def expert_chunk(e, q, slot):
                s = chunk_in[slot]
                dst = ring[slot]
                if q < 2:
                    w = (a["w_exp_gate"], a["w_exp_up"])[q][0]
                    src = w[bass.ds(e, 1)].rearrange("e (k p) n -> p (e k) n", p=P)
                    sp.dma_start(dst[:, :].rearrange("p (k n) -> p k n", k=KT), src).then_inc(s, 16)
                else:
                    src = a["w_exp_down"][0][bass.ds(e, 1)].rearrange("e (k p) n -> p (e k) n", p=P)
                    sp.dma_start(dst[:, :].rearrange("p (k n) -> p k n", k=FT), src).then_inc(s, 16)

            sp.dma_start(rows[0:8, :], a["c_prompt"].rearrange("a (k p) -> (a k) p", p=P)).then_inc(S["rows_in"], 16)
            sp.dma_start(rows[8:16, :], a["c_sample"].rearrange("a (k p) -> (a k) p", p=P)).then_inc(S["rows_in"], 16)
            sp.dma_start(rows[16:64, :], a["b_cond"].rearrange("a (k p) -> (a k) p", p=P)).then_inc(S["rows_in"], 16)
            sp.dma_start(rows[64:72, :], a["gla_norm_g"].rearrange("a h (j p) -> (a h j) p", p=P)).then_inc(S["rows_in"], 16)

            for i, (name, c0) in enumerate(DENSE):
                if i >= DENSE_RING:
                    sp.wait_ge(*consumed(i - DENSE_RING))
                src = SRC[name].rearrange("(k p) n -> p k n", p=P)[:, :, c0:c0 + CB]
                sp.dma_start(ring[i % DENSE_RING][:, :].rearrange("p (k n) -> p k n", k=KT), src)\
                  .then_inc(chunk_in[i % DENSE_RING], 16)
            sp.wait_ge(*consumed(DENSE.index(("bb", CB))))
            expert_chunk(1, 1, 7)
            expert_chunk(1, 2, 8)
            for q in range(3):
                sp.wait_ge(*consumed(max(range(q, ND, DENSE_RING))))
                expert_chunk(0, q, q)
            sp.wait_ge(S["stored"], 32)
            sp.wait_ge(*consumed(ND - 1))
            expert_chunk(1, 0, 6)
            sp.wait_ge(S["gm_t"], 6)
            expert_chunk(2, 1, 4)
            expert_chunk(2, 2, 5)
            sp.wait_ge(S["hb_t"], 6)
            expert_chunk(2, 0, 3)
            with sp.Fori(0, E // 3 - 1) as it:
                for r in range(3):
                    for q in range(3):
                        sp.wait_ge(S[USED[q]], it * 3 + (r + 1))
                        expert_chunk(it * 3 + (3 + r), q, base(r) + q)
            for e in (30, 31):
                for q in range(3):
                    sp.wait_ge(S[USED[q]], e - 2)
                    expert_chunk(e, q, base(e) + q)
            sp.wait_ge(S["plan_ready"], 1)
            n_over = sp.value_load(plan_i[0:1, 2 * EXTRA:2 * EXTRA + 1], min_val=0, max_val=EXTRA)
            with sp.If(n_over > 0):
                with sp.Fori(0, n_over) as i:
                    e = sp.value_load(plan_i[0:1, bass.ds(i, 1)], min_val=0, max_val=E - 1)
                    for q in range(3):
                        sp.wait_ge(S[USED[q]], i + E)
                        expert_chunk(e, q, q)
                sp.nop()
            with sp.Else():
                sp.nop()

        @block.gpsimd
        def _(pool):
            ch = Chain(pool, S["pool_chain"])

            def select(t, pattern, base, cm, fill, op=ALU.is_ge):
                ch.done()
                ch.add(pool.affine_select(out=t, in_=t, compare_op=op, fill=fill, base=base, pattern=pattern,
                                          channel_multiplier=cm))

            ch.add(pool.memset(ident[:, :], 0.0))
            ch.add(pool.memset(eps_col[:, :], EPS))
            ch.add(pool.memset(lraT, 1.0))
            ch.add(pool.memset(mv[:, :, :], 1.0))
            ch.add(pool.memset(silu_c[:, :, :], 0.0))
            select(ident[:, :], [[-1, P]], 0, 1, 1.0, ALU.not_equal)
            ch.done()
            pool.nop().then_inc(S["const_ready"], 1)
            for t, v in ((ones[:, :], 1.0), (neg_ones[:, :], -1.0),
                         (neg_tri[:, :], -1.0), (tri_strict[:, :], 1.0), (tri_tau[:, :], 1.0 / TAU),
                         (ident_b[:, :], 0.0), (mask_sb[:, :], 0.0), (valid[:, :], 1.0),
                         (levels[:, :, :], 1.0), (kb[:, :, T:T + 64], 0.0)):
                ch.add(pool.memset(t, v))
            select(ident_b[:, :], [[-1, P]], 0, 1, 1.0, ALU.not_equal)
            select(neg_tri[:, :], [[-1, P]], 0, 1, 0.0)
            select(tri_strict[:, :], [[1, P]], -1, -1, 0.0)
            select(tri_tau[:, 0:P], [[1, P]], 0, -1, 0.0)
            for c in (0, 256):
                select(mask_sb[:, c:c + P], [[1, P]], -1, -1, NEG)
            select(mask_sb[:, 448:512], [[1, 64]], -1, -1, NEG)
            select(valid[:, 2:3], [[0, 1]], 63, -1, 0.0)
            select(levels[:, 0, :], [[-1, P]], 0, 1, 0.0, ALU.is_equal)
            for n in range(1, LEVELS):
                size = 2 ** n
                view = levels[:, n, :].rearrange("p (b c) -> p b c", c=size)
                right = view[:, :, size // 2:size]
                blocks = P // size
                select(right, [[-size, blocks], [0, size // 2]], 0, 1, 0.0)
                select(right, [[size, blocks], [0, size // 2]], size // 2 - 1, -1, 0.0)
                ch.add(pool.memset(view[:, :, 0:size // 2], 0.0))

            def iota(dst, width, pattern, base, cm):
                ch.done()
                ch.add(pool.iota(iota_i[:, 0:width], pattern=pattern, base=base, channel_multiplier=cm))
                ch.done()
                ch.add(pool.tensor_copy(dst, iota_i[:, 0:width]))

            iota(slot_iota[:, :], SLOTS, [[1, SLOTS]], 0, 0)
            for t in range(3):
                iota(e_iota[:, t, :], E, [[1, E]], 0, 0)
                iota(g_iota[:, t, :], NG, [[1, NG]], 0, 0)
            iota(tokval[:, :], 3, [[2 * P, 3]], -SKIP, 2)
            ch.done()
            ch.add(pool.memset(half_base[0:SLOTS, :], 2.0 * SKIP))
            ch.done()
            ch.add(pool.memset(half_base[SLOTS:P, :], 2.0 * SKIP + 1.0))
            iota(x_iota[:, :], EXTRA, [[1, EXTRA]], 0, 0)
            for j in range(ROUNDS):
                ch.done()
                lo, hi = E * j, E * j + E
                ch.add(pool.memset(q_iota[lo:hi, 1:2], float(SLOTS * (j + 1))))
                ch.done()
                ch.add(pool.iota(iota_i[lo:hi, 0:1], pattern=[[0, 1]], base=0, channel_multiplier=1))
                ch.done()
                ch.add(pool.tensor_copy(q_iota[lo:hi, 0:1], iota_i[lo:hi, 0:1]))
            ch.done()
            pool.nop().then_inc(S["const_ready"], 1)

            for n in range(1, LEVELS):
                pool.wait_ge(S["lev_taken"], n + 1)
                if n < LEVELS - 1:
                    pool.tensor_tensor(acc[0:64, 2, :, 0:64], acc[0:64, 2, :, 0:64],
                                       mtmp_s[:, :, :], ALU.add)
                for t in range(2):
                    last = pool.tensor_tensor(acc[:, t, :, :], acc[:, t, :, :],
                                              mtmp[:, t, :].rearrange("p (h t) -> p h t", h=GH), ALU.add)
                last.then_inc(S["lev_added"], 1)

            pool.wait_ge(S["o_ready"], KT)
            pool.wait_ge(S["kb_t"], 6)
            pool.wait_ge(S["gla_stored"], 16 * 6)
            pool.dma_start(x1[:, 0:2, :], a["x_prompt"][0].rearrange("(t p) d -> p t d", p=P)).then_inc(S["x1_in"], 16)
            pool.dma_start(x1[0:64, 2, :], a["x_sample"][0]).then_inc(S["x1_in"], 16)
            pool.dma_start(w_route[:, :, 0:NG], a["w_group"][0].rearrange("(k p) n -> p k n", p=P)).then_inc(S["x1_in"], 16)
            pool.dma_start(w_route[:, :, NG:NG + E], a["w_router"][0].rearrange("(k p) n -> p k n", p=P)).then_inc(S["x1_in"], 16)
            pool.dma_start(b_route[0:NG, :], a["b_group"].rearrange("a n -> n a")).then_inc(S["x1_in"], 16)
            pool.dma_start(b_route[NG:NG + E, :], a["b_router"].rearrange("a n -> n a")).then_inc(S["x1_in"], 16)
            for j in range(KT):
                pool.wait_ge(S["taken_dve"], KT + j + 1)
                pool.tensor_tensor(merged[:, j, :], merged[:, j, :], gtb[:, j, :], ALU.add).then_inc(S["merged_ready"], 1)
            pool.dma_start(ln1[:, 0, :], a["ln1_g"][0].partition_broadcast(P)).then_inc(S["vecs_in"], 16)
            pool.dma_start(ln1[:, 1, :], a["ln1_b"][0].partition_broadcast(P)).then_inc(S["vecs_in"], 16)

            def scatter(n, r, b):
                pool.wait_ge(S["ys_ready"], n + 1)
                if not isinstance(n, int):
                    pool.sem_inc(S["pool_passed"], 1)
                pool.indirect_dma_start(out=ybuf[:, :], out_offset=bass.IndirectOffsetOnAxis(ap=sidx[r][:, 0:1], axis=0),
                                        in_=ystage[b][:, :], in_offset=None, bounds_check=4 * T - 1,
                                        oob_is_err=False).then_inc(S[f"scattered{b}"], 16)

            scatter(0, 0, 0)
            with pool.Fori(0, (E - 2) // 6) as it:
                for r in range(1, 7):
                    scatter(it * 6 + r, r % 3, r % 2)
            pool.wait_ge(S["down_ps"], E - 2)
            pool.dma_start(ln2[:, 0, :], a["ln2_g"][0].partition_broadcast(P)).then_inc(S["vecs_in"], 16)
            pool.dma_start(ln2[:, 1, :], a["ln2_b"][0].partition_broadcast(P)).then_inc(S["vecs_in"], 16)
            scatter(E - 1, (E - 1) % 3, (E - 1) % 2)
            pool.wait_ge(S["plan_ready"], 1)
            n_over = pool.value_load(plan_i[0:1, 2 * EXTRA:2 * EXTRA + 1], min_val=0, max_val=EXTRA)
            with pool.If(n_over > 0):
                with pool.Fori(0, n_over) as i:
                    scatter(i + E, 0, 0)
                pool.wait_ge(S["scattered1"], 8 * E)
                pool.wait_ge(S["scattered0"], n_over * 16 + 8 * E)
                pool.nop()
            with pool.Else():
                pool.wait_ge(S["scattered1"], 8 * E)
                pool.wait_ge(S["scattered0"], 8 * E)
                pool.nop()
            for t in range(3):
                n = TR[t]
                pool.dma_start(comb[t][0:n, :], ybuf[4 * P * t:4 * P * t + 4 * n, :].rearrange("(p k) d -> p (k d)", k=4))\
                    .then_inc(S[f"comb_in{t}"], 16)

        @block.scalar
        def _(act):
            ch = Chain(act, S["act_chain"])
            X = nc.scalar

            act.dma_start(xt[:, 0:2, :], a["x_prompt"][0].rearrange("(t p) d -> p t d", p=P)).then_inc(S["x_in"], 16)
            act.dma_start(xt[0:64, 2, :], a["x_sample"][0]).then_inc(S["x_in"], 16)
            act.wait_ge(S["const_ready"], 1)
            act.dma_start(w_lra[:, :, :], a["w_in"][0].rearrange("(k p) n -> p k n", p=P)[:, :, 3072:3088]).then_inc(S["lra_in"], 16)
            act.dma_start(wa2[0:RANK, :], a["w_gla_a2"][0]).then_inc(S["lra_in"], 16)
            act.dma_start(wa2[RANK:RANK + 1, :], a["b_gla_a"]).then_inc(S["lra_in"], 16)
            act.wait_ge(S["cols_t"], 1)
            X.activation(silu_c[:, :, 0:2], bank[7][:, 0:16].rearrange("p (g k) -> p k g", g=2), ACT.Silu).then_inc(S["silu_ready"], 1)

            g = [0]

            def take(name, i):
                n = g[0]
                assert GROUPS[n][:2] == (name, i)
                src = bank[n % PROJ_BANKS]
                act.wait_ge(S["proj_ready"], n + 1)
                if name == "cr":
                    ins = X.activation(crow[:, :], src[:, 0:P], ACT.Copy)
                elif name == "ct":
                    ins = X.activation(mod[:, 4 * i:4 * i + 4, :], src[:, 0:P].rearrange("p (m c) -> p m c", c=32)[:, :, 0:2],
                                       ACT.Copy)
                elif name == "lra":
                    ins = X.activation(lraT[0:RANK, :], src[0:RANK, 0:T], ACT.Copy)
                elif name == "qa":
                    ins = X.activation(qa[:, i, :], src[:, 0:T], ACT.Copy, scale=DK ** -0.5)
                elif name == "qb":
                    ins = X.activation(qb[:, i, :], src[:, 0:T], ACT.Copy, scale=SD ** -0.5)
                elif name == "ka":
                    ins = X.activation(ka[:, i, :], src[:, 0:T], ACT.Copy)
                elif name == "kb":
                    ins = X.activation(kb[:, i, 0:T], src[:, 0:T], ACT.Copy)
                elif name in ("va", "vb"):
                    dst = va if name == "va" else vb
                    c, t = divmod(i, 3)
                    ins = X.activation(dst[0:TR[t], t, c * CB:c * CB + CB], src[0:TR[t], :], ACT.Copy)
                else:
                    dst = {"ga": ga, "gta": gta, "gtb": gtb}[name]
                    ins = X.activation(dst[:, i, :], src[:, 0:T], ACT.Copy)
                ins.then_inc(S["taken_act"], 1)
                g[0] += 1

            def take_cond(first, n):
                for c in range(first, first + n):
                    take("cr", c)
                    take("ct", c)

            def conds():
                while GROUPS[g[0]][0] in ("cr", "ct"):
                    take(*GROUPS[g[0]][:2])

            def deviation(i0, n):
                X.activation(rstd[:, i0:i0 + n], mv[:, i0:i0 + n, 1], ACT.Sqrt, bias=eps_col[:, 0:1])\
                    .then_inc(S["rstd_ready"], 1)

            act.wait_ge(S["nrm_sum"], 1)
            deviation(0, 3)
            act.dma_start(s0[:, :, :], a["state_gla"][0, 0].rearrange("h k v -> k h v")).then_inc(S["misc_in"], 16)
            act.dma_start(cv[:, :], a["cache_sb_v"][0, 0].rearrange("s h d -> s (h d)")).then_inc(S["misc_in"], 16)
            act.dma_start(ck[0][:, :], a["cache_sb_k"][0, 0].rearrange("s h d -> s (h d)")[:, 0:512]).then_inc(S["misc_in"], 16)
            act.dma_start(ck[1][:, :], a["cache_sb_k"][0, 0].rearrange("s h d -> s (h d)")[:, 512:D]).then_inc(S["misc_in"], 16)
            take_cond(0, 4)
            act.wait_ge(S["mod_ready"], 1)
            for k in range(1, KT, 2):
                act.wait_ge(S["xn_t"], k + 1)
                for g_, c in ((0, slice(0, SEQ)), (1, slice(SEQ, T))):
                    last = X.activation(hT[:, k, c], bank[3 + k % 2][:, c], ACT.Identity, bias=mod[:, k, g_:g_ + 1],
                                        scale=mod[:, KT + k, g_:g_ + 1])
                last.then_inc(S["h_act"], 1)

            def log_gate(t):
                n = TR[t]
                act.wait_ge(S["xla_ps"], t + 1)
                ch.add(X.activation(la[0:n, t, :], bank[3 + t][0:n, :], ACT.Abs))
                ch.done()
                ch.add(X.activation(la[0:n, t, :], la[0:n, t, :], ACT.Exp, scale=-1.0))
                ch.done()
                X.activation(la[0:n, t, :], la[0:n, t, :], ACT.Ln, bias=1.0).then_inc(S["exp_ready"], 1)

            take("lra", 0)
            for i in range(4):
                take("qa", i)
            for t in range(3):
                log_gate(t)
            for i in range(4):
                take("ka", i)
            for i in range(6):
                take("va", i)

            def level_exp(n):
                act.wait_ge(S["dec_ready"], n)
                c = T if n < 7 else SEQ
                X.activation(pd[n % 2][:, :, 0:c], pd[n % 2][:, :, 0:c], ACT.Exp).then_inc(S["exp_ready"], 1)

            second = [("qb", i) for i in range(8)] + [("kb", i) for i in range(8)] + [("vb", i) for i in range(6)]
            for i, (name, j) in enumerate(second):
                take(name, j)
                conds()
                if i % 2 == 1 and i // 2 < LEVELS:
                    level_exp(i // 2 + 1)
                if i == 19:
                    act.wait_ge(S["lev_ps"], LEVELS + 1)
                    for h in range(GH):
                        X.activation(pd[0][:, h, 0:SEQ], bt[:, h, 0:SEQ], ACT.Exp, scale=-1.0, bias=bt[:, h, SEQ - 1:SEQ])
                        X.activation(pd[0][:, h, SEQ:T], bt[:, h, SEQ:T], ACT.Exp, scale=-1.0, bias=bt[:, h, T - 1:T])
                        last = X.activation(pd[1][:, h, 0:DSEQ], bt[:, h, SEQ:T], ACT.Exp)
                    last.then_inc(S["kd_ready"], 1)
            act.wait_ge(S["taken_act"], taken_count(group_index("vb", 5), "act"))
            act.dma_start(out["sb_v_prompt"][0, 0].rearrange("(t p) h d -> p t (h d)", p=P), vb[:, 0:2, :]).then_inc(S["gla_stored"], 16)
            act.dma_start(out["sb_v_sample"][0, 0].rearrange("s h d -> s (h d)"), vb[0:64, 2, :]).then_inc(S["gla_stored"], 16)
            for p in range(2):
                act.wait_ge(S["st_ready"], p + 1)
                act.dma_start(out["gla_state_prompt"][0, 0].rearrange("h k v -> k h v")[:, 2 * p:2 * p + 2, :],
                              sp_[p][:, :].rearrange("p (h v) -> p h v", h=2)).then_inc(S["gla_stored"], 16)
            for p in range(2):
                act.wait_ge(S["st_ready"], p + 3)
                act.dma_start(out["gla_state_sample"][0, 0].rearrange("h k v -> k h v")[:, 2 * p:2 * p + 2, :],
                              ab[p][:, :].rearrange("p (h v) -> p h v", h=2)).then_inc(S["gla_stored"], 16)
            act.wait_ge(S["nrm_sum"], 2)
            deviation(0, 12)

            def soft(h):
                b = ab[h % 2]
                act.wait_ge(S["z_ready"], h + 1)
                if h >= 2:
                    act.wait_ge(S["sp_ready"], h - 1)
                ch.add(X.activation(b[:, :], bank[5 + h % 3][:, :], ACT.Abs))
                ch.done()
                ch.add(X.activation(b[:, :], b[:, :], ACT.Exp, scale=-1.0))
                ch.done()
                X.activation(b[:, :], b[:, :], ACT.Ln, bias=1.0).then_inc(S["l_ready"], 1)

            def weights(h):
                act.wait_ge(S["rest_ready"], h + 1)
                X.activation(wgt[h % 2][:, :], bank[5 + h % 3][:, :], ACT.Exp).then_inc(S["w_ready"], 1)

            gates = [(n, i) for n in ("ga", "gta", "gtb") for i in range(8)]
            done = 0
            act.wait_ge(S["go_ps"], 6)
            act.wait_ge(S["gla_stored"], 16 * 6)
            for i in range(SH + 1):
                if i < SH:
                    soft(i)
                if i >= 1:
                    weights(i - 1)
                while done < min(len(gates), (i + 1) * 3 // 2):
                    take(*gates[done])
                    conds()
                    done += 1
            act.wait_ge(S["taken_act"], g[0])
            for src in (gta, gtb):
                ch.add(X.activation(src[:, :, :], src[:, :, :], ACT.Sigmoid))
            X.activation(ga[:, :, :], ga[:, :, :], ACT.Silu).then_inc(S["sig_ready"], 1)
            act.wait_ge(S["kb_tok"], 6)
            act.dma_start(out["sb_k_prompt"][0, 0].rearrange("(t p) h d -> p t (h d)", p=P), kbtok[:, 0:2, :]).then_inc(S["stored"], 16)
            act.dma_start(out["sb_k_sample"][0, 0].rearrange("s h d -> s (h d)"), kbtok[0:64, 2, :]).then_inc(S["stored"], 16)
            for n, i in enumerate(NORM_ORDER):
                act.wait_ge(S["nrm_sum"], 3 + n)
                deviation(i, 1)
            for k in range(1, KT, 2):
                act.wait_ge(S["norm_t"], k + 1)
                for g_, c in ((0, slice(0, SEQ)), (1, slice(SEQ, T))):
                    last = X.activation(h2T[:, k, c], bank[3 + k % 2][:, c], ACT.Identity, bias=mod[:, 24 + k, g_:g_ + 1],
                                        scale=mod[:, 32 + k, g_:g_ + 1])
                last.then_inc(S["h2_act"], 1)
            for n in range(6):
                t, c = divmod(n, 2)
                act.wait_ge(S["hb_t"], n + 1)
                X.activation(hf[0:TR[t], t, c * 512:c * 512 + 512], bank[5 + n % 3][0:TR[t], :], ACT.Copy)\
                    .then_inc(S["hb_ready"], 1)
            act.wait_ge(S["ex_in"], 1)
            X.activation(r4[1][:, :, :], r4[0][:, :, :], ACT.Exp).then_inc(S["ex_out"], 1)
            act.wait_ge(S["ex_in"], 2)
            X.activation(r1[:, 5, :], r1[:, 4, :], ACT.Exp).then_inc(S["ex_out"], 1)

            def rows_of(n):
                act.wait_ge(S["gather_ps"], n + 1)
                X.activation(xrow[:, :], bank[0][:, :], ACT.Copy).then_inc(S["xrow_ready"], 1)

            def silu(n):
                act.wait_ge(S["gu_ps"], n + 1)
                X.activation(gs[SLOTS:P, :], bank[1][0:SLOTS, :], ACT.Silu).then_inc(S["gs_ready"], 1)

            def rows_out(n, b, before):
                act.wait_ge(S["down_ps"], n + 1)
                if before is not None:
                    act.wait_ge(S[f"scattered{b}"], before * 16)
                X.activation(ystage[b][:, :], bank[3][:, :], ACT.Copy).then_inc(S["ys_ready"], 1)

            def step(n, b, before):
                silu(n)
                rows_of(n + 1)
                rows_out(n, b, before)

            rows_of(0)
            step(0, 0, None)
            step(1, 1, None)
            with act.Fori(0, (E - 4) // 2) as it:
                for r in range(2, 4):
                    step(it * 2 + r, r % 2, it + 1)
            step(E - 2, 0, E // 2 - 1)
            silu(E - 1)
            rows_out(E - 1, (E - 1) % 2, (E - 1) // 2)
            act.wait_ge(S["plan_ready"], 1)
            n_over = act.value_load(plan_i[0:1, 2 * EXTRA:2 * EXTRA + 1], min_val=0, max_val=EXTRA)
            with act.If(n_over > 0):
                with act.Fori(0, n_over) as i:
                    rows_of(i + E)
                    silu(i + E)
                    rows_out(i + E, 0, i + E // 2)
                act.nop()
            with act.Else():
                act.nop()
            for t in range(3):
                act.wait_ge(S["nrm_sum"], 9 + t)
                deviation(t, 1)
            for t in range(3):
                act.wait_ge(S["fin_ready"], t + 1)
                dst = out["y_prompt"][0][t * P:t * P + P, :] if t < 2 else out["y_sample"][0]
                act.dma_start(dst, x1[0:TR[t], t, :]).then_inc(S["stored"], 16)
            act.wait_ge(S["stored"], 16 * 5)

        @block.tensor
        def _(pe):
            mm = nc.tensor.matmul
            cur = [0]

            def chunk():
                i = cur[0]
                pe.wait_ge(chunk_in[i % DENSE_RING], dense_use(i))
                cur[0] += 1
                return ring[i % DENSE_RING][:, :].rearrange("p (k n) -> p k n", k=KT)

            pe.wait_ge(S["const_ready"], 1)
            pe.wait_ge(S["rows_in"], 64)
            nc.tensor.transpose(bank[7][:, 0:72], rows[0:72, :], ident[0:72, 0:72]).then_inc(S["cols_t"], 1)

            g = [0]

            def free_bank():
                n = g[0]
                if n >= PROJ_BANKS:
                    who = GROUPS[n - PROJ_BANKS][2]
                    pe.wait_ge(S["taken_act" if who == "act" else "taken_dve"], taken_count(n - PROJ_BANKS, who))
                return bank[n % PROJ_BANKS]

            def close(ins):
                g[0] += 1
                ins.then_inc(S["proj_ready"], 1)

            def cond_rows():
                w = chunk()
                b = free_bank()
                for k in range(KT):
                    for m in range(4):
                        last = mm(b[32 * m:32 * m + 32, 0:P], silu_c[:, k, :], w[:, k, m * P:m * P + P], start=(k == 0),
                                  stop=(k == KT - 1), skip_group_check=True)
                close(last)

            def cond_turn():
                n = max(i for i in range(g[0]) if GROUPS[i][0] == "cr")
                pe.wait_ge(S["taken_act"], taken_count(n, "act"))
                b = free_bank()
                close(nc.tensor.transpose(b[:, 0:P], crow[:, :], ident[:, :]))

            def conds():
                while GROUPS[g[0]][0] in ("cr", "ct"):
                    (cond_rows if GROUPS[g[0]][0] == "cr" else cond_turn)()

            pe.wait_ge(S["silu_ready"], 1)
            for c in range(4):
                cond_rows()
                cond_turn()
            pe.wait_ge(S["xn_ready"], 3)
            for k in range(KT):
                b = bank[3 + k % 2]
                if k >= 2:
                    pe.wait_ge(S["h_act" if k % 2 else "h_dve"], k // 2)
                for t in range(3):
                    n = TR[t]
                    last = nc.tensor.transpose(b[:, TC[t]], xn[0:n, t, k * P:k * P + P], ident[0:n, 0:n])
                last.then_inc(S["xn_t"], 1)

            state = {}

            def feat(i, rhs):
                if i % 4 == 0:
                    state["w"] = chunk()
                b = free_bank()
                for k in range(KT):
                    last = mm(b[:, 0:T], state["w"][:, k, (i % 4) * P:(i % 4 + 1) * P], rhs[:, k, :],
                              start=(k == 0), stop=(k == KT - 1))
                close(last)

            def tok(i, lhs):
                if i % 3 == 0:
                    state["w"] = chunk()
                b = free_bank()
                t = i % 3
                for k in range(KT):
                    last = mm(b[0:TR[t], :], lhs[:, k, TC[t]], state["w"][:, k, :], start=(k == 0), stop=(k == KT - 1))
                close(last)

            pe.wait_ge(S["h_dve"], KT // 2)
            pe.wait_ge(S["h_act"], KT // 2)
            pe.wait_ge(S["lra_in"], 48)
            b = free_bank()
            for k in range(KT):
                last = mm(b[0:RANK, 0:T], w_lra[:, k, :], hT[:, k, :], start=(k == 0), stop=(k == KT - 1))
            close(last)
            for i in range(4):
                feat(i, hT)
            pe.wait_ge(S["taken_act"], taken_count(group_index("lra", 0), "act"))
            pe.wait_ge(S["const_ready"], 2)
            for t in range(3):
                mm(bank[3 + t][0:TR[t], :], lraT[0:RANK + 1, TC[t]], wa2[0:RANK + 1, :], start=True, stop=True)\
                    .then_inc(S["xla_ps"], 1)
            for i in range(4):
                feat(i, hT)
            for i in range(3):
                tok(i, hT)
            pe.wait_ge(S["la_ready"], 3)
            for h in range(GH):
                b = bank[3 + h]
                hs = slice(h * DK, h * DK + DK)
                mm(b[:, 0:SEQ], la[:, 0, hs], tri_tau[:, :], start=True, stop=False, skip_group_check=True)
                mm(b[:, 128:SEQ], la[:, 1, hs], tri_tau[:, 0:P], start=False, stop=True, skip_group_check=True)
                mm(b[:, SEQ:T], la[0:64, 2, hs], tri_tau[0:64, 0:64], start=False, stop=True, skip_group_check=True)\
                    .then_inc(S["b_ps"], 1)
            for i in range(3, 6):
                tok(i, hT)

            def level(n):
                lhs, rhs = (ka, qa) if n == 0 else (pd[n % 2], pd[n % 2])
                if n:
                    pe.wait_ge(S["pd_ready"], n)
                else:
                    pe.wait_ge(S["b_ready"], 1)
                if n == LEVELS:
                    for h in range(GH):
                        last = mm(bank[6][:, h * P:h * P + P], lhs[:, h, TC[0]], rhs[:, h, TC[1]], start=True, stop=True)
                    last.then_inc(S["lev_ps"], 1)
                    return
                if n:
                    pe.wait_ge(S["lev_taken"], n)
                for h in range(GH):
                    for t in range(2):
                        last = mm(bank[3 + t][:, h * P:h * P + P], lhs[:, h, TC[t]], rhs[:, h, TC[t]], start=True, stop=True)
                    if n < 7:
                        last = mm(bank[5][0:64, h * 64:h * 64 + 64], lhs[:, h, SEQ:T], rhs[:, h, SEQ:T], start=True, stop=True)
                last.then_inc(S["lev_ps"], 1)

            def second(i):
                if i < 16:
                    feat(i % 8, hT)
                else:
                    tok(i - 16, hT)
                conds()

            for i in range(22):
                second(i)
                if i % 2 == 1 and i // 2 <= LEVELS:
                    level(i // 2)
            pe.wait_ge(S["ke_ready"], 1)
            pe.wait_ge(S["lev_taken"], LEVELS + 1)
            for t in range(3):
                n = TR[t]
                for h in range(GH):
                    last = nc.tensor.transpose(bank[3 + t][0:n, h * P:h * P + P], ke[:, h, TC[t]], ident[:, :])
                last.then_inc(S["ke_t"], 1)
            pe.wait_ge(S["misc_in"], 64)
            for j in range(KT):
                last = nc.tensor.transpose(bank[6 + j // 4][:, (j % 4) * P:(j % 4 + 1) * P],
                                           ck[j // 4][:, (j % 4) * P:(j % 4 + 1) * P], ident[:, :])
            last.then_inc(S["ck_t"], 1)
            pe.wait_ge(S["ket_ready"], 3)
            pe.wait_ge(S["ck_ready"], 2)
            for p in range(2):
                b = bank[6 + p]
                for h in (2 * p, 2 * p + 1):
                    c = slice((h % 2) * DV, (h % 2 + 1) * DV)
                    hv = slice(h * DV, h * DV + DV)
                    for t in range(2):
                        last = mm(b[:, c], ket[:, t, h * DK:h * DK + DK], va[:, t, hv], start=(t == 0), stop=(t == 1))
                last.then_inc(S["st_ps"], 1)
            for p in range(2):
                b = bank[3 + p]
                for h in (2 * p, 2 * p + 1):
                    c = slice((h % 2) * DV, (h % 2 + 1) * DV)
                    last = mm(b[:, c], ket[0:64, 2, h * DK:h * DK + DK], va[0:64, 2, h * DV:h * DV + DV], start=True, stop=True)
                last.then_inc(S["st_ps"], 1)
            pe.wait_ge(S["lev_added"], LEVELS - 1)
            pe.wait_ge(S["qe_ready"], 1)
            for n in range(6):
                t, p = divmod(n, 2)
                b = bank[5 + n % 3]
                if n == 1:
                    pe.wait_ge(S["st_ready"], 1)
                elif n == 2:
                    pe.wait_ge(S["st_ready"], 2)
                elif n >= 3:
                    pe.wait_ge(S["go_ready"], n - 2)
                for h in (2 * p, 2 * p + 1):
                    c = slice((h % 2) * DV, (h % 2 + 1) * DV)
                    hv = slice(h * DV, h * DV + DV)
                    if t == 0:
                        last = mm(b[:, c], acc[:, 0, h, :], va[:, 0, hv], start=True, stop=True)
                    elif t == 1:
                        mm(b[:, c], cross[:, h, :], va[:, 0, hv], start=True, stop=False)
                        last = mm(b[:, c], acc[:, 1, h, :], va[:, 1, hv], start=False, stop=True)
                    else:
                        mm(b[0:64, c], acc[0:64, 2, h, 0:64], va[0:64, 2, hv], start=True, stop=False)
                        last = mm(b[0:64, c], pd[1][:, h, 0:DSEQ], s0[:, h, :], start=False, stop=True)
                last.then_inc(S["go_ps"], 1)

            def scores(h):
                z, j, r = bank[5 + h % 3], h // 2, slice(64 * (h % 2), 64 * (h % 2) + 64)
                if h < 3:
                    pe.wait_ge(S["go_ready"], 6)
                else:
                    pe.wait_ge(S["w_ready"], h - 2)
                mm(z[:, :], ident_b[:, :], mask_sb[:, :], start=True, stop=False, skip_group_check=True)
                mm(z[:, 0:256], kb[r, j, 0:128], qb[r, j, 0:256], start=False, stop=False, skip_group_check=True)
                mm(z[:, 256:384], kb[r, j, 128:256], qb[r, j, 128:256], start=False, stop=False, skip_group_check=True)
                mm(z[:, 384:448], ckT[r, j, :], qb[r, j, SEQ:T], start=False, stop=False, skip_group_check=True)
                mm(z[:, 448:512], kb[r, j, SEQ:T + 64], qb[r, j, SEQ:T], start=False, stop=True, skip_group_check=True)\
                    .then_inc(S["z_ready"], 1)

            def rest(h):
                z, s = bank[5 + h % 3], sp_[h % 2]
                pe.wait_ge(S["sp_ready"], h + 1)
                mm(z[:, :], neg_tri[:, :], s[:, :], start=False, stop=False, skip_group_check=True)
                mm(z[:, 128:256], neg_ones[:, :], s[:, 256:384], start=False, stop=False, skip_group_check=True)
                mm(z[:, 384:448], neg_ones[:, :], s[:, 448:512], start=False, stop=True, skip_group_check=True)\
                    .then_inc(S["rest_ready"], 1)

            def attend(h):
                j, r, w = h // 2, slice(64 * (h % 2), 64 * (h % 2) + 64), wgt[h % 2]
                b, hd = bank[3 + j % 2], slice(h * SD, h * SD + SD)
                pe.wait_ge(S["w_ready"], h + 1)
                if h < 4:
                    pe.wait_ge(S["st_ready"], 4)
                elif h % 2 == 0:
                    pe.wait_ge(S["o_taken"], j - 1)
                mm(b[r, 0:256], vb[:, 0, hd], w[:, 0:256], start=True, stop=False, skip_group_check=True)
                mm(b[r, 128:256], vb[:, 1, hd], w[:, 256:384], start=False, stop=True, skip_group_check=True)
                mm(b[r, 256:T], cv[:, hd], w[:, 384:448], start=False, stop=False, skip_group_check=True)
                last = mm(b[r, 256:T], vb[0:64, 2, hd], w[0:64, 448:512], start=False, stop=True, skip_group_check=True)
                if h % 2:
                    last.then_inc(S["o_ready"], 1)

            done = 0
            for i in range(SH + 2):
                if i < SH:
                    scores(i)
                if 1 <= i <= SH:
                    rest(i - 1)
                if i >= 2:
                    attend(i - 2)
                while done < min(24, (i + 1) * 3 // 2):
                    feat(done % 8, hT)
                    conds()
                    done += 1
            for n in range(6):
                t, c = divmod(n, 2)
                b = bank[5 + n % 3]
                if n >= 3:
                    pe.wait_ge(S["kb_tok"], n - 2)
                elif n == 0:
                    pe.wait_ge(S["w_ready"], SH)
                for j in range(4):
                    last = nc.tensor.transpose(b[0:TR[t], j * P:j * P + P], kb[:, 4 * c + j, TC[t]], ident[:, :])
                last.then_inc(S["kb_t"], 1)
            pe.wait_ge(S["kb_tok"], 6)
            pe.wait_ge(S["on_ready"], 1)
            for j in range(KT):
                b = bank[3 + j % 2]
                if j >= 2:
                    pe.wait_ge(S["oa_ready"], j - 1)
                else:
                    pe.wait_ge(S["o_taken"], KT)
                for t in range(3):
                    n = TR[t]
                    last = nc.tensor.transpose(b[:, TC[t]], on[0:n, t, j * P:j * P + P], ident[0:n, 0:n])
                last.then_inc(S["on_t"], 1)
            pe.wait_ge(S["oa_ready"], KT)
            for i in range(8):
                feat(i, oaT)
                if i % 2 == 0:
                    pe.wait_ge(S["gfr_in"], i // 2 + 1)
                    if i:
                        pe.wait_ge(S["gf_ready"], i // 2)
                    mm(bank[5][:, :], ones[:, :], diag[:, :], start=True, stop=True).then_inc(S["gfr_ps"], 1)
            pe.wait_ge(S["gf_ready"], 4)
            for i in range(8):
                feat(i, obT)
            pe.wait_ge(S["merged_ready"], KT)
            for i in range(8):
                feat(i, merged)
            for n in range(6):
                t, c = divmod(n, 2)
                b = bank[5 + n % 3]
                pe.wait_ge(S["taken_dve"], 2 * KT + 4 * c + 4)
                if n >= 3:
                    pe.wait_ge(S["gm_added"], n - 2)
                for j in range(4):
                    last = nc.tensor.transpose(b[0:TR[t], j * P:j * P + P], gmT[:, 4 * c + j, TC[t]], ident[:, :])
                last.then_inc(S["gm_t"], 1)
            def turn_modulated(n):
                t, c = divmod(n, 2)
                b = bank[5 + n % 3]
                if n >= 3:
                    pe.wait_ge(S["hb_ready"], n - 2)
                for j in range(4):
                    last = nc.tensor.transpose(b[0:TR[t], j * P:j * P + P], h2T[:, 4 * c + j, TC[t]], ident[:, :])
                last.then_inc(S["hb_t"], 1)

            def logits(k):
                pe.wait_ge(S["h2_act" if k % 2 else "h2_dve"], k // 2 + 1)
                return mm(bank[0][0:NG + E, 0:T], w_route[:, k, :], h2T[:, k, :], start=(k == 0), stop=(k == KT - 1))

            pe.wait_ge(S["x1_in"], 96)
            pe.wait_ge(S["gm_added"], 6)
            pe.wait_ge(S["norm_ready"], 3)
            for k in range(KT):
                b = bank[3 + k % 2]
                if k >= 2:
                    logits(k - 2)
                for t in range(3):
                    n = TR[t]
                    last = nc.tensor.transpose(b[:, TC[t]], x2n[0:n, t, k * P:k * P + P], ident[0:n, 0:n])
                last.then_inc(S["norm_t"], 1)
            for k in (KT - 2, KT - 1):
                last = logits(k)
            last.then_inc(S["lgt_ps"], 1)
            turn_modulated(0)
            pe.wait_ge(S["lgt_ready"], 1)
            for t in range(3):
                nc.tensor.transpose(bank[1][0:TR[t], 40 * t:40 * t + NG + E], lgT[:, TC[t]], ident[0:NG + E, 0:NG + E])\
                    .then_inc(S["lg_ps"], 1)
            for n in range(1, 6):
                turn_modulated(n)
            pe.wait_ge(S["rank_in"], 1)
            for t in range(3):
                r = bank[1][:, E * t:E * t + E]
                for u in range(t):
                    mm(r, ones_b[:, :], chosen[:, u, :], start=(u == 0), stop=False)
                mm(r, tri_b[:, :], chosen[:, t, :], start=(t == 0), stop=True)
            for t in range(3):
                last = mm(bank[1][:, 128:129], rep[:, t, :, :].rearrange("p j e -> p (j e)"),
                          ones_b[:, 0:1], start=(t == 0), stop=(t == 2))
            last.then_inc(S["rank_ps"], 1)
            pe.wait_ge(S["flag_ready"], 1)
            mm(bank[4][:, 0:1], tri_strict[:, :], flags[:, 0:1], start=True, stop=True).then_inc(S["xr_ps"], 1)

            def gather(n):
                pe.wait_ge(S["onehot_ready"], n + 1)
                for t in range(3):
                    m = TR[t]
                    for c in range(2):
                        mm(bank[0][64 * c:64 * c + 64, :], onehot[0:m, t, :], hf[0:m, t, c * CB:c * CB + CB],
                           start=(t == 0), stop=(t == 2), skip_group_check=True)
                for t in range(3):
                    m = TR[t]
                    for c in range(2):
                        last = mm(bank[5][64 * c:64 * c + 64, 0:1], onehot[0:m, t, :], vcol[0:m, t:t + 1],
                                  start=(t == 0), stop=(t == 2), skip_group_check=True)
                last.then_inc(S["gather_ps"], 1)

            def turn_rows(n):
                pe.wait_ge(S["xrow_ready"], n + 1)
                if not isinstance(n, int):
                    pe.sem_inc(S["pe_passed"], 1)
                for q in range(4):
                    last = nc.tensor.transpose(bank[2][:, q * P:q * P + P], xrow[:, q * P:q * P + P], ident[:, :])
                last.then_inc(S["xg_t"], 1)

            def gate_up(n, s, turn):
                pe.wait_ge(S["xg_ready"], n + 1)
                pe.wait_ge(chunk_in[s], turn(s))
                pe.wait_ge(chunk_in[s + 1], turn(s + 1))
                for k in range(KT):
                    for q in range(2):
                        last = mm(bank[1][64 * q:64 * q + 64, :], xg[:, k % 4, k // 4, :],
                                  ring[s + q][:, k * FF:k * FF + FF], start=(k == 0), stop=(k == KT - 1),
                                  skip_group_check=True)
                last.then_inc(S["gu_ps"], 1)

            def turn_hidden(n):
                pe.wait_ge(S["hrow_ready"], n + 1)
                if not isinstance(n, int):
                    pe.sem_inc(S["pe_passed"], 1)
                for f in range(FT):
                    last = nc.tensor.transpose(bank[6][:, f * SLOTS:(f + 1) * SLOTS], gs[0:SLOTS, f * P:f * P + P],
                                               ident[0:SLOTS, 0:SLOTS])
                last.then_inc(S["he_t"], 1)

            def down(n, s, turn):
                pe.wait_ge(S["he_ready"], n + 1)
                pe.wait_ge(chunk_in[s + 2], turn(s + 2))
                if not isinstance(n, int) or n:
                    pe.wait_ge(S["ys_ready"], n)
                for f in range(FT):
                    for c in range(2):
                        last = mm(bank[3][64 * c:64 * c + 64, :], he[:, f, :],
                                  ring[s + 2][:, f * D + c * CB:f * D + c * CB + CB], start=(f == 0),
                                  stop=(f == FT - 1), skip_group_check=True)
                last.then_inc(S["down_ps"], 1)

            def step(e, s, use):
                gate_up(e, s, use)
                gather(e + 1)
                turn_hidden(e)
                turn_rows(e + 1)
                down(e, s, use)

            pe.wait_ge(S["hb_ready"], 6)
            gather(0)
            pe.wait_ge(S["pick_ready"], 1)
            mm(bank[4][:, 64:64 + EXTRA], q_rep[:, :], pick[:, :], start=True, stop=True)
            mm(bank[4][0:1, 96:96 + EXTRA], q_iota[:, 0:1], pick[:, :], start=True, stop=True)
            mm(bank[4][0:1, 128:129], flags[:, 0:1], ones[:, 0:1], start=True, stop=True).then_inc(S["plan_ps"], 1)
            turn_rows(0)
            step(0, 0, lambda s: expert_use(s, 0))
            with pe.Fori(0, (E - 2) // 3) as it:
                for r in range(1, 4):
                    step(it * 3 + r, base(r), lambda s, r=r: it * 16 + expert_use(s, r // 3))
            last_use = lambda s: expert_use(s, (E - 1) // 3)
            pe.wait_ge(S["plan_ready"], 1)
            gate_up(E - 1, base(E - 1), last_use)
            turn_hidden(E - 1)
            down(E - 1, base(E - 1), last_use)
            n_over = pe.value_load(plan_i[0:1, 2 * EXTRA:2 * EXTRA + 1], min_val=0, max_val=EXTRA)
            with pe.If(n_over > 0):
                with pe.Fori(0, n_over) as i:
                    use = lambda s: i * 16 + expert_use(s, len(range(0, E, 3)))
                    gather(i + E)
                    turn_rows(i + E)
                    gate_up(i + E, 0, use)
                    turn_hidden(i + E)
                    down(i + E, 0, use)
                pe.nop()
            with pe.Else():
                pe.nop()

        @block.vector
        def _(dve):
            V = nc.vector
            ch = Chain(dve, S["dve_chain"])

            def tile_stats(i0, src, n):
                for c in range(2):
                    ch.add(V.bn_stats(stats[0:n, i0, 6 * c:6 * c + 6], src[:, c * 512:c * 512 + 512]))
                ch.done()
                return V.bn_aggr(mv[0:n, i0, :], stats[0:n, i0, :])

            def reciprocal(n, i0, count):
                r, q, var = rstd[:, i0:i0 + count], newton[:, i0:i0 + count], mv[:, i0:i0 + count, 1]
                dve.wait_ge(S["rstd_ready"], n)
                for f in (lambda: V.reciprocal(r, r),
                          lambda: V.tensor_tensor(q, r, r, ALU.mult),
                          lambda: V.scalar_tensor_tensor(out=q, in0=var, scalar=eps_col[:, 0:1], in1=q, op0=ALU.add,
                                                         op1=ALU.mult),
                          lambda: V.tensor_scalar(q, q, -0.5, 1.5, ALU.mult, ALU.add),
                          lambda: V.tensor_tensor(r, r, q, ALU.mult)):
                    ch.add(f())
                    ch.done()

            dve.wait_ge(S["const_ready"], 1)
            dve.wait_ge(S["x_in"], 32)
            for t in range(3):
                last = tile_stats(t, xt[0:TR[t], t, :], TR[t])
            last.then_inc(S["nrm_sum"], 1)
            dve.wait_ge(S["silu_ready"], 1)
            ch.add(V.tensor_copy(cols[:, :], bank[7][:, 0:72]))
            reciprocal(1, 0, 3)
            for t in range(3):
                n = TR[t]
                V.tensor_scalar(xn[0:n, t, :], xt[0:n, t, :], mv[0:n, t, 0:1], rstd[0:n, t:t + 1], ALU.subtract,
                                ALU.mult).then_inc(S["xn_ready"], 1)

            def take_mod(first, n):
                ch.done()
                for g_ in range(2):
                    ch.add(V.tensor_tensor(mod[:, first:first + n, g_], mod[:, first:first + n, g_],
                                           cols[:, 16 + first:16 + first + n], ALU.add))
                ch.done()
                s = 8 if first == 0 else 32
                V.tensor_scalar(mod[:, s:s + 8, :], mod[:, s:s + 8, :], 1.0, None, ALU.add).then_inc(S["mod_ready"], 1)

            dve.wait_ge(S["taken_act"], taken_count(group_index("ct", 3), "act"))
            take_mod(0, 16)
            dve.wait_ge(S["mod_ready"], 1)
            for k in range(0, KT, 2):
                dve.wait_ge(S["xn_t"], k + 1)
                for g_, c in ((0, slice(0, SEQ)), (1, slice(SEQ, T))):
                    last = V.tensor_scalar(hT[:, k, c], bank[3 + k % 2][:, c], mod[:, KT + k, g_:g_ + 1],
                                           mod[:, k, g_:g_ + 1], ALU.mult, ALU.add)
                last.then_inc(S["h_dve"], 1)
            for t in range(3):
                n = TR[t]
                dve.wait_ge(S["exp_ready"], t + 1)
                V.scalar_tensor_tensor(out=la[0:n, t, :], in0=bank[3 + t][0:n, :], scalar=0.0, in1=la[0:n, t, :],
                                       op0=ALU.min, op1=ALU.subtract).then_inc(S["la_ready"], 1)
            dve.wait_ge(S["b_ps"], GH)
            for h in range(GH):
                last = V.tensor_copy(bt[:, h, :], bank[3 + h][:, 0:T])
            last.then_inc(S["b_ready"], 1)

            def halves(t, n):
                size = 2 ** n
                if n < 7:
                    v = t[:, :, :].rearrange("p h t -> p (h t)").rearrange("p (b c) -> p b c", c=size)
                    return v[:, :, 0:size // 2], v[:, :, size // 2:size], v[:, :, size // 2 - 1:size // 2]
                v = t[:, :, 0:SEQ].rearrange("p h (b c) -> p h b c", c=size)
                return v[:, :, :, 0:size // 2], v[:, :, :, size // 2:size], v[:, :, :, size // 2 - 1:size // 2]

            def log_decay(n):
                bl, br, mid = halves(bt, n)
                dl, dr, _ = halves(pd[n % 2], n)
                if n >= 3:
                    dve.wait_ge(S["lev_ps"], n - 1)
                V.tensor_tensor(dl, mid.to_broadcast(list(bl.shape)), bl, ALU.subtract)
                V.tensor_tensor(dr, br, mid.to_broadcast(list(br.shape)), ALU.subtract).then_inc(S["dec_ready"], 1)

            def decayed(n):
                dl, dr, _ = halves(pd[n % 2], n)
                dve.wait_ge(S["exp_ready"], 3 + n)
                V.tensor_tensor(dl, dl, halves(ka, n)[0], ALU.mult)
                V.tensor_tensor(dr, dr, halves(qa, n)[1], ALU.mult).then_inc(S["pd_ready"], 1)

            def masked(n):
                dve.wait_ge(S["lev_ps"], n + 1)
                if n == LEVELS:
                    V.tensor_copy(cross[:, :, :].rearrange("p h t -> p (h t)"), bank[6][:, :]).then_inc(S["lev_taken"], 1)
                    return
                if n >= 2:
                    dve.wait_ge(S["lev_added"], n - 1)
                mask = levels[:, n, :].unsqueeze(1)
                for t in range(2):
                    dst = acc[:, t, :, :] if n == 0 else mtmp[:, t, :].rearrange("p (h t) -> p h t", h=GH)
                    last = V.tensor_tensor(dst, bank[3 + t][:, :].rearrange("p (h t) -> p h t", h=GH),
                                           mask.to_broadcast([P, GH, P]), ALU.mult)
                if n < 7:
                    dst = acc[0:64, 2, :, 0:64] if n == 0 else mtmp_s[:, :, :]
                    last = V.tensor_tensor(dst, bank[5][0:64, 0:256].rearrange("p (h t) -> p h t", h=GH),
                                           levels[0:64, n, 0:64].unsqueeze(1).to_broadcast([64, GH, 64]), ALU.mult)
                last.then_inc(S["lev_taken"], 1)

            dve.wait_ge(S["const_ready"], 2)
            dve.wait_ge(S["b_ready"], 1)
            dve.wait_ge(S["taken_act"], taken_count(group_index("ka", 3), "act"))
            log_decay(1)
            log_decay(2)
            decayed(1)
            masked(0)
            for n in range(2, LEVELS + 1):
                decayed(n)
                masked(n - 1)
                if n < LEVELS:
                    log_decay(n + 1)
            masked(LEVELS)
            dve.wait_ge(S["kd_ready"], 1)
            V.tensor_tensor(ke[:, :, :], ke[:, :, :], ka[:, :, :], ALU.mult).then_inc(S["ke_ready"], 1)
            ch.add(V.tensor_copy(total[:, :], pd[1][:, :, DSEQ - 1]))
            ch.done()
            V.tensor_tensor(pd[1][:, :, 0:DSEQ], pd[1][:, :, 0:DSEQ], qa[:, :, SEQ:T], ALU.mult).then_inc(S["qe_ready"], 1)
            for t in range(3):
                dve.wait_ge(S["ke_t"], t + 1)
                V.tensor_copy(ket[0:TR[t], t, :], bank[3 + t][0:TR[t], :]).then_inc(S["ket_ready"], 1)
            dve.wait_ge(S["ck_t"], 1)
            for c in range(2):
                V.tensor_copy(ckT[:, 4 * c:4 * c + 4, :].rearrange("p k s -> p (k s)"), bank[6 + c][:, :]).then_inc(S["ck_ready"], 1)
            for p in range(2):
                dve.wait_ge(S["st_ps"], p + 1)
                V.tensor_copy(sp_[p][:, :], bank[6 + p][:, :]).then_inc(S["st_ready"], 1)
            for p in range(2):
                dve.wait_ge(S["st_ps"], 3 + p)
                for h in (2 * p, 2 * p + 1):
                    last = V.scalar_tensor_tensor(out=ab[p][:, (h % 2) * DV:(h % 2 + 1) * DV], in0=s0[:, h, :], scalar=total[:, h:h + 1],
                                                  in1=bank[3 + p][:, (h % 2) * DV:(h % 2 + 1) * DV], op0=ALU.mult, op1=ALU.add)
                last.then_inc(S["st_ready"], 1)
            for n in range(6):
                t, p = divmod(n, 2)
                m = TR[t]
                dve.wait_ge(S["go_ps"], n + 1)
                V.tensor_copy(on[0:m, t, p * 512:p * 512 + 512], bank[5 + n % 3][0:m, :])
                for h in range(2):
                    ins = V.bn_stats(stats[0:m, 4 * t + 2 * p + h, 0:6], bank[5 + n % 3][0:m, h * DV:h * DV + DV])
                ins.then_inc(S["go_ready"], 1)
            dve.wait_ge(S["go_ready"], 6)
            ch.done()
            for i in range(12):
                m = TR[i // 4]
                ch.add(V.bn_aggr(mv[0:m, i, :], stats[0:m, i, 0:6]))
            ch.done()
            ch.add(V.tensor_tensor(mv[:, :, 0], mv[:, :, 0], mv[:, :, 0], ALU.mult))
            ch.done()
            V.tensor_tensor(mv[:, :, 1], mv[:, :, 1], mv[:, :, 0], ALU.add).then_inc(S["nrm_sum"], 1)

            def soft_sum(h):
                dve.wait_ge(S["l_ready"], h + 1)
                if h >= 2:
                    dve.wait_ge(S["rest_ready"], h - 1)
                V.scalar_tensor_tensor(out=sp_[h % 2][:, :], in0=bank[5 + h % 3][:, :], scalar=0.0, in1=ab[h % 2][:, :],
                                       op0=ALU.max, op1=ALU.add).then_inc(S["sp_ready"], 1)

            def take_o(j):
                dve.wait_ge(S["o_ready"], j + 1)
                V.tensor_copy(obT[:, j, :], bank[3 + j % 2][:, 0:T]).then_inc(S["o_taken"], 1)

            dve.wait_ge(S["gla_stored"], 16 * 6)
            dve.wait_ge(S["ck_ready"], 2)
            for i in range(SH + 2):
                if i < SH:
                    soft_sum(i)
                if i == 2:
                    reciprocal(2, 0, 12)
                    for n in range(12):
                        t, h = divmod(n, GH)
                        m = TR[t]
                        v = on[0:m, t, h * DV:h * DV + DV]
                        last = V.tensor_scalar(v, v, rstd[0:m, n:n + 1], None, ALU.mult)
                    last.then_inc(S["on_ready"], 1)
                if i >= 3 and i % 2 == 1:
                    take_o((i - 3) // 2)
            for n in range(6):
                t, c = divmod(n, 2)
                dve.wait_ge(S["kb_t"], n + 1)
                V.tensor_copy(kbtok[0:TR[t], t, c * 512:c * 512 + 512], bank[5 + n % 3][0:TR[t], :]).then_inc(S["kb_tok"], 1)
            dve.wait_ge(S["taken_act"], taken_count(group_index("ct", 11), "act"))
            take_mod(16, 32)
            dve.wait_ge(S["sig_ready"], 1)
            for j in range(KT):
                dve.wait_ge(S["on_t"], j + 1)
                V.scalar_tensor_tensor(out=oaT[:, j, :], in0=bank[3 + j % 2][:, 0:T], scalar=cols[:, 64 + j:65 + j],
                                       in1=ga[:, j, :], op0=ALU.mult, op1=ALU.mult).then_inc(S["oa_ready"], 1)
            ch.add(V.tensor_copy(ones_b[:, :], ones[:, :]))
            ch.add(V.tensor_copy(tri_b[:, :], tri_strict[:, :]))
            ch.add(V.memset(lg[:, :, :], 0.0))

            def diagonals(n):
                g_, c = divmod(n, 2)
                V.tensor_tensor(diag[:, :].rearrange("p (j i) -> p j i", j=4), ident[:, :].unsqueeze(1).to_broadcast([P, 4, P]),
                                mod[:, 40 + 4 * c:44 + 4 * c, g_].unsqueeze(2).to_broadcast([P, 4, P]), ALU.mult)\
                    .then_inc(S["gfr_in"], 1)

            diagonals(0)
            g0 = group_index("ba", 0)
            for j in range(KT):
                n = g0 + j
                if j % 2:
                    dve.wait_ge(S["gfr_ps"], j // 2 + 1)
                    c = j // 2
                    V.tensor_copy(gf_rows[:, c // 2, (c % 2) * 512:(c % 2) * 512 + 512], bank[5][:, :]).then_inc(S["gf_ready"], 1)
                    if j < KT - 1:
                        diagonals(c + 1)
                dve.wait_ge(S["proj_ready"], n + 1)
                V.tensor_tensor(merged[:, j, :], bank[n % PROJ_BANKS][:, 0:T], gta[:, j, :], ALU.mult).then_inc(S["taken_dve"], 1)
            for j in range(KT):
                n = g0 + 8 + j
                dve.wait_ge(S["proj_ready"], n + 1)
                V.tensor_tensor(gtb[:, j, :], bank[n % PROJ_BANKS][:, 0:T], gtb[:, j, :], ALU.mult).then_inc(S["taken_dve"], 1)
            dve.wait_ge(S["mod_ready"], 2)
            for j in range(KT):
                n = g0 + 16 + j
                src = bank[n % PROJ_BANKS]
                dve.wait_ge(S["proj_ready"], n + 1)
                if j == 0:
                    dve.wait_ge(S["merged_ready"], KT)
                V.tensor_scalar(gmT[:, j, 0:SEQ], src[:, 0:SEQ], mod[:, 16 + j, 0:1], None, ALU.mult)
                V.tensor_scalar(gmT[:, j, SEQ:T], src[:, SEQ:T], mod[:, 16 + j, 1:2], None, ALU.mult)\
                    .then_inc(S["taken_dve"], 1)
            dve.wait_ge(S["x1_in"], 96)

            def residual(t):
                m = TR[t]
                for c in range(2):
                    n = 2 * t + c
                    v = x1[0:m, t, c * 512:c * 512 + 512]
                    dve.wait_ge(S["gm_t"], n + 1)
                    V.scalar_tensor_tensor(out=v, in0=v, scalar=ALPHA, in1=bank[5 + n % 3][0:m, :], op0=ALU.mult,
                                           op1=ALU.add).then_inc(S["gm_added"], 1)
                dve.wait_ge(S["gm_added"], 2 * t + 2)
                tile_stats(t, x1[0:m, t, :], m).then_inc(S["nrm_sum"], 1)

            def affine(t, n, vec):
                m = TR[t]
                v = x1[0:m, t, :]
                ch.add(V.scalar_tensor_tensor(out=v, in0=v, scalar=mv[0:m, t, 0:1], in1=vec[0:m, 0, :],
                                              op0=ALU.subtract, op1=ALU.mult))
                reciprocal(n, t, 1)
                return V.scalar_tensor_tensor(out=v, in0=v, scalar=rstd[0:m, t:t + 1], in1=vec[0:m, 1, :],
                                              op0=ALU.mult, op1=ALU.add)

            def mixed(t, n):
                ch.add(affine(t, n, ln1))
                ch.done()
                tile_stats(3 + t, x1[0:TR[t], t, :], TR[t]).then_inc(S["nrm_sum"], 1)

            def normed(t, n):
                m = TR[t]
                reciprocal(n, 3 + t, 1)
                V.tensor_scalar(x2n[0:m, t, :], x1[0:m, t, :], mv[0:m, 3 + t, 0:1], rstd[0:m, 3 + t:4 + t],
                                ALU.subtract, ALU.mult).then_inc(S["norm_ready"], 1)

            residual(0)
            residual(1)
            dve.wait_ge(S["vecs_in"], 32)
            mixed(0, 3)
            residual(2)
            mixed(1, 4)
            normed(0, 5)
            mixed(2, 6)
            normed(1, 7)
            normed(2, 8)
            for k in range(0, KT, 2):
                dve.wait_ge(S["norm_t"], k + 1)
                b = bank[3 + k % 2]
                V.tensor_scalar(h2T[:, k, 0:SEQ], b[:, 0:SEQ], mod[:, 32 + k, 0:1], mod[:, 24 + k, 0:1], ALU.mult, ALU.add)
                V.tensor_scalar(h2T[:, k, SEQ:T], b[:, SEQ:T], mod[:, 32 + k, 1:2], mod[:, 24 + k, 1:2], ALU.mult,
                                ALU.add).then_inc(S["h2_dve"], 1)
            dve.wait_ge(S["lgt_ps"], 1)
            V.tensor_scalar(lgT, bank[0][0:NG + E, 0:T], b_route[:, 0:1], None, ALU.add).then_inc(S["lgt_ready"], 1)
            dve.wait_ge(S["lg_ps"], 3)
            for t in range(3):
                V.tensor_copy(lg[0:TR[t], t, :], bank[1][0:TR[t], 40 * t:40 * t + NG + E]).then_inc(S["lg_ready"], 1)
            dve.wait_ge(S["lg_ready"], 3)

            def op(ins):
                ch.add(ins)
                ch.done()

            gl, el = lg[:, :, 0:NG], lg[:, :, NG:NG + E]

            def wide(col, n):
                return col.unsqueeze(2).to_broadcast([P, 3, n])

            def first_max(vals, iota, n, top, tmp, oh):
                op(V.tensor_reduce(top, vals, AXX, ALU.max))
                op(V.tensor_tensor(tmp, vals, wide(top, n), ALU.is_ge))
                op(V.scalar_tensor_tensor(out=tmp, in0=tmp, scalar=-100.0, in1=iota, op0=ALU.mult, op1=ALU.add))
                op(V.tensor_reduce(r1[:, 15, :], tmp, AXX, ALU.min))
                op(V.tensor_tensor(oh, tmp, wide(r1[:, 15, :], n), ALU.is_equal))

            first_max(gl, g_iota[:, :, :], NG, r1[:, 0, :], r4[2][:, :, :], r4[3][:, :, :])
            V.tensor_tensor(r4[0][:, :, :], gl, wide(r1[:, 0, :], NG), ALU.subtract).then_inc(S["ex_in"], 1)
            op(V.tensor_scalar(r4[2][:, :, :], r4[3][:, :, :], 1.0, -NEG, ALU.subtract, ALU.mult))
            selm, tmp32, oh1 = (r[:, :, :] for r in r32)
            for t in range(3):
                ch.add(V.tensor_tensor(r32[0][:, t, :].rearrange("p (g e) -> p g e", g=NG),
                                       lg[:, t, NG:NG + E].rearrange("p (g e) -> p g e", g=NG),
                                       r4[2][:, t, :].unsqueeze(2).to_broadcast([P, NG, EPG]), ALU.add))
            ch.done()
            first_max(selm, e_iota[:, :, :], E, r1[:, 1, :], tmp32, oh1)
            op(V.scalar_tensor_tensor(out=selm, in0=oh1, scalar=2 * NEG, in1=selm, op0=ALU.mult, op1=ALU.add))
            first_max(selm, e_iota[:, :, :], E, r1[:, 2, :], tmp32, oh2[:, :, :])
            V.tensor_tensor(r1[:, 4, :], r1[:, 2, :], r1[:, 1, :], ALU.subtract).then_inc(S["ex_in"], 1)
            op(V.tensor_tensor(chosen[:, :, :], oh1, oh2[:, :, :], ALU.add))
            op(V.tensor_tensor(chosen[:, :, :], chosen[:, :, :], wide(valid[:, :], E), ALU.mult))
            op(V.tensor_copy(q_rep[:, :], q_iota[:, 1:2].to_broadcast([P, P])))
            for t in range(3):
                last = V.tensor_copy(rep[:, t, :, :], chosen[:, t, :].unsqueeze(1).to_broadcast([P, ROUNDS, E]))
            last.then_inc(S["rank_in"], 1)
            dve.wait_ge(S["ex_out"], 2)
            op(V.tensor_reduce(r1[:, 6, :], r4[1][:, :, :], AXX, ALU.add))
            op(V.tensor_scalar(r1[:, 7, :], r1[:, 5, :], 1.0, None, ALU.add))
            op(V.tensor_tensor(r1[:, 8, :], r1[:, 6, :], r1[:, 7, :], ALU.mult))
            op(V.reciprocal(wts[:, 0, :], r1[:, 8, :]))
            op(V.tensor_tensor(wts[:, 1, :], wts[:, 0, :], r1[:, 5, :], ALU.mult))
            op(V.tensor_tensor(val[:, :, :], oh2[:, :, :], wide(tokval[:, :], E), ALU.add))
            dve.wait_ge(S["rank_ps"], 1)
            V.tensor_tensor(flags[:, 0:1], bank[1][:, 128:129], q_iota[:, 1:2], ALU.is_gt).then_inc(S["flag_ready"], 1)
            op(V.scalar_tensor_tensor(out=pos[:, :, :], in0=chosen[:, :, :], scalar=-FAR,
                                      in1=bank[1][:, 0:3 * E].rearrange("p (t e) -> p t e", t=3), op0=ALU.mult, op1=ALU.add))
            op(V.tensor_scalar(pos[:, :, :], pos[:, :, :], FAR, None, ALU.add))
            def one_hots(n, e, shift):
                if not isinstance(n, int) or n:
                    dve.wait_ge(S["gather_ps"], n)
                V.tensor_copy(vcol[:, :], val[:, :, bass.ds(e, 1)].rearrange("p t e -> p (t e)"))\
                    .then_inc(S["vcol_ready"], 1)
                src = pos[:, :, bass.ds(e, 1)].rearrange("p t e -> p (t e)")
                if shift is None:
                    V.tensor_copy(pcol[:, :], src).then_inc(S["pcol_ready"], 1)
                else:
                    V.tensor_scalar(pcol[:, :], src, shift, None, ALU.subtract).then_inc(S["pcol_ready"], 1)
                dve.wait_ge(S["pcol_ready"], n + 1)
                dve.wait_ge(S["vcol_ready"], n + 1)
                for t in range(3):
                    last = V.tensor_scalar(onehot[:, t, :], slot_iota[:, :], pcol[:, t:t + 1], None, ALU.is_equal)
                last.then_inc(S["onehot_ready"], 1)

            def gathered(n, r):
                dve.wait_ge(S["gather_ps"], n + 1)
                V.tensor_scalar(sidx[r][:, :], bank[5][:, 0:1], 2.0, half_base[:, 0:1], ALU.mult, ALU.add)
                dve.wait_ge(S["xg_t"], n + 1)
                V.tensor_copy(xg[:, :, :, :].rearrange("p q c s -> p (q c s)"), bank[2][:, :]).then_inc(S["xg_ready"], 1)

            def gated(n):
                dve.wait_ge(S["gs_ready"], n + 1)
                V.tensor_tensor(gs[0:SLOTS, :], gs[SLOTS:P, :], bank[1][SLOTS:P, :], ALU.mult).then_inc(S["hrow_ready"], 1)

            def turned(n):
                dve.wait_ge(S["he_t"], n + 1)
                V.tensor_copy(he[:, :, :].rearrange("p f s -> p (f s)"), bank[6][:, 0:FT * SLOTS]).then_inc(S["he_ready"], 1)

            def step(n, r):
                one_hots(n + 1, n + 1, None)
                gated(n)
                turned(n)
                gathered(n + 1, r)

            one_hots(0, 0, None)
            dve.wait_ge(S["xr_ps"], 1)
            op(V.tensor_copy(flags[:, 1:2], bank[4][:, 0:1]))
            V.tensor_scalar(pick[:, :], x_iota[:, :], flags[:, 1:2], flags[:, 0:1], ALU.is_equal, ALU.mult)\
                .then_inc(S["pick_ready"], 1)
            dve.wait_ge(S["plan_ps"], 1)
            op(V.tensor_copy(first_slot[:, :], bank[4][:, 64:64 + EXTRA]))
            op(V.tensor_copy(plan_i[0:1, 0:EXTRA], bank[4][0:1, 96:96 + EXTRA]))
            op(V.memset(plan_i[0:1, EXTRA:2 * EXTRA], 0))
            V.tensor_copy(plan_i[0:1, 2 * EXTRA:2 * EXTRA + 1], bank[4][0:1, 128:129]).then_inc(S["plan_ready"], 1)
            gathered(0, 0)
            step(0, 1)
            step(1, 2)
            with dve.Fori(0, (E - 3) // 6) as it:
                for r in range(2, 8):
                    dve.wait_ge(S[f"scattered{r % 2}"], it * 48 + 16 * (r // 2))
                    step(it * 6 + r, (r + 1) % 3)
            for e in range(2 + (E - 3) // 6 * 6, E - 1):
                dve.wait_ge(S[f"scattered{e % 2}"], 16 * (e // 2))
                step(e, (e + 1) % 3)
            gated(E - 1)
            turned(E - 1)
            n_over = dve.value_load(plan_i[0:1, 2 * EXTRA:2 * EXTRA + 1], min_val=0, max_val=EXTRA)
            with dve.If(n_over > 0):
                with dve.Fori(0, n_over) as i:
                    e = dve.value_load(plan_i[0:1, bass.ds(i, 1)], min_val=0, max_val=E - 1)
                    dve.wait_ge(S["scattered0"], i * 16 + 8 * E)
                    one_hots(i + E, e, first_slot[:, bass.ds(i, 1)])
                    gathered(i + E, 0)
                    gated(i + E)
                    turned(i + E)
                dve.nop()
            with dve.Else():
                dve.nop()
            for t in range(3):
                m = TR[t]
                y1, y2 = comb[t][0:m, 0:D], comb[t][0:m, D:2 * D]
                dve.wait_ge(S[f"comb_in{t}"], 16)
                op(V.tensor_scalar(y1, y1, wts[0:m, 0, t:t + 1], None, ALU.mult))
                op(V.scalar_tensor_tensor(out=y1, in0=y2, scalar=wts[0:m, 1, t:t + 1], in1=y1, op0=ALU.mult, op1=ALU.add))
                op(V.tensor_tensor(y1, y1, gf_rows[0:m, t // 2, :], ALU.mult))
                op(V.scalar_tensor_tensor(out=x1[0:m, t, :], in0=x1[0:m, t, :], scalar=ALPHA, in1=y1, op0=ALU.mult, op1=ALU.add))
            for t in range(3):
                tile_stats(t, x1[0:TR[t], t, :], TR[t]).then_inc(S["nrm_sum"], 1)
            dve.wait_ge(S["vecs_in"], 64)
            for t in range(3):
                affine(t, 9 + t, ln2).then_inc(S["fin_ready"], 1)


_INS = ['x_prompt', 'x_sample', 'cache_sb_k', 'cache_sb_v', 'state_gla', 'c_prompt', 'c_sample', 'w_cond', 'b_cond',
        'w_in', 'w_gla_a2', 'b_gla_a', 'gla_norm_g', 'w_branch_a', 'w_branch_b', 'w_out', 'ln1_g', 'ln1_b', 'w_group',
        'b_group', 'w_router', 'b_router', 'w_exp_gate', 'w_exp_up', 'w_exp_down', 'ln2_g', 'ln2_b']
_OUTS = [("y_prompt", (1, SEQ, D)), ("y_sample", (1, DSEQ, D)), ("sb_k_prompt", (1, 1, SEQ, SH, SD)),
         ("sb_v_prompt", (1, 1, SEQ, SH, SD)), ("gla_state_prompt", (1, 1, GH, DK, DV)),
         ("sb_k_sample", (1, 1, DSEQ, SH, SD)), ("sb_v_sample", (1, 1, DSEQ, SH, SD)),
         ("gla_state_sample", (1, 1, GH, DK, DV))]


def kernel(**inputs):
    import numpy as _np
    import concourse.bacc as _bacc
    from concourse.bass_utils import run_bass_kernel_spmd as _run

    nc = _bacc.Bacc("TRN2", target_bir_lowering=False, num_devices=1)
    arrays, args, outs = {}, {}, {}
    for name in _INS:
        v = _np.ascontiguousarray(inputs[name])
        arrays[f"in_{name}"] = v
        args[name] = nc.dram_tensor(f"in_{name}", v.shape, mybir.dt.from_np(v.dtype), kind="ExternalInput").ap()
    for name, shape in _OUTS:
        outs[name] = nc.dram_tensor(f"out_{name}", shape, F32, kind="ExternalOutput").ap()
    build(nc, args, outs)
    r = _run(nc, [arrays], core_ids=[0])
    return tuple(r.results[0][f"out_{name}"] for name, _ in _OUTS)
```

```python
from contextlib import ExitStack

import concourse.bass as bass
from concourse import mybir

F32 = mybir.dt.float32
F32R = mybir.dt.float32r
BF16 = mybir.dt.bfloat16
I32 = mybir.dt.int32
ALU = mybir.AluOpType
ACT = mybir.ActivationFunctionType
AXX = mybir.AxisListType.X

P = 128
D = 1024
KT = D // P
SEQ, DSEQ, PAST = 256, 64, 128
T = SEQ + DSEQ
TR = (128, 128, 64)
TC = (slice(0, 128), slice(128, 256), slice(256, 320))
GH, DK, DV = 4, 128, 256
SH, SD = 16, 64
RANK = 16
NG, EPG = 4, 8
E = NG * EPG
FF = 512
FT = FF // P
EPS = 1e-5
ALPHA = 2.0 ** 0.25
TAU = 16.0
NEG = -1e30
FAR = 1e4
SKIP = 100000
SLOTS = 64
OVER = (2 * T) // SLOTS
ROUNDS = -(-T // SLOTS) - 1
CB = 512
CW = KT * CB
DENSE_RING = 2
HI_SLOT, COND_SLOT = 2, 3
RING = 9
LAST_ORDER = (0, 2, 1)
LEVELS = 8
NORM_BANKS = ((3, 4), (1, 2), (3, 4))
NORM_ORDER = (0, 1, 3, 2, 4, 5)


EXTRA = ("cr", "ct", "vat", "vbt")


def projection_groups():
    groups, chunks, turns = [], [], []

    def chunk(matrix, col, slot=None):
        if slot is None:
            slot = sum(c[2] < DENSE_RING for c in chunks) % DENSE_RING
        chunks.append((matrix, col, slot))

    def cond(c, slot=None):
        chunk("cond", c * CB, slot)
        groups.append(("cr", c, "act", len(chunks) - 1))
        turns.append(("ct", c, "act", None))

    def turned():
        groups.extend(turns)
        turns.clear()

    weight = {}

    def project(name, i, matrix, first, engine="act"):
        if i % 4 == 0:
            chunk(matrix, first + i * P)
            weight[0] = len(chunks) - 1
        groups.append((name, i, engine, weight[0]))
        turned()
        if name in ("va", "vb"):
            turns.append((name + "t", i, "act", None))

    for c in range(4):
        cond(c, c)
        turned()
    groups.append(("lra", 0, "act", None))
    for name, first, n in (("qa", 0, 4), ("ka", 512, 4), ("va", 1024, 8)):
        for i in range(n):
            project(name, i, "in", first)
    turned()
    for name, first in (("qb", 3088), ("kb", 4112), ("vb", 5136)):
        for i in range(KT):
            project(name, i, "in", first)
    turned()
    n = 0
    for name, first in (("ga", 2048), ("gta", 6160), ("gtb", 7184)):
        for i in range(KT):
            project(name, i, "in", first)
            if n % 3 == 1:
                cond(4 + n // 3, COND_SLOT)
            n += 1
    turned()
    for name in ("bb", "ba", "out"):
        for i in range(KT):
            project(name, i, name, 0, "dve")
    return groups, chunks


GROUPS, DENSE = projection_groups()
ND = len(DENSE)
PROJ_BANKS = 3
PROJECTIONS = [n for n, g in enumerate(GROUPS) if g[0] not in EXTRA + ("lra",)]


def group_index(name, i):
    return [g[:2] for g in GROUPS].index((name, i))


def taken_count(upto, engine):
    return sum(g[2] == engine for g in GROUPS[:upto + 1])


def build(nc, a, out):
    ctx = ExitStack()
    with ctx:
        def sb(name, shape, dt=F32, stack=ctx):
            return stack.enter_context(nc.sbuf_tensor(name, shape, dt))

        def sem(name):
            return ctx.enter_context(nc.semaphore(name))

        ident = sb("ident", [P, P])
        ones = sb("ones", [P, P])
        neg_tri = sb("neg_tri", [P, P])
        neg_ones = sb("neg_ones", [P, P])
        tri_strict = sb("tri_strict", [P, P])
        tri_tau = sb("tri_tau", [P, 2 * P])
        ident_b = sb("ident_b", [P, P], BF16)
        mask_sb = sb("mask_sb", [P, 512], BF16)
        slot_iota = sb("slot_iota", [P, SLOTS])
        iota_i = sb("iota_i", [P, SLOTS], I32)
        e_iota = sb("e_iota", [P, 3, E])
        g_iota = sb("g_iota", [P, 3, NG])
        tokval = sb("tokval", [P, 3])
        half_base = sb("half_base", [P, 1])
        valid = sb("valid", [P, 3])
        q_iota = sb("q_iota", [P, 2])
        x_iota = sb("x_iota", [P, OVER])
        cols = sb("cols", [P, 72])
        silu_c = sb("silu_c", [P, KT, 32])
        mod = sb("mod", [P, 6 * KT, 2])
        total = sb("total", [P, GH])
        eps_col = sb("eps_col", [P, 1])
        stats = sb("stats", [P, 12, 12])
        mv = sb("mv", [P, 12, 2])
        rstd = sb("rstd", [P, 12])
        newton = sb("newton", [P, 12])
        half_var = sb("half_var", [P, 12])
        wts = sb("wts", [P, 2, 3])
        dense_alias = ExitStack()
        w_lo = [sb(f"w_lo{i}", [P, KT, CB], F32R, dense_alias) for i in range(DENSE_RING)]
        w_hi = sb("w_hi", [P, KT, CB], F32R, dense_alias)
        dense_alias.close()
        ring = [sb(f"ring{i}", [P, CW]) for i in range(DENSE_RING + 1)]

        s1 = ExitStack()
        levels = sb("levels", [P, LEVELS, P], F32, s1)
        qa = sb("qa", [P, GH, T], F32, s1)
        ka = sb("ka", [P, GH, T], F32, s1)
        la = sb("la", [P, 3, 512], F32, s1)
        pd = [sb(f"pd{i}", [P, GH, T], F32, s1) for i in range(2)]
        bt = sb("bt", [P, GH, T], F32, s1)
        va = sb("va", [P, 3, D], F32, s1)
        acc = sb("acc", [P, 3, GH, P], F32, s1)
        cross = sb("cross", [P, GH, P], F32, s1)
        s0 = sb("s0", [P, GH, DV], F32, s1)
        alias = ExitStack()
        w_lra_hi = sb("w_lra_hi", [P, KT, RANK], F32R, alias)
        alias.close()
        mtmp = sb("mtmp", [P, 2, 512], F32, s1)
        mtmp_s = sb("mtmp_s", [DSEQ, GH, DSEQ], F32, s1)
        h_hi = sb("h_hi", [P, KT, T], F32R, s1)
        on = sb("on", [P, 3, D], F32, s1)
        alias = ExitStack()
        h_lo1 = sb("h_lo1", [P, KT, T], F32R, alias)
        alias.close()
        obT = sb("obT", [P, KT, T], F32, s1)
        ckT = sb("ckT", [P, KT, P], F32, s1)
        cv = sb("cv", [P, D], F32, s1)
        qb = sb("qb", [P, KT, T], F32, s1)
        kb = sb("kb", [P, KT, T + 64], F32, s1)
        vb = sb("vb", [P, 3, D], F32, s1)
        ab = [sb(f"ab{i}", [P, 512], F32, s1) for i in range(2)]
        alias = ExitStack()
        sp_lo = [sb(f"sp_lo{i}", [P, 512], F32R, alias) for i in range(2)]
        alias.close()
        sp_ = [sb(f"sp{i}", [P, 512], F32, s1) for i in range(2)]
        wgt = [sb(f"wgt{i}", [P, 512], F32, s1) for i in range(2)]
        alias = ExitStack()
        w_lra_lo = sb("w_lra_lo", [P, KT, RANK], F32R, alias)
        alias.close()
        w_lra = sb("w_lra", [P, KT, RANK], F32, s1)
        crow = sb("crow", [P, P], F32, s1)
        lraT = ab[1][0:32, 0:T]
        wa2 = sp_[1][0:32, :]
        rows = ab[0][:, 0:P]
        xt = vb
        xn = on
        ck = wgt
        ke = pd[0]
        htmp = [pd[k % 2][:, k // 2, :] for k in range(KT)]
        vtmp = [sp_[0][:, 0:T], ab[0][:, 0:T]]
        ob_hi, ob_lo = h_hi, h_lo1
        ket = la
        s1.close()

        s2 = ExitStack()
        alias = ExitStack()
        m_hi = sb("m_hi", [P, KT, T], F32R, alias)
        m_lo = sb("m_lo", [P, KT, T], F32R, alias)
        alias.close()
        ga = sb("ga", [P, KT, T], F32, s2)
        gta = sb("gta", [P, KT, T], F32, s2)
        gtb = sb("gtb", [P, KT, T], F32, s2)
        oa_hi = sb("oa_hi", [P, KT, T], F32R, s2)
        h_lo2 = oa_hi
        alias = ExitStack()
        cond_slot = sb("cond_slot", [P, CW], F32, alias)
        sp_hi = [sb(f"sp_hi{i}", [P, 512], F32R, alias) for i in range(2)]
        tri_r = sb("tri_r", [P, P], F32R, alias)
        ones_r = sb("ones_r", [P, P], F32R, alias)
        alias.close()
        oa_lo = sb("oa_lo", [P, KT, T], F32R, s2)
        kbtok = sb("kbtok", [P, 3, D], F32, s2)
        s2.close()
        s3 = ExitStack()
        h2T = sb("h2T", [P, KT, T], F32, s3)
        sb("unused", [P, KT, T], F32, s3)
        gmT = sb("gmT", [P, KT, T], F32, s3)
        s3.close()

        ring += [sb(f"ring{i}", [P, CW]) for i in range(DENSE_RING + 1, RING)]
        x1 = sb("x1", [P, 3, D])
        hf = sb("hf", [P, 3, D])
        x2n = hf
        gf_rows = sb("gf_rows", [P, 2, D])
        ones_b = sb("ones_b", [P, P], BF16)
        tri_b = sb("tri_b", [P, P], BF16)
        w_route = sb("w_route", [P, KT, NG + E])
        b_route = sb("b_route", [NG + E, 1])
        lg = sb("lg", [P, 3, NG + E])
        r4 = [sb(f"r4_{i}", [P, 3, NG]) for i in range(4)]
        r32 = [sb(f"r32_{i}", [P, 3, E]) for i in range(3)]
        r1 = sb("r1", [P, 16, 3])
        oh2 = sb("oh2", [P, 3, E])
        chosen = sb("chosen", [P, 3, E], BF16)
        pos = sb("pos", [P, 3, E])
        val = sb("val", [P, 3, E])
        rep = sb("rep", [P, 3, ROUNDS, E], BF16)
        q_rep = sb("q_rep", [P, P])
        flags = sb("flags", [P, 4])
        pick = sb("pick", [P, OVER])
        plan_i = sb("plan_i", [1, 2 * OVER + 1], I32)
        first_slot = sb("first_slot", [P, OVER])
        onehot = sb("onehot", [P, 3, SLOTS])
        pcol = sb("pcol", [P, 3])
        vcol = sb("vcol", [P, 3])
        sidx = [sb(f"sidx{i}", [P, 1], I32) for i in range(6)]
        s4 = ExitStack()
        ln1 = sb("ln1", [P, 2, D], F32, s4)
        s4.close()
        xrow = sb("xrow", [P, CB])
        xg = sb("xg", [P, 4, 2, SLOTS])
        gs = sb("gs", [P, FF])
        ystage = [sb(f"ystage{i}", [P, CB]) for i in range(3)]
        he = sb("he", [P, FT, SLOTS])
        diag = ystage[1]
        lgT = xrow[0:NG + E, 0:T]
        comb = [ring[3 + t // 2][:, (t % 2) * 2 * D:(t % 2 + 1) * 2 * D] for t in range(3)]
        ln2 = ring[5][:, 0:2 * D].rearrange("p (a d) -> p a d", a=2)

        ybuf = nc.dram_tensor("expert_rows", [4 * T, CB], F32, kind="Internal").ap()

        bank = [ctx.enter_context(nc.psum_tensor(f"bank{i}", [P, 512], F32)) for i in range(8)]

        names = """const_ready rows_in x_in lra_in misc_in vecs_in x1_in cols_t silu_ready mod_ready xn_ready xn_t
            h_dve h_act h_pool hi_ready lo_ready lra_hi lra_lo h_moved ob_hi_ready ob_lo_ready cond_in
            proj_ready taken_act taken_dve xla_ps la_ready b_ps b_ready dec_ready exp_ready pd_ready lev_ps
            lev_taken lev_added kd_ready ke_ready ke_t ket_ready st_ps st_ready qe_ready go_ps go_ready ck_t
            ck_ready z_ready l_ready sp_ready rest_ready w_ready o_ready o_taken kb_t kb_tok on_ready on_t
            oa_ready oa_hi_ready oa_lo_ready sig_ready m_ready m_hi_ready m_lo_ready gm_t gm_added norm_ready
            norm_t h2_dve h2_act lgt_ps lgt_ready lg_ps lg_ready ex_in ex_out rank_in rank_ps hb_t hb_ready
            flag_ready xr_ps pick_ready plan_ps plan_ready gfr_in gfr_ps gf_ready onehot_ready gather_ps
            xrow_ready xg_t xg_ready gu_ps gs_ready hrow_ready he_t he_ready down_ps ys_ready scattered0
            scattered1 scattered2 index_ps weighted summed_pool gated_pool comb_in0 comb_in1 comb_in2 vcol_ready
            pcol_ready fin_ready stored act_chain dve_chain pool_chain gla_stored rstd_ready nrm_sum pe_passed
            pool_passed""".split()
        S = {n: sem(n) for n in names}
        chunk_in = [sem(f"chunk_in{i}") for i in range(RING)]

        class Chain:

            def __init__(self, eng, s):
                self.eng, self.s, self.n = eng, s, 0

            def add(self, ins):
                self.n += 1
                return ins.then_inc(self.s, 1)

            def done(self):
                self.eng.wait_ge(self.s, self.n)

        def consumed(i):
            return S["proj_ready"], max(n for n, g in enumerate(GROUPS) if g[3] == i) + 1

        USED = ("gu_ps", "gu_ps", "down_ps")

        def arrived(i):
            slot = DENSE[i][2]
            return (S["cond_in"] if slot == COND_SLOT else chunk_in[slot]), 16 * sum(c[2] == slot for c in DENSE[:i + 1])

        def base(e):
            return 3 * (-e % 3)

        def expert_use(s, turn):
            before = sum(c[2] == s for c in DENSE) if s <= HI_SLOT else 0
            return 16 * (before + turn + 1)

        USES = [len(range(b, E, 3)) for b in range(3)]

        SRC = {"cond": a["w_cond"][0], "in": a["w_in"][0], "ba": a["w_branch_a"][0], "bb": a["w_branch_b"][0],
               "out": a["w_out"][0]}

        block = ctx.enter_context(nc.Block())

        @block.sync
        def _(sp):
            def expert_chunk(e, q, slot):
                s = chunk_in[slot]
                dst = ring[slot]
                if q < 2:
                    w = (a["w_exp_gate"], a["w_exp_up"])[q][0]
                    src = w[bass.ds(e, 1)].rearrange("e (k p) n -> p (e k) n", p=P)
                    sp.dma_start(dst[:, :].rearrange("p (k n) -> p k n", k=KT), src).then_inc(s, 16)
                else:
                    src = a["w_exp_down"][0][bass.ds(e, 1)].rearrange("e (k p) n -> p (e k) n", p=P)
                    sp.dma_start(dst[:, :].rearrange("p (k n) -> p k n", k=FT), src).then_inc(s, 16)

            sp.dma_start(rows[0:8, :], a["c_prompt"].rearrange("a (k p) -> (a k) p", p=P)).then_inc(S["rows_in"], 16)
            sp.dma_start(rows[8:16, :], a["c_sample"].rearrange("a (k p) -> (a k) p", p=P)).then_inc(S["rows_in"], 16)
            sp.dma_start(rows[16:64, :], a["b_cond"].rearrange("a (k p) -> (a k) p", p=P)).then_inc(S["rows_in"], 16)
            sp.dma_start(rows[64:72, :], a["gla_norm_g"].rearrange("a h (j p) -> (a h j) p", p=P)).then_inc(S["rows_in"], 16)

            def freed(i):
                before = [n for n in range(i) if DENSE[n][2] == DENSE[i][2]]
                if DENSE[i][2] == COND_SLOT and len(before) == 1:
                    return group_index("ga", 0)
                return consumed(before[-1])[1] if before else 0

            for i in sorted(range(ND), key=freed):
                name, c0, slot = DENSE[i]
                before = [n for n in range(i) if DENSE[n][2] == slot]
                if before:
                    sp.wait_ge(*consumed(before[-1]))
                if slot == COND_SLOT and len(before) == 1:
                    sp.wait_ge(S["go_ps"], 6)
                    sp.wait_ge(S["st_ready"], 4)
                src = SRC[name].rearrange("(k p) n -> p k n", p=P)[:, :, c0:c0 + CB]
                dst = cond_slot if slot == COND_SLOT else ring[slot]
                sp.dma_start(dst[:, :].rearrange("p (k n) -> p k n", k=KT), src).then_inc(arrived(i)[0], 16)
                if i == 1:
                    sp.dma_start(xt[:, 0:2, :], a["x_prompt"][0].rearrange("(t p) d -> p t d", p=P)).then_inc(S["x_in"], 16)
                    sp.dma_start(xt[0:64, 2, :], a["x_sample"][0]).then_inc(S["x_in"], 16)
            sp.wait_ge(S["proj_ready"], group_index("bb", KT - 1) + 1)
            sp.wait_ge(S["on_t"], KT)
            expert_chunk(1, 1, 7)
            expert_chunk(1, 2, 8)
            for q in range(3):
                sp.wait_ge(*consumed(max(n for n in range(ND) if DENSE[n][2] == q) if q < DENSE_RING else ND - 1))
                expert_chunk(0, q, q)
            sp.wait_ge(S["stored"], 32)
            sp.wait_ge(*consumed(ND - 1))
            expert_chunk(1, 0, 6)
            sp.wait_ge(S["gm_t"], 6)
            expert_chunk(2, 1, 4)
            expert_chunk(2, 2, 5)
            sp.wait_ge(S["hb_t"], 6)
            expert_chunk(2, 0, 3)
            with sp.Fori(0, E // 3 - 1) as it:
                for r in range(3):
                    for q in range(3):
                        sp.wait_ge(S[USED[q]], it * 3 + (r + 1))
                        expert_chunk(it * 3 + (3 + r), q, base(r) + q)
            for e in (30, 31):
                for q in range(3):
                    sp.wait_ge(S[USED[q]], e - 2)
                    expert_chunk(e, q, base(e) + q)
            sp.wait_ge(S["plan_ready"], 1)
            n_over = sp.value_load(plan_i[0:1, 2 * OVER:2 * OVER + 1], min_val=0, max_val=OVER)
            with sp.If(n_over > 0):
                with sp.Fori(0, n_over) as i:
                    e = sp.value_load(plan_i[0:1, bass.ds(i, 1)], min_val=0, max_val=E - 1)
                    for q in range(3):
                        sp.wait_ge(S[USED[q]], i + E)
                        expert_chunk(e, q, q)
                sp.nop()
            with sp.Else():
                sp.nop()

        @block.gpsimd
        def _(pool):
            ch = Chain(pool, S["pool_chain"])

            def select(t, pattern, base, cm, fill, op=ALU.is_ge):
                ch.done()
                ch.add(pool.affine_select(out=t, in_=t, compare_op=op, fill=fill, base=base, pattern=pattern,
                                          channel_multiplier=cm))

            ch.add(pool.memset(ident[:, :], 0.0))
            ch.add(pool.memset(eps_col[:, :], EPS))
            ch.add(pool.memset(lraT, 1.0))
            ch.add(pool.memset(mv[:, :, :], 1.0))
            ch.add(pool.memset(silu_c[:, :, :], 0.0))
            select(ident[:, :], [[-1, P]], 0, 1, 1.0, ALU.not_equal)
            ch.done()
            pool.nop().then_inc(S["const_ready"], 1)
            for t, v in ((ones[:, :], 1.0), (neg_ones[:, :], -1.0),
                         (neg_tri[:, :], -1.0), (tri_strict[:, :], 1.0), (tri_tau[:, :], 1.0 / TAU),
                         (ident_b[:, :], 0.0), (mask_sb[:, :], 0.0), (valid[:, :], 1.0),
                         (levels[:, :, :], 1.0), (kb[:, :, T:T + 64], 0.0)):
                ch.add(pool.memset(t, v))
            select(ident_b[:, :], [[-1, P]], 0, 1, 1.0, ALU.not_equal)
            select(neg_tri[:, :], [[-1, P]], 0, 1, 0.0)
            select(tri_strict[:, :], [[1, P]], -1, -1, 0.0)
            select(tri_tau[:, 0:P], [[1, P]], 0, -1, 0.0)
            for c in (0, 256):
                select(mask_sb[:, c:c + P], [[1, P]], -1, -1, NEG)
            select(mask_sb[:, 448:512], [[1, 64]], -1, -1, NEG)
            select(valid[:, 2:3], [[0, 1]], 63, -1, 0.0)
            select(levels[:, 0, :], [[-1, P]], 0, 1, 0.0, ALU.is_equal)
            for n in range(1, LEVELS):
                size = 2 ** n
                view = levels[:, n, :].rearrange("p (b c) -> p b c", c=size)
                right = view[:, :, size // 2:size]
                blocks = P // size
                select(right, [[-size, blocks], [0, size // 2]], 0, 1, 0.0)
                select(right, [[size, blocks], [0, size // 2]], size // 2 - 1, -1, 0.0)
                ch.add(pool.memset(view[:, :, 0:size // 2], 0.0))

            def iota(dst, width, pattern, base, cm):
                ch.done()
                ch.add(pool.iota(iota_i[:, 0:width], pattern=pattern, base=base, channel_multiplier=cm))
                ch.done()
                ch.add(pool.tensor_copy(dst, iota_i[:, 0:width]))

            iota(slot_iota[:, :], SLOTS, [[1, SLOTS]], 0, 0)
            for t in range(3):
                iota(e_iota[:, t, :], E, [[1, E]], 0, 0)
                iota(g_iota[:, t, :], NG, [[1, NG]], 0, 0)
            iota(tokval[:, :], 3, [[2 * P, 3]], -SKIP, 2)
            ch.done()
            ch.add(pool.memset(half_base[0:SLOTS, :], 2.0 * SKIP))
            ch.done()
            ch.add(pool.memset(half_base[SLOTS:P, :], 2.0 * SKIP + 1.0))
            iota(x_iota[:, :], OVER, [[1, OVER]], 0, 0)
            for j in range(ROUNDS):
                ch.done()
                lo, hi = E * j, E * j + E
                ch.add(pool.memset(q_iota[lo:hi, 1:2], float(SLOTS * (j + 1))))
                ch.done()
                ch.add(pool.iota(iota_i[lo:hi, 0:1], pattern=[[0, 1]], base=0, channel_multiplier=1))
                ch.done()
                ch.add(pool.tensor_copy(q_iota[lo:hi, 0:1], iota_i[lo:hi, 0:1]))
            ch.done()
            pool.nop().then_inc(S["const_ready"], 1)

            def rest(upto):
                while rests[0] < min(upto, len(PROJECTIONS)):
                    n = rests[0]
                    slot, c = DENSE[GROUPS[PROJECTIONS[n]][3]][2], slice((n % 4) * P, (n % 4 + 1) * P)
                    raw = ring[slot][:, :].rearrange("p (k n) -> p k n", k=KT)
                    pool.wait_ge(S["hi_ready"], n + 1)
                    pool.tensor_tensor(w_lo[slot][:, :, c], raw[:, :, c], w_hi[:, :, c].bitcast(F32), ALU.subtract)\
                        .then_inc(S["lo_ready"], 1)
                    rests[0] += 1

            rests = [0]
            pool.wait_ge(S["lra_hi"], 1)
            pool.tensor_tensor(w_lra_lo[:, :, :], w_lra[:, :, :], w_lra_hi[:, :, :].bitcast(F32), ALU.subtract)\
                .then_inc(S["lra_lo"], 1)
            for k in range(1, KT, 2):
                pool.wait_ge(S["h_act"], k // 2 + 1)
                pool.tensor_tensor(h_lo1[:, k, :], htmp[k], h_hi[:, k, :].bitcast(F32), ALU.subtract)\
                    .then_inc(S["h_pool"], 1)
            second = PROJECTIONS.index(group_index("qb", 0))
            for n in range(1, LEVELS):
                rest(second + 2 * n + 5)
                pool.wait_ge(S["lev_taken"], n + 1)
                if n < LEVELS - 1:
                    pool.tensor_tensor(acc[0:64, 2, :, 0:64], acc[0:64, 2, :, 0:64],
                                       mtmp_s[:, :, :], ALU.add)
                for t in range(2):
                    last = pool.tensor_tensor(acc[:, t, :, :], acc[:, t, :, :],
                                              mtmp[:, t, :].rearrange("p (h t) -> p h t", h=GH), ALU.add)
                last.then_inc(S["lev_added"], 1)

            rest(PROJECTIONS.index(group_index("bb", 0)) + 3)
            pool.wait_ge(S["o_ready"], KT)
            pool.wait_ge(S["kb_t"], 6)
            pool.wait_ge(S["gla_stored"], 16 * 6)
            pool.dma_start(x1[:, 0:2, :], a["x_prompt"][0].rearrange("(t p) d -> p t d", p=P)).then_inc(S["x1_in"], 16)
            pool.dma_start(x1[0:64, 2, :], a["x_sample"][0]).then_inc(S["x1_in"], 16)
            rest(PROJECTIONS.index(group_index("ba", 0)) + 3)
            pool.dma_start(w_route[:, :, 0:NG], a["w_group"][0].rearrange("(k p) n -> p k n", p=P)).then_inc(S["x1_in"], 16)
            pool.dma_start(w_route[:, :, NG:NG + E], a["w_router"][0].rearrange("(k p) n -> p k n", p=P)).then_inc(S["x1_in"], 16)
            rest(PROJECTIONS.index(group_index("ba", 0)) + 4)
            pool.dma_start(b_route[0:NG, :], a["b_group"].rearrange("a n -> n a")).then_inc(S["x1_in"], 16)
            pool.dma_start(b_route[NG:NG + E, :], a["b_router"].rearrange("a n -> n a")).then_inc(S["x1_in"], 16)
            rest(PROJECTIONS.index(group_index("out", 0)))
            pool.dma_start(ln1[:, 0, :], a["ln1_g"][0].partition_broadcast(P)).then_inc(S["vecs_in"], 16)
            pool.dma_start(ln1[:, 1, :], a["ln1_b"][0].partition_broadcast(P)).then_inc(S["vecs_in"], 16)
            rest(len(PROJECTIONS))

            def scatter(n, r, b):
                pool.wait_ge(S["ys_ready"], n + 1)
                if not isinstance(n, int):
                    pool.sem_inc(S["pool_passed"], 1)
                pool.indirect_dma_start(out=ybuf[:, :], out_offset=bass.IndirectOffsetOnAxis(ap=sidx[r][:, 0:1], axis=0),
                                        in_=ystage[b][:, :], in_offset=None, bounds_check=4 * T - 1,
                                        oob_is_err=False).then_inc(S[f"scattered{b}"], 16)

            scatter(0, 0, 0)
            with pool.Fori(0, (E - 2) // 6) as it:
                for r in range(1, 7):
                    scatter(it * 6 + r, r % 6, r % 3)
            pool.wait_ge(S["down_ps"], E - 2)
            pool.dma_start(ln2[:, 0, :], a["ln2_g"][0].partition_broadcast(P)).then_inc(S["vecs_in"], 16)
            pool.dma_start(ln2[:, 1, :], a["ln2_b"][0].partition_broadcast(P)).then_inc(S["vecs_in"], 16)
            scatter(E - 1, (E - 1) % 6, (E - 1) % 3)
            pool.wait_ge(S["plan_ready"], 1)
            n_over = pool.value_load(plan_i[0:1, 2 * OVER:2 * OVER + 1], min_val=0, max_val=OVER)
            with pool.If(n_over > 0):
                with pool.Fori(0, n_over) as i:
                    scatter(i + E, 0, 0)
                pool.wait_ge(S["scattered1"], 16 * USES[1])
                pool.wait_ge(S["scattered2"], 16 * USES[2])
                pool.wait_ge(S["scattered0"], n_over * 16 + 16 * USES[0])
                pool.nop()
            with pool.Else():
                for b in range(3):
                    pool.wait_ge(S[f"scattered{b}"], 16 * USES[b])
                pool.nop()
            for t in range(3):
                n = TR[t]
                pool.dma_start(comb[t][0:n, :], ybuf[4 * P * t:4 * P * t + 4 * n, :].rearrange("(p k) d -> p (k d)", k=4))\
                    .then_inc(S[f"comb_in{t}"], 16)
            pool.wait_ge(S["weighted"], 3)
            y1 = comb[1][:, 0:D]
            pool.tensor_tensor(y1, y1, comb[1][:, D:2 * D], ALU.add).then_inc(S["summed_pool"], 1)
            pool.wait_ge(S["summed_pool"], 1)
            pool.tensor_tensor(y1, y1, gf_rows[:, 0, :], ALU.mult).then_inc(S["gated_pool"], 1)

        @block.scalar
        def _(act):
            ch = Chain(act, S["act_chain"])
            X = nc.scalar

            act.wait_ge(S["const_ready"], 1)
            act.dma_start(w_lra[:, :, :], a["w_in"][0].rearrange("(k p) n -> p k n", p=P)[:, :, 3072:3088]).then_inc(S["lra_in"], 16)
            act.dma_start(wa2[0:RANK, :], a["w_gla_a2"][0]).then_inc(S["lra_in"], 16)
            act.dma_start(wa2[RANK:RANK + 1, :], a["b_gla_a"]).then_inc(S["lra_in"], 16)
            act.wait_ge(S["cols_t"], 1)
            X.activation(silu_c[:, :, 0:2], bank[7][:, 0:16].rearrange("p (g k) -> p k g", g=2), ACT.Silu).then_inc(S["silu_ready"], 1)

            g = [0]

            def take(name, i):
                n = g[0]
                assert GROUPS[n][:2] == (name, i)
                src = bank[n % PROJ_BANKS]
                act.wait_ge(S["proj_ready"], n + 1)
                if name == "cr":
                    ins = X.activation(crow[:, :], src[:, 0:P], ACT.Copy)
                elif name == "ct":
                    ins = X.activation(mod[:, 4 * i:4 * i + 4, :], src[:, 0:P].rearrange("p (m c) -> p m c", c=32)[:, :, 0:2],
                                       ACT.Copy)
                elif name == "lra":
                    ins = X.activation(lraT[0:RANK, :], src[0:RANK, 0:T], ACT.Copy)
                elif name == "qa":
                    ins = X.activation(qa[:, i, :], src[:, 0:T], ACT.Copy, scale=DK ** -0.5)
                elif name == "qb":
                    ins = X.activation(qb[:, i, :], src[:, 0:T], ACT.Copy, scale=SD ** -0.5)
                elif name == "ka":
                    ins = X.activation(ka[:, i, :], src[:, 0:T], ACT.Copy)
                elif name == "kb":
                    ins = X.activation(kb[:, i, 0:T], src[:, 0:T], ACT.Copy)
                elif name in ("va", "vb"):
                    ins = X.activation(vtmp[i % 2], src[:, 0:T], ACT.Copy)
                elif name in ("vat", "vbt"):
                    dst = va if name == "vat" else vb
                    X.activation(dst[:, 0:2, i * P:i * P + P], src[:, 0:2 * P].rearrange("p (t d) -> p t d", t=2), ACT.Copy)
                    ins = X.activation(dst[0:64, 2, i * P:i * P + P], src[0:64, 2 * P:3 * P], ACT.Copy)
                else:
                    dst = {"ga": ga, "gta": gta, "gtb": gtb}[name]
                    ins = X.activation(dst[:, i, :], src[:, 0:T], ACT.Copy)
                ins.then_inc(S["taken_act"], 1)
                g[0] += 1
                if n in PROJECTIONS:
                    high(PROJECTIONS.index(n) + 3)

            def take_cond(first, n):
                for c in range(first, first + n):
                    take("cr", c)
                    take("ct", c)

            def extras():
                while GROUPS[g[0]][0] in EXTRA:
                    take(*GROUPS[g[0]][:2])

            def deviation(i0, n):
                X.activation(rstd[:, i0:i0 + n], mv[:, i0:i0 + n, 1], ACT.Sqrt, bias=eps_col[:, 0:1])\
                    .then_inc(S["rstd_ready"], 1)

            act.wait_ge(S["nrm_sum"], 1)
            deviation(0, 3)
            take_cond(0, 4)
            act.dma_start(s0[:, :, :], a["state_gla"][0, 0].rearrange("h k v -> k h v")).then_inc(S["misc_in"], 16)

            def high(n):
                if n >= len(PROJECTIONS):
                    return
                i = GROUPS[PROJECTIONS[n]][3]
                c = slice((n % 4) * P, (n % 4 + 1) * P)
                act.wait_ge(*arrived(i))
                if n >= 4:
                    act.wait_ge(S["proj_ready"], PROJECTIONS[n - 4] + 1)
                raw = ring[DENSE[i][2]][:, :].rearrange("p (k n) -> p k n", k=KT)
                X.activation(w_hi[:, :, c], raw[:, :, c], ACT.Copy).then_inc(S["hi_ready"], 1)

            act.wait_ge(S["lra_in"], 48)
            X.activation(w_lra_hi[:, :, :], w_lra[:, :, :], ACT.Copy).then_inc(S["lra_hi"], 1)
            act.wait_ge(S["mod_ready"], 1)
            for k in range(1, KT, 2):
                act.wait_ge(S["xn_t"], k + 1)
                for g_, c in ((0, slice(0, SEQ)), (1, slice(SEQ, T))):
                    last = X.activation(htmp[k][:, c], bank[3 + k % 5][:, c], ACT.Identity, bias=mod[:, k, g_:g_ + 1],
                                        scale=mod[:, KT + k, g_:g_ + 1])
                    ch.add(last)
                ch.done()
                X.activation(h_hi[:, k, :], htmp[k], ACT.Copy).then_inc(S["h_act"], 1)
            for n in range(3):
                high(n)
            act.dma_start(cv[:, :], a["cache_sb_v"][0, 0].rearrange("s h d -> s (h d)")).then_inc(S["misc_in"], 16)
            act.dma_start(ck[0][:, :], a["cache_sb_k"][0, 0].rearrange("s h d -> s (h d)")[:, 0:512]).then_inc(S["misc_in"], 16)
            act.dma_start(ck[1][:, :], a["cache_sb_k"][0, 0].rearrange("s h d -> s (h d)")[:, 512:D]).then_inc(S["misc_in"], 16)

            def log_gate(t):
                n = TR[t]
                act.wait_ge(S["xla_ps"], t + 1)
                ch.add(X.activation(la[0:n, t, :], bank[3 + t][0:n, :], ACT.Abs))
                ch.done()
                ch.add(X.activation(la[0:n, t, :], la[0:n, t, :], ACT.Exp, scale=-1.0))
                ch.done()
                X.activation(la[0:n, t, :], la[0:n, t, :], ACT.Ln, bias=1.0).then_inc(S["exp_ready"], 1)

            take("lra", 0)
            for i in range(4):
                take("qa", i)
            for t in range(3):
                log_gate(t)
            for i in range(4):
                take("ka", i)
            for i in range(KT):
                take("va", i)
                extras()

            def level_exp(n):
                act.wait_ge(S["dec_ready"], n)
                c = T if n < 7 else SEQ
                X.activation(pd[n % 2][:, :, 0:c], pd[n % 2][:, :, 0:c], ACT.Exp).then_inc(S["exp_ready"], 1)

            second = [("qb", i) for i in range(8)] + [("kb", i) for i in range(8)] + [("vb", i) for i in range(8)]
            for i, (name, j) in enumerate(second):
                take(name, j)
                extras()
                if i % 2 == 1 and i // 2 < LEVELS:
                    level_exp(i // 2 + 1)
                if i == 19:
                    act.wait_ge(S["lev_ps"], LEVELS + 1)
                    for h in range(GH):
                        X.activation(pd[0][:, h, 0:SEQ], bt[:, h, 0:SEQ], ACT.Exp, scale=-1.0, bias=bt[:, h, SEQ - 1:SEQ])
                        X.activation(pd[0][:, h, SEQ:T], bt[:, h, SEQ:T], ACT.Exp, scale=-1.0, bias=bt[:, h, T - 1:T])
                        last = X.activation(pd[1][:, h, 0:DSEQ], bt[:, h, SEQ:T], ACT.Exp)
                    last.then_inc(S["kd_ready"], 1)
            act.wait_ge(S["taken_act"], taken_count(group_index("vbt", 7), "act"))
            act.dma_start(out["sb_v_prompt"][0, 0].rearrange("(t p) h d -> p t (h d)", p=P), vb[:, 0:2, :]).then_inc(S["gla_stored"], 16)
            act.dma_start(out["sb_v_sample"][0, 0].rearrange("s h d -> s (h d)"), vb[0:64, 2, :]).then_inc(S["gla_stored"], 16)
            for p in range(2):
                act.wait_ge(S["st_ready"], p + 1)
                act.dma_start(out["gla_state_prompt"][0, 0].rearrange("h k v -> k h v")[:, 2 * p:2 * p + 2, :],
                              sp_[p][:, :].rearrange("p (h v) -> p h v", h=2)).then_inc(S["gla_stored"], 16)
            for p in range(2):
                act.wait_ge(S["st_ready"], p + 3)
                act.dma_start(out["gla_state_sample"][0, 0].rearrange("h k v -> k h v")[:, 2 * p:2 * p + 2, :],
                              ab[p][:, :].rearrange("p (h v) -> p h v", h=2)).then_inc(S["gla_stored"], 16)
            act.wait_ge(S["nrm_sum"], 2)
            deviation(0, 12)

            def soft(h):
                b = ab[h % 2]
                act.wait_ge(S["z_ready"], h + 1)
                if h >= 2:
                    act.wait_ge(S["sp_ready"], h - 1)
                ch.add(X.activation(b[:, :], bank[5 + h % 3][:, :], ACT.Abs))
                ch.done()
                ch.add(X.activation(b[:, :], b[:, :], ACT.Exp, scale=-1.0))
                ch.done()
                X.activation(b[:, :], b[:, :], ACT.Ln, bias=1.0).then_inc(S["l_ready"], 1)

            def weights(h):
                act.wait_ge(S["rest_ready"], h + 1)
                X.activation(wgt[h % 2][:, :], bank[5 + h % 3][:, :], ACT.Exp).then_inc(S["w_ready"], 1)

            gates = [(n, i) for n in ("ga", "gta", "gtb") for i in range(8)]
            done = 0
            act.wait_ge(S["go_ps"], 6)
            act.wait_ge(S["gla_stored"], 16 * 6)
            for i in range(SH + 1):
                if i < SH:
                    soft(i)
                if i >= 1:
                    weights(i - 1)
                while done < min(len(gates), (i + 1) * 3 // 2):
                    take(*gates[done])
                    extras()
                    done += 1
            assert GROUPS[g[0]][0] == "bb"
            first = PROJECTIONS.index(g[0])
            act.wait_ge(S["proj_ready"], g[0])
            for j in range(KT):
                act.wait_ge(S["o_taken"], j + 1)
                X.activation(ob_hi[:, j, :], obT[:, j, :], ACT.Copy).then_inc(S["ob_hi_ready"], 1)
            high(first + 3)
            act.wait_ge(S["taken_act"], g[0])
            X.activation(gtb[:, :, :], gtb[:, :, :], ACT.Sigmoid).then_inc(S["sig_ready"], 1)
            X.activation(ga[:, :, :], ga[:, :, :], ACT.Silu).then_inc(S["sig_ready"], 1)
            high(first + 4)
            X.activation(gta[:, :, :], gta[:, :, :], ACT.Sigmoid).then_inc(S["sig_ready"], 1)
            for j in range(KT):
                if j >= 2:
                    high(first + 3 + j)
                act.wait_ge(S["oa_ready"], j + 1)
                X.activation(oa_hi[:, j, :], ga[:, j, :], ACT.Copy).then_inc(S["oa_hi_ready"], 1)
            act.wait_ge(S["kb_tok"], 6)
            act.dma_start(out["sb_k_prompt"][0, 0].rearrange("(t p) h d -> p t (h d)", p=P), kbtok[:, 0:2, :]).then_inc(S["stored"], 16)
            act.dma_start(out["sb_k_sample"][0, 0].rearrange("s h d -> s (h d)"), kbtok[0:64, 2, :]).then_inc(S["stored"], 16)
            for j in range(KT):
                high(first + KT + 3 + j)
                if j == 0:
                    act.wait_ge(S["oa_lo_ready"], KT)
                act.wait_ge(S["m_ready"], j + 1)
                X.activation(m_hi[:, j, :], gta[:, j, :], ACT.Copy).then_inc(S["m_hi_ready"], 1)
            for j in range(KT - 3):
                high(first + 2 * KT + 3 + j)

            def modulated(t):
                g_, m = t // 2, TR[t]
                for c in range(2):
                    act.wait_ge(S["norm_t"], 2 * t + c + 1)
                    for j in range(4):
                        k = 4 * c + j
                        last = X.activation(h2T[:, k, TC[t]], bank[NORM_BANKS[t][c]][:, j * P:j * P + m], ACT.Identity,
                                            bias=mod[:, 24 + k, g_:g_ + 1], scale=mod[:, 32 + k, g_:g_ + 1])
                    last.then_inc(S["h2_act"], 1)

            def modulated_rows(n):
                t, c = divmod(n, 2)
                act.wait_ge(S["hb_t"], n + 1)
                X.activation(hf[0:TR[t], t, c * 512:c * 512 + 512], bank[5 + n % 3][0:TR[t], :], ACT.Copy)\
                    .then_inc(S["hb_ready"], 1)

            for n, i in enumerate(NORM_ORDER):
                act.wait_ge(S["nrm_sum"], 3 + n)
                deviation(i, 1)
                if i == 4:
                    modulated(0)
            modulated_rows(0)
            modulated_rows(1)
            modulated(1)
            for n in range(2, 6):
                modulated_rows(n)

            act.wait_ge(S["ex_in"], 1)
            X.activation(r4[1][:, :, :], r4[0][:, :, :], ACT.Exp).then_inc(S["ex_out"], 1)
            act.wait_ge(S["ex_in"], 2)
            X.activation(r1[:, 5, :], r1[:, 4, :], ACT.Exp).then_inc(S["ex_out"], 1)

            def rows_of(n):
                act.wait_ge(S["gather_ps"], n + 1)
                X.activation(xrow[:, :], bank[0][:, :], ACT.Copy).then_inc(S["xrow_ready"], 1)

            def silu(n):
                act.wait_ge(S["gu_ps"], n + 1)
                X.activation(gs[SLOTS:P, :], bank[1][0:SLOTS, :], ACT.Silu).then_inc(S["gs_ready"], 1)

            def rows_out(n, b, before):
                act.wait_ge(S["down_ps"], n + 1)
                if before is not None:
                    act.wait_ge(S[f"scattered{b}"], before * 16)
                X.activation(ystage[b][:, :], bank[3][:, :], ACT.Copy).then_inc(S["ys_ready"], 1)

            def step(n, b, before):
                silu(n)
                rows_of(n + 1)
                rows_out(n, b, before)

            rows_of(0)
            for e in range(3):
                step(e, e, None)
            with act.Fori(0, (E - 4) // 3) as it:
                for r in range(3, 6):
                    step(it * 3 + r, r % 3, it + 1)
            for e in range(3 + (E - 4) // 3 * 3, E - 1):
                step(e, e % 3, e // 3)
            silu(E - 1)
            rows_out(E - 1, (E - 1) % 3, (E - 1) // 3)
            act.wait_ge(S["plan_ready"], 1)
            n_over = act.value_load(plan_i[0:1, 2 * OVER:2 * OVER + 1], min_val=0, max_val=OVER)
            with act.If(n_over > 0):
                with act.Fori(0, n_over) as i:
                    rows_of(i + E)
                    silu(i + E)
                    rows_out(i + E, 0, i + USES[0])
                act.nop()
            with act.Else():
                act.nop()
            for t in range(3):
                m = TR[t]
                act.wait_ge(S[f"comb_in{t}"], 16)
                for k in range(2 if t == 1 else 1):
                    y = comb[t][0:m, k * D:k * D + D]
                    X.activation(y, y, ACT.Copy, scale=wts[0:m, k, t:t + 1]).then_inc(S["weighted"], 1)
            for i, t in enumerate(LAST_ORDER):
                act.wait_ge(S["nrm_sum"], 9 + i)
                deviation(t, 1)
            for i, t in enumerate(LAST_ORDER):
                act.wait_ge(S["fin_ready"], i + 1)
                dst = out["y_prompt"][0][t * P:t * P + P, :] if t < 2 else out["y_sample"][0]
                act.dma_start(dst, x1[0:TR[t], t, :]).then_inc(S["stored"], 16)
            act.wait_ge(S["stored"], 16 * 5)

        @block.tensor
        def _(pe):
            mm = nc.tensor.matmul
            cur = [0]

            def chunk():
                while DENSE[cur[0]][0] != "cond":
                    cur[0] += 1
                i = cur[0]
                pe.wait_ge(*arrived(i))
                cur[0] += 1
                return (cond_slot if DENSE[i][2] == COND_SLOT else ring[DENSE[i][2]])[:, :].rearrange("p (k n) -> p k n", k=KT)

            pe.wait_ge(S["const_ready"], 1)
            pe.wait_ge(S["rows_in"], 64)
            nc.tensor.transpose(bank[7][:, 0:72], rows[0:72, :], ident[0:72, 0:72]).then_inc(S["cols_t"], 1)

            g = [0]

            def free_bank():
                n = g[0]
                if n >= PROJ_BANKS:
                    who = GROUPS[n - PROJ_BANKS][2]
                    pe.wait_ge(S["taken_act" if who == "act" else "taken_dve"], taken_count(n - PROJ_BANKS, who))
                return bank[n % PROJ_BANKS]

            def close(ins):
                g[0] += 1
                ins.then_inc(S["proj_ready"], 1)

            def cond_rows():
                w = chunk()
                b = free_bank()
                for k in range(KT):
                    for m in range(4):
                        last = mm(b[32 * m:32 * m + 32, 0:P], silu_c[:, k, :], w[:, k, m * P:m * P + P], start=(k == 0),
                                  stop=(k == KT - 1), skip_group_check=True)
                close(last)

            def cond_turn():
                n = max(i for i in range(g[0]) if GROUPS[i][0] == "cr")
                pe.wait_ge(S["taken_act"], taken_count(n, "act"))
                b = free_bank()
                close(nc.tensor.transpose(b[:, 0:P], crow[:, :], ident[:, :]))

            def extras():
                while GROUPS[g[0]][0] in EXTRA:
                    name, i = GROUPS[g[0]][:2]
                    {"cr": cond_rows, "ct": cond_turn}.get(name, lambda: value_turn(name, i))()

            def value_turn(name, i):
                pe.wait_ge(S["taken_act"], taken_count(group_index(name[:2], i), "act"))
                b = free_bank()
                for t in range(3):
                    last = nc.tensor.transpose(b[0:TR[t], t * P:t * P + P], vtmp[i % 2][:, TC[t]], ident[:, :])
                close(last)

            pe.wait_ge(S["silu_ready"], 1)
            for c in range(4):
                cond_rows()
                cond_turn()
            pe.wait_ge(S["xn_ready"], 3)
            for k in range(KT):
                b = bank[3 + k % 5]
                if k >= 5:
                    pe.wait_ge(S["h_act" if (k - 5) % 2 else "h_dve"], (k - 5) // 2 + 1)
                for t in range(3):
                    n = TR[t]
                    last = nc.tensor.transpose(b[:, TC[t]], xn[0:n, t, k * P:k * P + P], ident[0:n, 0:n])
                last.then_inc(S["xn_t"], 1)

            def three(b, c, hi, lo, x_hi, x_lo):
                for k in range(KT):
                    mm(b, hi[:, k, c], x_hi[:, k, :], start=(k == 0), stop=False)
                    mm(b, hi[:, k, c], x_lo[:, k, :], start=False, stop=False)
                    last = mm(b, lo[:, k, c], x_hi[:, k, :], start=False, stop=(k == KT - 1))
                return last

            def feat(x_hi, x_lo):
                n = PROJECTIONS.index(g[0])
                b = free_bank()
                pe.wait_ge(S["lo_ready"], n + 1)
                close(three(b[:, 0:T], slice((n % 4) * P, (n % 4 + 1) * P), w_hi, w_lo[DENSE[GROUPS[g[0]][3]][2]], x_hi, x_lo))

            pe.wait_ge(S["h_dve"], KT // 2)
            pe.wait_ge(S["h_pool"], KT // 2)
            pe.wait_ge(S["lra_lo"], 1)
            b = free_bank()
            close(three(b[0:RANK, 0:T], slice(0, RANK), w_lra_hi, w_lra_lo, h_hi, h_lo1))
            for i in range(4):
                feat(h_hi, h_lo1)
            pe.wait_ge(S["taken_act"], taken_count(group_index("lra", 0), "act"))
            pe.wait_ge(S["const_ready"], 2)
            for t in range(3):
                mm(bank[3 + t][0:TR[t], :], lraT[0:RANK + 1, TC[t]], wa2[0:RANK + 1, :], start=True, stop=True)\
                    .then_inc(S["xla_ps"], 1)
            for i in range(4):
                feat(h_hi, h_lo1)
            for i in range(4):
                feat(h_hi, h_lo1)
                extras()
            pe.wait_ge(S["la_ready"], 3)
            for h in range(GH):
                b = bank[3 + h]
                hs = slice(h * DK, h * DK + DK)
                mm(b[:, 0:SEQ], la[:, 0, hs], tri_tau[:, :], start=True, stop=False, skip_group_check=True)
                mm(b[:, 128:SEQ], la[:, 1, hs], tri_tau[:, 0:P], start=False, stop=True, skip_group_check=True)
                mm(b[:, SEQ:T], la[0:64, 2, hs], tri_tau[0:64, 0:64], start=False, stop=True, skip_group_check=True)\
                    .then_inc(S["b_ps"], 1)
            for i in range(4):
                feat(h_hi, h_lo1)
                extras()

            def level(n):
                lhs, rhs = (ka, qa) if n == 0 else (pd[n % 2], pd[n % 2])
                if n:
                    pe.wait_ge(S["pd_ready"], n)
                else:
                    pe.wait_ge(S["b_ready"], 1)
                if n == LEVELS:
                    for h in range(GH):
                        last = mm(bank[6][:, h * P:h * P + P], lhs[:, h, TC[0]], rhs[:, h, TC[1]], start=True, stop=True)
                    last.then_inc(S["lev_ps"], 1)
                    return
                if n:
                    pe.wait_ge(S["lev_taken"], n)
                for h in range(GH):
                    for t in range(2):
                        last = mm(bank[3 + t][:, h * P:h * P + P], lhs[:, h, TC[t]], rhs[:, h, TC[t]], start=True, stop=True)
                    if n < 7:
                        last = mm(bank[5][0:64, h * 64:h * 64 + 64], lhs[:, h, SEQ:T], rhs[:, h, SEQ:T], start=True, stop=True)
                last.then_inc(S["lev_ps"], 1)

            def second(i):
                feat(h_hi, h_lo1)
                extras()

            for i in range(24):
                second(i)
                if i % 2 == 1 and i // 2 <= LEVELS:
                    level(i // 2)
            pe.wait_ge(S["ke_ready"], 1)
            pe.wait_ge(S["lev_taken"], LEVELS + 1)
            for t in range(3):
                n = TR[t]
                for h in range(GH):
                    last = nc.tensor.transpose(bank[3 + t][0:n, h * P:h * P + P], ke[:, h, TC[t]], ident[:, :])
                last.then_inc(S["ke_t"], 1)
            pe.wait_ge(S["misc_in"], 64)
            for j in range(KT):
                last = nc.tensor.transpose(bank[6 + j // 4][:, (j % 4) * P:(j % 4 + 1) * P],
                                           ck[j // 4][:, (j % 4) * P:(j % 4 + 1) * P], ident[:, :])
            last.then_inc(S["ck_t"], 1)
            pe.wait_ge(S["ket_ready"], 3)
            pe.wait_ge(S["ck_ready"], 2)
            for p in range(2):
                b = bank[6 + p]
                for h in (2 * p, 2 * p + 1):
                    c = slice((h % 2) * DV, (h % 2 + 1) * DV)
                    hv = slice(h * DV, h * DV + DV)
                    for t in range(2):
                        last = mm(b[:, c], ket[:, t, h * DK:h * DK + DK], va[:, t, hv], start=(t == 0), stop=(t == 1))
                last.then_inc(S["st_ps"], 1)
            for p in range(2):
                b = bank[3 + p]
                for h in (2 * p, 2 * p + 1):
                    c = slice((h % 2) * DV, (h % 2 + 1) * DV)
                    last = mm(b[:, c], ket[0:64, 2, h * DK:h * DK + DK], va[0:64, 2, h * DV:h * DV + DV], start=True, stop=True)
                last.then_inc(S["st_ps"], 1)
            pe.wait_ge(S["lev_added"], LEVELS - 1)
            pe.wait_ge(S["qe_ready"], 1)
            for n in range(6):
                t, p = divmod(n, 2)
                b = bank[5 + n % 3]
                if n == 1:
                    pe.wait_ge(S["st_ready"], 1)
                elif n == 2:
                    pe.wait_ge(S["st_ready"], 2)
                elif n >= 3:
                    pe.wait_ge(S["go_ready"], n - 2)
                for h in (2 * p, 2 * p + 1):
                    c = slice((h % 2) * DV, (h % 2 + 1) * DV)
                    hv = slice(h * DV, h * DV + DV)
                    if t == 0:
                        last = mm(b[:, c], acc[:, 0, h, :], va[:, 0, hv], start=True, stop=True)
                    elif t == 1:
                        mm(b[:, c], cross[:, h, :], va[:, 0, hv], start=True, stop=False)
                        last = mm(b[:, c], acc[:, 1, h, :], va[:, 1, hv], start=False, stop=True)
                    else:
                        mm(b[0:64, c], acc[0:64, 2, h, 0:64], va[0:64, 2, hv], start=True, stop=False)
                        last = mm(b[0:64, c], pd[1][:, h, 0:DSEQ], s0[:, h, :], start=False, stop=True)
                last.then_inc(S["go_ps"], 1)

            def scores(h):
                z, j, r = bank[5 + h % 3], h // 2, slice(64 * (h % 2), 64 * (h % 2) + 64)
                if h < 3:
                    pe.wait_ge(S["go_ready"], 6)
                else:
                    pe.wait_ge(S["w_ready"], h - 2)
                mm(z[:, :], ident_b[:, :], mask_sb[:, :], start=True, stop=False, skip_group_check=True)
                mm(z[:, 0:256], kb[r, j, 0:128], qb[r, j, 0:256], start=False, stop=False, skip_group_check=True)
                mm(z[:, 256:384], kb[r, j, 128:256], qb[r, j, 128:256], start=False, stop=False, skip_group_check=True)
                mm(z[:, 384:448], ckT[r, j, :], qb[r, j, SEQ:T], start=False, stop=False, skip_group_check=True)
                mm(z[:, 448:512], kb[r, j, SEQ:T + 64], qb[r, j, SEQ:T], start=False, stop=True, skip_group_check=True)\
                    .then_inc(S["z_ready"], 1)

            def rest(h):
                z, s = bank[5 + h % 3], (sp_hi[h % 2], sp_lo[h % 2])
                pe.wait_ge(S["sp_ready"], h + 1)
                for part in s:
                    mm(z[:, :], tri_r[:, :], part[:, :], start=False, stop=False, skip_group_check=True)
                for i, part in enumerate(s):
                    mm(z[:, 128:256], ones_r[:, :], part[:, 256:384], start=False, stop=False, skip_group_check=True)
                    last = mm(z[:, 384:448], ones_r[:, :], part[:, 448:512], start=False, stop=(i == 1), skip_group_check=True)
                last.then_inc(S["rest_ready"], 1)

            def attend(h):
                j, r, w = h // 2, slice(64 * (h % 2), 64 * (h % 2) + 64), wgt[h % 2]
                b, hd = bank[3 + j % 2], slice(h * SD, h * SD + SD)
                pe.wait_ge(S["w_ready"], h + 1)
                if h < 4:
                    pe.wait_ge(S["st_ready"], 4)
                elif h % 2 == 0:
                    pe.wait_ge(S["o_taken"], j - 1)
                mm(b[r, 0:256], vb[:, 0, hd], w[:, 0:256], start=True, stop=False, skip_group_check=True)
                mm(b[r, 128:256], vb[:, 1, hd], w[:, 256:384], start=False, stop=True, skip_group_check=True)
                mm(b[r, 256:T], cv[:, hd], w[:, 384:448], start=False, stop=False, skip_group_check=True)
                last = mm(b[r, 256:T], vb[0:64, 2, hd], w[0:64, 448:512], start=False, stop=True, skip_group_check=True)
                if h % 2:
                    last.then_inc(S["o_ready"], 1)

            done = 0
            pe.wait_ge(S["h_moved"], 1)
            for i in range(SH + 2):
                if i < SH:
                    scores(i)
                if 1 <= i <= SH:
                    rest(i - 1)
                if i >= 2:
                    attend(i - 2)
                while done < min(24, (i + 1) * 3 // 2):
                    feat(h_hi, h_lo2)
                    extras()
                    done += 1
            def turn_keys(n):
                t, c = divmod(n, 2)
                b = bank[5 + n % 3]
                if n >= 3:
                    pe.wait_ge(S["kb_tok"], n - 2)
                elif n == 0:
                    pe.wait_ge(S["w_ready"], SH)
                for j in range(4):
                    last = nc.tensor.transpose(b[0:TR[t], j * P:j * P + P], kb[:, 4 * c + j, TC[t]], ident[:, :])
                last.then_inc(S["kb_t"], 1)

            for n in range(3):
                turn_keys(n)
            pe.wait_ge(S["ob_lo_ready"], KT)
            for i in range(KT):
                feat(ob_hi, ob_lo)
                if i == 0:
                    for n in range(3, 6):
                        turn_keys(n)
                if i % 2:
                    pe.wait_ge(S["gfr_in"], i // 2 + 1)
                    if i == 1:
                        pe.wait_ge(S["kb_tok"], 6)
                    else:
                        pe.wait_ge(S["gf_ready"], i // 2)
                    mm(bank[5][:, :], ones[:, :], diag[:, :], start=True, stop=True).then_inc(S["gfr_ps"], 1)
                if i == 0:
                    pe.wait_ge(S["on_ready"], 1)
                if i >= 2:
                    pe.wait_ge(S["oa_ready"], i - 1)
                else:
                    pe.wait_ge(S["o_taken"], KT)
                for t in range(3):
                    n = TR[t]
                    last = nc.tensor.transpose(bank[3 + i % 2][:, TC[t]], on[0:n, t, i * P:i * P + P], ident[0:n, 0:n])
                last.then_inc(S["on_t"], 1)
            pe.wait_ge(S["gf_ready"], 4)
            pe.wait_ge(S["oa_lo_ready"], KT)
            for i in range(KT):
                feat(oa_hi, oa_lo)
            pe.wait_ge(S["m_lo_ready"], KT)
            for i in range(KT):
                feat(m_hi, m_lo)
            for n in range(6):
                t, c = divmod(n, 2)
                b = bank[5 + n % 3]
                pe.wait_ge(S["taken_dve"], 2 * KT + 4 * c + 4)
                if n >= 3:
                    pe.wait_ge(S["gm_added"], n - 2)
                for j in range(4):
                    last = nc.tensor.transpose(b[0:TR[t], j * P:j * P + P], gmT[:, 4 * c + j, TC[t]], ident[:, :])
                last.then_inc(S["gm_t"], 1)
            def turn_modulated(n):
                t, c = divmod(n, 2)
                b = bank[5 + n % 3]
                if n >= 3:
                    pe.wait_ge(S["hb_ready"], n - 2)
                for j in range(4):
                    last = nc.tensor.transpose(b[0:TR[t], j * P:j * P + P], h2T[:, 4 * c + j, TC[t]], ident[:, :])
                last.then_inc(S["hb_t"], 1)

            def turn_norm(t):
                m = TR[t]
                pe.wait_ge(S["norm_ready"], t + 1)
                if t == 2:
                    pe.wait_ge(S["h2_act"], 2)
                for c in range(2):
                    for j in range(4):
                        k = 4 * c + j
                        last = nc.tensor.transpose(bank[NORM_BANKS[t][c]][:, j * P:j * P + m],
                                                   x2n[0:m, t, k * P:k * P + P], ident[0:m, 0:m])
                    last.then_inc(S["norm_t"], 1)

            def logits(t):
                for k in range(KT):
                    last = mm(bank[0][0:NG + E, TC[t]], w_route[:, k, :], h2T[:, k, TC[t]], start=(k == 0),
                              stop=(k == KT - 1), skip_group_check=True)
                return last

            pe.wait_ge(S["x1_in"], 96)
            turn_norm(0)
            pe.wait_ge(S["h2_act"], 2)
            logits(0)
            pe.wait_ge(S["gm_added"], 6)
            turn_modulated(0)
            turn_modulated(1)
            turn_norm(1)
            turn_norm(2)
            pe.wait_ge(S["h2_act"], 4)
            logits(1)
            pe.wait_ge(S["h2_dve"], 2)
            logits(2).then_inc(S["lgt_ps"], 1)
            turn_modulated(2)
            pe.wait_ge(S["lgt_ready"], 1)
            for t in range(3):
                nc.tensor.transpose(bank[1][0:TR[t], 40 * t:40 * t + NG + E], lgT[:, TC[t]], ident[0:NG + E, 0:NG + E])\
                    .then_inc(S["lg_ps"], 1)
            for n in range(3, 6):
                turn_modulated(n)
            pe.wait_ge(S["rank_in"], 1)
            for t in range(3):
                r = bank[1][:, E * t:E * t + E]
                for u in range(t):
                    mm(r, ones_b[:, :], chosen[:, u, :], start=(u == 0), stop=False)
                mm(r, tri_b[:, :], chosen[:, t, :], start=(t == 0), stop=True)
            for t in range(3):
                last = mm(bank[1][:, 128:129], rep[:, t, :, :].rearrange("p j e -> p (j e)"),
                          ones_b[:, 0:1], start=(t == 0), stop=(t == 2))
            last.then_inc(S["rank_ps"], 1)
            pe.wait_ge(S["flag_ready"], 1)
            mm(bank[4][:, 0:1], tri_strict[:, :], flags[:, 0:1], start=True, stop=True).then_inc(S["xr_ps"], 1)

            def gather(n):
                pe.wait_ge(S["onehot_ready"], n + 1)
                for t in range(3):
                    m = TR[t]
                    for c in range(2):
                        last = mm(bank[0][64 * c:64 * c + 64, :], onehot[0:m, t, :], hf[0:m, t, c * CB:c * CB + CB],
                           start=(t == 0), stop=(t == 2), skip_group_check=True)
                last.then_inc(S["gather_ps"], 1)
                for t in range(3):
                    m = TR[t]
                    for c in range(2):
                        last = mm(bank[5][64 * c:64 * c + 64, 0:1], onehot[0:m, t, :], vcol[0:m, t:t + 1],
                                  start=(t == 0), stop=(t == 2), skip_group_check=True)
                last.then_inc(S["index_ps"], 1)

            def turn_rows(n):
                pe.wait_ge(S["xrow_ready"], n + 1)
                if not isinstance(n, int):
                    pe.sem_inc(S["pe_passed"], 1)
                for q in range(4):
                    last = nc.tensor.transpose(bank[2][:, q * P:q * P + P], xrow[:, q * P:q * P + P], ident[:, :])
                last.then_inc(S["xg_t"], 1)

            def gate_up(n, s, turn):
                pe.wait_ge(S["xg_ready"], n + 1)
                pe.wait_ge(chunk_in[s], turn(s))
                pe.wait_ge(chunk_in[s + 1], turn(s + 1))
                for k in range(KT):
                    for q in range(2):
                        last = mm(bank[1][64 * q:64 * q + 64, :], xg[:, k % 4, k // 4, :],
                                  ring[s + q][:, k * FF:k * FF + FF], start=(k == 0), stop=(k == KT - 1),
                                  skip_group_check=True)
                last.then_inc(S["gu_ps"], 1)

            def turn_hidden(n):
                pe.wait_ge(S["hrow_ready"], n + 1)
                if not isinstance(n, int):
                    pe.sem_inc(S["pe_passed"], 1)
                for f in range(FT):
                    last = nc.tensor.transpose(bank[6][:, f * SLOTS:(f + 1) * SLOTS], gs[0:SLOTS, f * P:f * P + P],
                                               ident[0:SLOTS, 0:SLOTS])
                last.then_inc(S["he_t"], 1)

            def down(n, s, turn):
                pe.wait_ge(S["he_ready"], n + 1)
                pe.wait_ge(chunk_in[s + 2], turn(s + 2))
                if not isinstance(n, int) or n:
                    pe.wait_ge(S["ys_ready"], n)
                for f in range(FT):
                    for c in range(2):
                        last = mm(bank[3][64 * c:64 * c + 64, :], he[:, f, :],
                                  ring[s + 2][:, f * D + c * CB:f * D + c * CB + CB], start=(f == 0),
                                  stop=(f == FT - 1), skip_group_check=True)
                last.then_inc(S["down_ps"], 1)

            def step(e, s, use):
                gate_up(e, s, use)
                gather(e + 1)
                turn_hidden(e)
                turn_rows(e + 1)
                down(e, s, use)

            pe.wait_ge(S["hb_ready"], 6)
            gather(0)
            pe.wait_ge(S["pick_ready"], 1)
            mm(bank[4][:, 64:64 + OVER], q_rep[:, :], pick[:, :], start=True, stop=True)
            mm(bank[4][0:1, 96:96 + OVER], q_iota[:, 0:1], pick[:, :], start=True, stop=True)
            mm(bank[4][0:1, 128:129], flags[:, 0:1], ones[:, 0:1], start=True, stop=True).then_inc(S["plan_ps"], 1)
            turn_rows(0)
            step(0, 0, lambda s: expert_use(s, 0))
            with pe.Fori(0, (E - 2) // 3) as it:
                for r in range(1, 4):
                    step(it * 3 + r, base(r), lambda s, r=r: it * 16 + expert_use(s, r // 3))
            last_use = lambda s: expert_use(s, (E - 1) // 3)
            pe.wait_ge(S["plan_ready"], 1)
            gate_up(E - 1, base(E - 1), last_use)
            turn_hidden(E - 1)
            down(E - 1, base(E - 1), last_use)
            n_over = pe.value_load(plan_i[0:1, 2 * OVER:2 * OVER + 1], min_val=0, max_val=OVER)
            with pe.If(n_over > 0):
                with pe.Fori(0, n_over) as i:
                    use = lambda s: i * 16 + expert_use(s, len(range(0, E, 3)))
                    gather(i + E)
                    turn_rows(i + E)
                    gate_up(i + E, 0, use)
                    turn_hidden(i + E)
                    down(i + E, 0, use)
                pe.nop()
            with pe.Else():
                pe.nop()

        @block.vector
        def _(dve):
            V = nc.vector
            ch = Chain(dve, S["dve_chain"])

            def tile_stats(i0, src, n):
                for c in range(2):
                    ch.add(V.bn_stats(stats[0:n, i0, 6 * c:6 * c + 6], src[:, c * 512:c * 512 + 512]))
                ch.done()
                return V.bn_aggr(mv[0:n, i0, :], stats[0:n, i0, :])

            def reciprocal(n, i0, count):
                r, q, h = (a_[:, i0:i0 + count] for a_ in (rstd, newton, half_var))
                dve.wait_ge(S["rstd_ready"], n)
                ch.add(V.tensor_scalar(h, mv[:, i0:i0 + count, 1], EPS, -0.5, ALU.add, ALU.mult))
                ch.add(V.reciprocal(r, r))
                ch.done()
                if count == 1:
                    ch.add(V.tensor_scalar(q, r, r, h, ALU.mult, ALU.mult))
                else:
                    ch.add(V.tensor_tensor(q, r, r, ALU.mult))
                    ch.done()
                    ch.add(V.tensor_tensor(q, q, h, ALU.mult))
                ch.done()
                ch.add(V.scalar_tensor_tensor(out=r, in0=q, scalar=1.5, in1=r, op0=ALU.add, op1=ALU.mult))
                ch.done()

            dve.wait_ge(S["const_ready"], 1)
            dve.wait_ge(S["x_in"], 32)
            for t in range(3):
                last = tile_stats(t, xt[0:TR[t], t, :], TR[t])
            last.then_inc(S["nrm_sum"], 1)
            dve.wait_ge(S["silu_ready"], 1)
            ch.add(V.tensor_copy(cols[:, :], bank[7][:, 0:72]))
            reciprocal(1, 0, 3)
            for t in range(3):
                n = TR[t]
                V.tensor_scalar(xn[0:n, t, :], xt[0:n, t, :], mv[0:n, t, 0:1], rstd[0:n, t:t + 1], ALU.subtract,
                                ALU.mult).then_inc(S["xn_ready"], 1)

            def take_mod(first, n):
                ch.done()
                for g_ in range(2):
                    ch.add(V.tensor_tensor(mod[:, first:first + n, g_], mod[:, first:first + n, g_],
                                           cols[:, 16 + first:16 + first + n], ALU.add))
                ch.done()
                s = 8 if first == 0 else 32
                V.tensor_scalar(mod[:, s:s + 8, :], mod[:, s:s + 8, :], 1.0, None, ALU.add).then_inc(S["mod_ready"], 1)

            dve.wait_ge(S["taken_act"], taken_count(group_index("ct", 3), "act"))
            take_mod(0, 16)
            dve.wait_ge(S["mod_ready"], 1)
            for k in range(0, KT, 2):
                dve.wait_ge(S["xn_t"], k + 1)
                for g_, c in ((0, slice(0, SEQ)), (1, slice(SEQ, T))):
                    ch.add(V.tensor_scalar(htmp[k][:, c], bank[3 + k % 5][:, c], mod[:, KT + k, g_:g_ + 1],
                                           mod[:, k, g_:g_ + 1], ALU.mult, ALU.add))
                ch.done()
                ch.add(V.tensor_copy(h_hi[:, k, :], htmp[k]))
                ch.done()
                V.tensor_tensor(h_lo1[:, k, :], htmp[k], h_hi[:, k, :].bitcast(F32), ALU.subtract).then_inc(S["h_dve"], 1)
            for t in range(3):
                n = TR[t]
                dve.wait_ge(S["exp_ready"], t + 1)
                V.scalar_tensor_tensor(out=la[0:n, t, :], in0=bank[3 + t][0:n, :], scalar=0.0, in1=la[0:n, t, :],
                                       op0=ALU.min, op1=ALU.subtract).then_inc(S["la_ready"], 1)
            dve.wait_ge(S["b_ps"], GH)
            for h in range(GH):
                last = V.tensor_copy(bt[:, h, :], bank[3 + h][:, 0:T])
            last.then_inc(S["b_ready"], 1)

            def halves(t, n):
                size = 2 ** n
                if n < 7:
                    v = t[:, :, :].rearrange("p h t -> p (h t)").rearrange("p (b c) -> p b c", c=size)
                    return v[:, :, 0:size // 2], v[:, :, size // 2:size], v[:, :, size // 2 - 1:size // 2]
                v = t[:, :, 0:SEQ].rearrange("p h (b c) -> p h b c", c=size)
                return v[:, :, :, 0:size // 2], v[:, :, :, size // 2:size], v[:, :, :, size // 2 - 1:size // 2]

            def log_decay(n):
                bl, br, mid = halves(bt, n)
                dl, dr, _ = halves(pd[n % 2], n)
                if n >= 3:
                    dve.wait_ge(S["lev_ps"], n - 1)
                V.tensor_tensor(dl, mid.to_broadcast(list(bl.shape)), bl, ALU.subtract)
                V.tensor_tensor(dr, br, mid.to_broadcast(list(br.shape)), ALU.subtract).then_inc(S["dec_ready"], 1)

            def decayed(n):
                dl, dr, _ = halves(pd[n % 2], n)
                dve.wait_ge(S["exp_ready"], 3 + n)
                V.tensor_tensor(dl, dl, halves(ka, n)[0], ALU.mult)
                V.tensor_tensor(dr, dr, halves(qa, n)[1], ALU.mult).then_inc(S["pd_ready"], 1)

            def masked(n):
                dve.wait_ge(S["lev_ps"], n + 1)
                if n == LEVELS:
                    V.tensor_copy(cross[:, :, :].rearrange("p h t -> p (h t)"), bank[6][:, :]).then_inc(S["lev_taken"], 1)
                    return
                if n >= 2:
                    dve.wait_ge(S["lev_added"], n - 1)
                mask = levels[:, n, :].unsqueeze(1)
                for t in range(2):
                    dst = acc[:, t, :, :] if n == 0 else mtmp[:, t, :].rearrange("p (h t) -> p h t", h=GH)
                    last = V.tensor_tensor(dst, bank[3 + t][:, :].rearrange("p (h t) -> p h t", h=GH),
                                           mask.to_broadcast([P, GH, P]), ALU.mult)
                if n < 7:
                    dst = acc[0:64, 2, :, 0:64] if n == 0 else mtmp_s[:, :, :]
                    last = V.tensor_tensor(dst, bank[5][0:64, 0:256].rearrange("p (h t) -> p h t", h=GH),
                                           levels[0:64, n, 0:64].unsqueeze(1).to_broadcast([64, GH, 64]), ALU.mult)
                last.then_inc(S["lev_taken"], 1)

            dve.wait_ge(S["const_ready"], 2)
            dve.wait_ge(S["b_ready"], 1)
            dve.wait_ge(S["taken_act"], taken_count(group_index("ka", 3), "act"))
            log_decay(1)
            log_decay(2)
            decayed(1)
            masked(0)
            for n in range(2, LEVELS + 1):
                decayed(n)
                masked(n - 1)
                if n < LEVELS:
                    log_decay(n + 1)
            masked(LEVELS)
            dve.wait_ge(S["kd_ready"], 1)
            V.tensor_tensor(ke[:, :, :], ke[:, :, :], ka[:, :, :], ALU.mult).then_inc(S["ke_ready"], 1)
            ch.add(V.tensor_copy(total[:, :], pd[1][:, :, DSEQ - 1]))
            ch.done()
            V.tensor_tensor(pd[1][:, :, 0:DSEQ], pd[1][:, :, 0:DSEQ], qa[:, :, SEQ:T], ALU.mult).then_inc(S["qe_ready"], 1)
            for t in range(3):
                dve.wait_ge(S["ke_t"], t + 1)
                V.tensor_copy(ket[0:TR[t], t, :], bank[3 + t][0:TR[t], :]).then_inc(S["ket_ready"], 1)
            dve.wait_ge(S["ck_t"], 1)
            for c in range(2):
                V.tensor_copy(ckT[:, 4 * c:4 * c + 4, :].rearrange("p k s -> p (k s)"), bank[6 + c][:, :]).then_inc(S["ck_ready"], 1)
            for p in range(2):
                dve.wait_ge(S["st_ps"], p + 1)
                V.tensor_copy(sp_[p][:, :], bank[6 + p][:, :]).then_inc(S["st_ready"], 1)
            for p in range(2):
                dve.wait_ge(S["st_ps"], 3 + p)
                for h in (2 * p, 2 * p + 1):
                    last = V.scalar_tensor_tensor(out=ab[p][:, (h % 2) * DV:(h % 2 + 1) * DV], in0=s0[:, h, :], scalar=total[:, h:h + 1],
                                                  in1=bank[3 + p][:, (h % 2) * DV:(h % 2 + 1) * DV], op0=ALU.mult, op1=ALU.add)
                last.then_inc(S["st_ready"], 1)
            for n in range(6):
                t, p = divmod(n, 2)
                m = TR[t]
                dve.wait_ge(S["go_ps"], n + 1)
                V.tensor_copy(on[0:m, t, p * 512:p * 512 + 512], bank[5 + n % 3][0:m, :])
                for h in range(2):
                    ins = V.bn_stats(stats[0:m, 4 * t + 2 * p + h, 0:6], bank[5 + n % 3][0:m, h * DV:h * DV + DV])
                ins.then_inc(S["go_ready"], 1)
            V.tensor_copy(tri_r[:, :], neg_tri[:, :])
            V.tensor_copy(ones_r[:, :], neg_ones[:, :])
            V.tensor_copy(h_lo2[:, :, :], h_lo1[:, :, :]).then_inc(S["h_moved"], 1)
            dve.wait_ge(S["go_ready"], 6)
            ch.done()
            for i in range(12):
                m = TR[i // 4]
                ch.add(V.bn_aggr(mv[0:m, i, :], stats[0:m, i, 0:6]))
            ch.done()
            ch.add(V.tensor_tensor(mv[:, :, 0], mv[:, :, 0], mv[:, :, 0], ALU.mult))
            ch.done()
            V.tensor_tensor(mv[:, :, 1], mv[:, :, 1], mv[:, :, 0], ALU.add).then_inc(S["nrm_sum"], 1)

            def soft_sum(h):
                dve.wait_ge(S["l_ready"], h + 1)
                if h >= 2:
                    dve.wait_ge(S["rest_ready"], h - 1)
                sp, hi = sp_[h % 2][:, :], sp_hi[h % 2][:, :]
                ch.add(V.scalar_tensor_tensor(out=sp, in0=bank[5 + h % 3][:, :], scalar=0.0, in1=ab[h % 2][:, :],
                                              op0=ALU.max, op1=ALU.add))
                ch.done()
                ch.add(V.tensor_copy(hi, sp))
                ch.done()
                V.tensor_tensor(sp_lo[h % 2][:, :], sp, hi.bitcast(F32), ALU.subtract).then_inc(S["sp_ready"], 1)

            def take_o(j):
                dve.wait_ge(S["o_ready"], j + 1)
                V.tensor_copy(obT[:, j, :], bank[3 + j % 2][:, 0:T]).then_inc(S["o_taken"], 1)

            dve.wait_ge(S["gla_stored"], 16 * 6)
            dve.wait_ge(S["ck_ready"], 2)
            for i in range(SH + 2):
                if i < SH:
                    soft_sum(i)
                if i == 2:
                    reciprocal(2, 0, 12)
                    for n in range(12):
                        t, h = divmod(n, GH)
                        m = TR[t]
                        v = on[0:m, t, h * DV:h * DV + DV]
                        last = V.tensor_scalar(v, v, rstd[0:m, n:n + 1], None, ALU.mult)
                    last.then_inc(S["on_ready"], 1)
                if i >= 3 and i % 2 == 1:
                    take_o((i - 3) // 2)
            def take_keys(n):
                t, c = divmod(n, 2)
                dve.wait_ge(S["kb_t"], n + 1)
                V.tensor_copy(kbtok[0:TR[t], t, c * 512:c * 512 + 512], bank[5 + n % 3][0:TR[t], :]).then_inc(S["kb_tok"], 1)

            take_keys(0)
            for j in range(KT):
                dve.wait_ge(S["ob_hi_ready"], j + 1)
                V.tensor_tensor(ob_lo[:, j, :], obT[:, j, :], ob_hi[:, j, :].bitcast(F32), ALU.subtract)\
                    .then_inc(S["ob_lo_ready"], 1)

            for n in range(1, 6):
                take_keys(n)
            dve.wait_ge(S["taken_act"], taken_count(group_index("ct", 11), "act"))
            take_mod(16, 32)
            ch.add(V.tensor_copy(ones_b[:, :], ones[:, :]))
            ch.add(V.tensor_copy(tri_b[:, :], tri_strict[:, :]))
            ch.add(V.memset(lg[:, :, :], 0.0))

            def diagonals(n):
                g_, c = divmod(n, 2)
                V.tensor_tensor(diag[:, :].rearrange("p (j i) -> p j i", j=4), ident[:, :].unsqueeze(1).to_broadcast([P, 4, P]),
                                mod[:, 40 + 4 * c:44 + 4 * c, g_].unsqueeze(2).to_broadcast([P, 4, P]), ALU.mult)\
                    .then_inc(S["gfr_in"], 1)

            def oa_rest(j):
                dve.wait_ge(S["oa_hi_ready"], j + 1)
                V.tensor_tensor(oa_lo[:, j, :], ga[:, j, :], oa_hi[:, j, :].bitcast(F32), ALU.subtract)\
                    .then_inc(S["oa_lo_ready"], 1)

            def m_rest(j):
                dve.wait_ge(S["m_hi_ready"], j + 1)
                V.tensor_tensor(m_lo[:, j, :], gta[:, j, :], m_hi[:, j, :].bitcast(F32), ALU.subtract)\
                    .then_inc(S["m_lo_ready"], 1)

            def take_gate_rows(n):
                g_, c = divmod(n, 2)
                dve.wait_ge(S["gfr_ps"], n + 1)
                V.tensor_copy(gf_rows[:, g_, c * 512:c * 512 + 512], bank[5][:, :]).then_inc(S["gf_ready"], 1)

            diagonals(0)
            dve.wait_ge(S["sig_ready"], 1)
            g0 = group_index("bb", 0)
            for j in range(KT):
                n = g0 + j
                dve.wait_ge(S["proj_ready"], n + 1)
                V.tensor_tensor(gtb[:, j, :], bank[n % PROJ_BANKS][:, 0:T], gtb[:, j, :], ALU.mult).then_inc(S["taken_dve"], 1)
                if j and j % 2 == 0:
                    take_gate_rows(j // 2 - 1)
                    diagonals(j // 2)
                if j == 0:
                    dve.wait_ge(S["sig_ready"], 2)
                dve.wait_ge(S["on_t"], j + 1)
                V.scalar_tensor_tensor(out=ga[:, j, :], in0=bank[3 + j % 2][:, 0:T], scalar=cols[:, 64 + j:65 + j],
                                       in1=ga[:, j, :], op0=ALU.mult, op1=ALU.mult).then_inc(S["oa_ready"], 1)
                if j:
                    oa_rest(j - 1)
            oa_rest(KT - 1)
            take_gate_rows(3)
            dve.wait_ge(S["sig_ready"], 3)
            for j in range(KT):
                n = g0 + KT + j
                dve.wait_ge(S["proj_ready"], n + 1)
                ins = V.tensor_tensor(gta[:, j, :], bank[n % PROJ_BANKS][:, 0:T], gta[:, j, :], ALU.mult)
                ins.then_inc(S["taken_dve"], 1)
                dve.wait_ge(S["taken_dve"], KT + j + 1)
                V.tensor_tensor(gta[:, j, :], gta[:, j, :], gtb[:, j, :], ALU.add).then_inc(S["m_ready"], 1)
                if j:
                    m_rest(j - 1)
            m_rest(KT - 1)
            dve.wait_ge(S["mod_ready"], 2)
            for j in range(KT):
                n = g0 + 2 * KT + j
                src = bank[n % PROJ_BANKS]
                dve.wait_ge(S["proj_ready"], n + 1)
                V.tensor_scalar(gmT[:, j, 0:SEQ], src[:, 0:SEQ], mod[:, 16 + j, 0:1], None, ALU.mult)
                V.tensor_scalar(gmT[:, j, SEQ:T], src[:, SEQ:T], mod[:, 16 + j, 1:2], None, ALU.mult)\
                    .then_inc(S["taken_dve"], 1)
            dve.wait_ge(S["x1_in"], 96)

            def residual(t):
                m = TR[t]
                for c in range(2):
                    n = 2 * t + c
                    v = x1[0:m, t, c * 512:c * 512 + 512]
                    dve.wait_ge(S["gm_t"], n + 1)
                    V.scalar_tensor_tensor(out=v, in0=v, scalar=ALPHA, in1=bank[5 + n % 3][0:m, :], op0=ALU.mult,
                                           op1=ALU.add).then_inc(S["gm_added"], 1)
                dve.wait_ge(S["gm_added"], 2 * t + 2)
                tile_stats(t, x1[0:m, t, :], m).then_inc(S["nrm_sum"], 1)

            def affine(t, n, vec):
                m = TR[t]
                v = x1[0:m, t, :]
                ch.add(V.scalar_tensor_tensor(out=v, in0=v, scalar=mv[0:m, t, 0:1], in1=vec[0:m, 0, :],
                                              op0=ALU.subtract, op1=ALU.mult))
                reciprocal(n, t, 1)
                return V.scalar_tensor_tensor(out=v, in0=v, scalar=rstd[0:m, t:t + 1], in1=vec[0:m, 1, :],
                                              op0=ALU.mult, op1=ALU.add)

            def mixed(t, n):
                ch.add(affine(t, n, ln1))
                ch.done()
                tile_stats(3 + t, x1[0:TR[t], t, :], TR[t]).then_inc(S["nrm_sum"], 1)

            def normed(t, n):
                m = TR[t]
                reciprocal(n, 3 + t, 1)
                V.tensor_scalar(x2n[0:m, t, :], x1[0:m, t, :], mv[0:m, 3 + t, 0:1], rstd[0:m, 3 + t:4 + t],
                                ALU.subtract, ALU.mult).then_inc(S["norm_ready"], 1)

            residual(0)
            residual(1)
            dve.wait_ge(S["vecs_in"], 32)
            mixed(0, 3)
            residual(2)
            mixed(1, 4)
            normed(0, 5)
            mixed(2, 6)
            normed(1, 7)
            normed(2, 8)
            for c in range(2):
                dve.wait_ge(S["norm_t"], 5 + c)
                for j in range(4):
                    k = 4 * c + j
                    last = V.tensor_scalar(h2T[:, k, TC[2]], bank[NORM_BANKS[2][c]][:, j * P:j * P + TR[2]],
                                           mod[:, 32 + k, 1:2], mod[:, 24 + k, 1:2], ALU.mult, ALU.add)
                last.then_inc(S["h2_dve"], 1)
            dve.wait_ge(S["lgt_ps"], 1)
            V.tensor_scalar(lgT, bank[0][0:NG + E, 0:T], b_route[:, 0:1], None, ALU.add).then_inc(S["lgt_ready"], 1)
            dve.wait_ge(S["lg_ps"], 3)
            for t in range(3):
                V.tensor_copy(lg[0:TR[t], t, :], bank[1][0:TR[t], 40 * t:40 * t + NG + E]).then_inc(S["lg_ready"], 1)
            dve.wait_ge(S["lg_ready"], 3)

            def op(ins):
                ch.add(ins)
                ch.done()

            gl, el = lg[:, :, 0:NG], lg[:, :, NG:NG + E]

            def wide(col, n):
                return col.unsqueeze(2).to_broadcast([P, 3, n])

            def first_max(vals, iota, n, top, tmp, oh):
                op(V.tensor_reduce(top, vals, AXX, ALU.max))
                op(V.tensor_tensor(tmp, vals, wide(top, n), ALU.is_ge))
                op(V.scalar_tensor_tensor(out=tmp, in0=tmp, scalar=-100.0, in1=iota, op0=ALU.mult, op1=ALU.add))
                op(V.tensor_reduce(r1[:, 15, :], tmp, AXX, ALU.min))
                op(V.tensor_tensor(oh, tmp, wide(r1[:, 15, :], n), ALU.is_equal))

            first_max(gl, g_iota[:, :, :], NG, r1[:, 0, :], r4[2][:, :, :], r4[3][:, :, :])
            V.tensor_tensor(r4[0][:, :, :], gl, wide(r1[:, 0, :], NG), ALU.subtract).then_inc(S["ex_in"], 1)
            op(V.tensor_scalar(r4[2][:, :, :], r4[3][:, :, :], 1.0, -NEG, ALU.subtract, ALU.mult))
            selm, tmp32, oh1 = (r[:, :, :] for r in r32)
            for t in range(3):
                ch.add(V.tensor_tensor(r32[0][:, t, :].rearrange("p (g e) -> p g e", g=NG),
                                       lg[:, t, NG:NG + E].rearrange("p (g e) -> p g e", g=NG),
                                       r4[2][:, t, :].unsqueeze(2).to_broadcast([P, NG, EPG]), ALU.add))
            ch.done()
            first_max(selm, e_iota[:, :, :], E, r1[:, 1, :], tmp32, oh1)
            op(V.scalar_tensor_tensor(out=selm, in0=oh1, scalar=2 * NEG, in1=selm, op0=ALU.mult, op1=ALU.add))
            first_max(selm, e_iota[:, :, :], E, r1[:, 2, :], tmp32, oh2[:, :, :])
            V.tensor_tensor(r1[:, 4, :], r1[:, 2, :], r1[:, 1, :], ALU.subtract).then_inc(S["ex_in"], 1)
            op(V.tensor_tensor(chosen[:, :, :], oh1, oh2[:, :, :], ALU.add))
            op(V.tensor_tensor(chosen[:, :, :], chosen[:, :, :], wide(valid[:, :], E), ALU.mult))
            op(V.tensor_copy(q_rep[:, :], q_iota[:, 1:2].to_broadcast([P, P])))
            for t in range(3):
                last = V.tensor_copy(rep[:, t, :, :], chosen[:, t, :].unsqueeze(1).to_broadcast([P, ROUNDS, E]))
            last.then_inc(S["rank_in"], 1)
            dve.wait_ge(S["ex_out"], 2)
            op(V.tensor_reduce(r1[:, 6, :], r4[1][:, :, :], AXX, ALU.add))
            op(V.tensor_scalar(r1[:, 7, :], r1[:, 5, :], 1.0, None, ALU.add))
            op(V.tensor_tensor(r1[:, 8, :], r1[:, 6, :], r1[:, 7, :], ALU.mult))
            op(V.reciprocal(wts[:, 0, :], r1[:, 8, :]))
            op(V.tensor_tensor(wts[:, 1, :], wts[:, 0, :], r1[:, 5, :], ALU.mult))
            op(V.tensor_tensor(val[:, :, :], oh2[:, :, :], wide(tokval[:, :], E), ALU.add))
            dve.wait_ge(S["rank_ps"], 1)
            V.tensor_tensor(flags[:, 0:1], bank[1][:, 128:129], q_iota[:, 1:2], ALU.is_gt).then_inc(S["flag_ready"], 1)
            op(V.scalar_tensor_tensor(out=pos[:, :, :], in0=chosen[:, :, :], scalar=-FAR,
                                      in1=bank[1][:, 0:3 * E].rearrange("p (t e) -> p t e", t=3), op0=ALU.mult, op1=ALU.add))
            op(V.tensor_scalar(pos[:, :, :], pos[:, :, :], FAR, None, ALU.add))
            def one_hots(n, e, shift):
                if not isinstance(n, int) or n:
                    dve.wait_ge(S["index_ps"], n)
                V.tensor_copy(vcol[:, :], val[:, :, bass.ds(e, 1)].rearrange("p t e -> p (t e)"))\
                    .then_inc(S["vcol_ready"], 1)
                src = pos[:, :, bass.ds(e, 1)].rearrange("p t e -> p (t e)")
                if shift is None:
                    V.tensor_copy(pcol[:, :], src).then_inc(S["pcol_ready"], 1)
                else:
                    V.tensor_scalar(pcol[:, :], src, shift, None, ALU.subtract).then_inc(S["pcol_ready"], 1)
                dve.wait_ge(S["pcol_ready"], n + 1)
                dve.wait_ge(S["vcol_ready"], n + 1)
                for t in range(3):
                    last = V.tensor_scalar(onehot[:, t, :], slot_iota[:, :], pcol[:, t:t + 1], None, ALU.is_equal)
                last.then_inc(S["onehot_ready"], 1)

            def gathered(n, r):
                dve.wait_ge(S["index_ps"], n + 1)
                V.tensor_scalar(sidx[r][:, :], bank[5][:, 0:1], 2.0, half_base[:, 0:1], ALU.mult, ALU.add)
                dve.wait_ge(S["xg_t"], n + 1)
                V.tensor_copy(xg[:, :, :, :].rearrange("p q c s -> p (q c s)"), bank[2][:, :]).then_inc(S["xg_ready"], 1)

            def gated(n):
                dve.wait_ge(S["gs_ready"], n + 1)
                V.tensor_tensor(gs[0:SLOTS, :], gs[SLOTS:P, :], bank[1][SLOTS:P, :], ALU.mult).then_inc(S["hrow_ready"], 1)

            def turned(n):
                dve.wait_ge(S["he_t"], n + 1)
                V.tensor_copy(he[:, :, :].rearrange("p f s -> p (f s)"), bank[6][:, 0:FT * SLOTS]).then_inc(S["he_ready"], 1)

            def step(n, r):
                one_hots(n + 1, n + 1, None)
                gated(n)
                turned(n)
                gathered(n + 1, r)

            one_hots(0, 0, None)
            dve.wait_ge(S["xr_ps"], 1)
            op(V.tensor_copy(flags[:, 1:2], bank[4][:, 0:1]))
            V.tensor_scalar(pick[:, :], x_iota[:, :], flags[:, 1:2], flags[:, 0:1], ALU.is_equal, ALU.mult)\
                .then_inc(S["pick_ready"], 1)
            dve.wait_ge(S["plan_ps"], 1)
            op(V.tensor_copy(first_slot[:, :], bank[4][:, 64:64 + OVER]))
            op(V.tensor_copy(plan_i[0:1, 0:OVER], bank[4][0:1, 96:96 + OVER]))
            op(V.memset(plan_i[0:1, OVER:2 * OVER], 0))
            V.tensor_copy(plan_i[0:1, 2 * OVER:2 * OVER + 1], bank[4][0:1, 128:129]).then_inc(S["plan_ready"], 1)
            gathered(0, 0)
            step(0, 1)
            step(1, 2)
            with dve.Fori(0, (E - 3) // 6) as it:
                for r in range(2, 8):
                    dve.wait_ge(S["ys_ready"], it * 6 + (r - 1))
                    step(it * 6 + r, (r + 1) % 6)
            for e in range(2 + (E - 3) // 6 * 6, E - 1):
                dve.wait_ge(S["ys_ready"], e - 1)
                step(e, (e + 1) % 6)
            gated(E - 1)
            turned(E - 1)
            n_over = dve.value_load(plan_i[0:1, 2 * OVER:2 * OVER + 1], min_val=0, max_val=OVER)
            with dve.If(n_over > 0):
                with dve.Fori(0, n_over) as i:
                    e = dve.value_load(plan_i[0:1, bass.ds(i, 1)], min_val=0, max_val=E - 1)
                    dve.wait_ge(S["scattered0"], i * 16 + 16 * USES[0])
                    one_hots(i + E, e, first_slot[:, bass.ds(i, 1)])
                    gathered(i + E, 0)
                    gated(i + E)
                    turned(i + E)
                dve.nop()
            with dve.Else():
                dve.nop()
            for i, t in enumerate(LAST_ORDER):
                m = TR[t]
                y1, y2 = comb[t][0:m, 0:D], comb[t][0:m, D:2 * D]
                if t == 1:
                    dve.wait_ge(S["gated_pool"], 1)
                else:
                    dve.wait_ge(S["weighted"], 1 if t == 0 else 4)
                    op(V.scalar_tensor_tensor(out=y1, in0=y2, scalar=wts[0:m, 1, t:t + 1], in1=y1, op0=ALU.mult, op1=ALU.add))
                    op(V.tensor_tensor(y1, y1, gf_rows[0:m, t // 2, :], ALU.mult))
                op(V.scalar_tensor_tensor(out=x1[0:m, t, :], in0=x1[0:m, t, :], scalar=ALPHA, in1=y1, op0=ALU.mult, op1=ALU.add))
                tile_stats(t, x1[0:m, t, :], m).then_inc(S["nrm_sum"], 1)
            dve.wait_ge(S["vecs_in"], 64)
            for i, t in enumerate(LAST_ORDER):
                affine(t, 9 + i, ln2).then_inc(S["fin_ready"], 1)


_INS = ['x_prompt', 'x_sample', 'cache_sb_k', 'cache_sb_v', 'state_gla', 'c_prompt', 'c_sample', 'w_cond', 'b_cond',
        'w_in', 'w_gla_a2', 'b_gla_a', 'gla_norm_g', 'w_branch_a', 'w_branch_b', 'w_out', 'ln1_g', 'ln1_b', 'w_group',
        'b_group', 'w_router', 'b_router', 'w_exp_gate', 'w_exp_up', 'w_exp_down', 'ln2_g', 'ln2_b']
_OUTS = [("y_prompt", (1, SEQ, D)), ("y_sample", (1, DSEQ, D)), ("sb_k_prompt", (1, 1, SEQ, SH, SD)),
         ("sb_v_prompt", (1, 1, SEQ, SH, SD)), ("gla_state_prompt", (1, 1, GH, DK, DV)),
         ("sb_k_sample", (1, 1, DSEQ, SH, SD)), ("sb_v_sample", (1, 1, DSEQ, SH, SD)),
         ("gla_state_sample", (1, 1, GH, DK, DV))]


def kernel(**inputs):
    import numpy as _np
    import concourse.bacc as _bacc
    from concourse.bass_utils import run_bass_kernel_spmd as _run

    nc = _bacc.Bacc("TRN2", target_bir_lowering=False, num_devices=1)
    arrays, args, outs = {}, {}, {}
    for name in _INS:
        v = _np.ascontiguousarray(inputs[name])
        arrays[f"in_{name}"] = v
        args[name] = nc.dram_tensor(f"in_{name}", v.shape, mybir.dt.from_np(v.dtype), kind="ExternalInput").ap()
    for name, shape in _OUTS:
        outs[name] = nc.dram_tensor(f"out_{name}", shape, F32, kind="ExternalOutput").ap()
    build(nc, args, outs)
    r = _run(nc, [arrays], core_ids=[0])
    return tuple(r.results[0][f"out_{name}"] for name, _ in _OUTS)
```
